# Optimizing a Trainium2 kernel written in Bass

```python
import jax, jax.numpy as jnp
from jax import lax
import numpy as np
import math

D_MODEL = 1024
BATCH = 1
SEQ = 512
DEPTH = 1

CHUNK = 64
Q_BLOCK = 128
SB_HEADS = 8
SB_HEAD_DIM = 64
SB_WIDTH = SB_HEADS * SB_HEAD_DIM
GLA_HEADS = 4
GLA_KEY_WIDTH = D_MODEL // 2
GLA_VALUE_WIDTH = D_MODEL
GLA_DK = GLA_KEY_WIDTH // GLA_HEADS
GLA_DV = GLA_VALUE_WIDTH // GLA_HEADS
GLA_GATE_RANK = 16
GLA_GATE_TAU = 16.0
D_FF = 4 * D_MODEL
EPS = 1e-6

SPLIT_SIZES = (SB_WIDTH, SB_WIDTH, SB_WIDTH,
               GLA_KEY_WIDTH, GLA_KEY_WIDTH, GLA_VALUE_WIDTH, GLA_VALUE_WIDTH, GLA_GATE_RANK,
               D_MODEL, D_MODEL)
D_IN = 3 * SB_WIDTH + 2 * GLA_KEY_WIDTH + 2 * GLA_VALUE_WIDTH + GLA_GATE_RANK + 2 * D_MODEL


def rms_norm(x, g):
    xf = x.astype(jnp.float32)
    y = xf * lax.rsqrt(jnp.mean(xf * xf, axis=-1, keepdims=True) + EPS)
    return (y * g.astype(jnp.float32)).astype(x.dtype)

def split_heads(t, n_heads):
    b, s, _ = t.shape
    return t.reshape(b, s, n_heads, -1).transpose(0, 2, 1, 3)

def merge_heads(t):
    b, h, s, d = t.shape
    return t.transpose(0, 2, 1, 3).reshape(b, s, h * d)

def stick_breaking_attention(q, k, v):
    _, _, s_len, d = q.shape
    scale = d ** -0.5
    outs = []
    for start in range(0, s_len, Q_BLOCK):
        end = start + Q_BLOCK
        kb = k[:, :, :end]
        vb = v[:, :, :end]
        z = jnp.einsum('bhtd,bhsd->bhts', q[:, :, start:end], kb) * scale
        t_idx = start + jnp.arange(Q_BLOCK)[:, None]
        s_idx = jnp.arange(end)[None, :]
        past = s_idx < t_idx
        log_beta = jax.nn.log_sigmoid(z)
        log_fail = jnp.where(past, log_beta - z, 0.0)
        later = lax.cumsum(log_fail, axis=3, reverse=True) - log_fail
        w = jnp.where(past, jnp.exp(log_beta + later), 0.0)
        outs.append(jnp.einsum('bhts,bhsd->bhtd', w, vb))
    return jnp.concatenate(outs, axis=2)

def gla_chunked(q, k, v, log_a):
    b, h, s_len, dk = q.shape
    dv = v.shape[-1]
    nc = s_len // CHUNK

    def to_chunks(t):
        return t.reshape(b, h, nc, CHUNK, t.shape[-1]).transpose(2, 0, 1, 3, 4)

    qc, kc, vc, ac = (to_chunks(t) for t in (q * dk ** -0.5, k, v, log_a))
    bc = jnp.cumsum(ac, axis=3)
    causal = jnp.tril(jnp.ones((CHUNK, CHUNK), dtype=bool))

    def step(state, inp):
        qi, ki, vi, bi = inp
        b_last = bi[:, :, -1:, :]
        o_inter = jnp.einsum('bhtk,bhkv->bhtv', qi * jnp.exp(bi), state)
        diff = bi[:, :, :, None, :] - bi[:, :, None, :, :]
        decay = jnp.exp(jnp.where(causal[:, :, None], diff, -jnp.inf))
        scores = jnp.einsum('bhtk,bhsk,bhtsk->bhts', qi, ki, decay)
        o_intra = jnp.einsum('bhts,bhsv->bhtv', scores, vi)
        new_state = (jnp.exp(b_last[:, :, 0, :, None]) * state
                     + jnp.einsum('bhsk,bhsv->bhkv', ki * jnp.exp(b_last - bi), vi))
        return new_state, o_inter + o_intra

    state0 = jnp.zeros((b, h, dk, dv), jnp.float32)
    _, o = lax.scan(step, state0, (qc, kc, vc, bc))
    return o.transpose(1, 2, 0, 3, 4).reshape(b, h, s_len, dv)

def first_inputs(seed: int = 0) -> dict:
    key = jax.random.key(seed)
    ks = jax.random.split(key, 16)
    f32 = jnp.float32

    def w(k, shape, fan_in):
        return jax.random.normal(k, shape, f32) * (fan_in ** -0.5)

    def gain(k, shape):
        return 1.0 + 0.02 * jax.random.normal(k, shape, f32)

    return {
        'x': jax.random.normal(ks[0], (BATCH, SEQ, D_MODEL), f32),
        'norm_mix': gain(ks[1], (DEPTH, D_MODEL)),
        'w_in': w(ks[2], (DEPTH, D_MODEL, D_IN), D_MODEL),
        'w_gate_up': w(ks[3], (DEPTH, GLA_GATE_RANK, GLA_KEY_WIDTH), GLA_GATE_RANK),
        'b_gate_up': 0.1 * jax.random.normal(ks[4], (DEPTH, GLA_KEY_WIDTH), f32),
        'gla_norm': gain(ks[5], (DEPTH, GLA_DV)),
        'w_proj_sb': w(ks[6], (DEPTH, SB_WIDTH, D_MODEL), SB_WIDTH),
        'w_proj_gla': w(ks[7], (DEPTH, GLA_VALUE_WIDTH, D_MODEL), GLA_VALUE_WIDTH),
        'w_out': w(ks[8], (DEPTH, D_MODEL, D_MODEL), D_MODEL),
        'norm_mlp': gain(ks[9], (DEPTH, D_MODEL)),
        'w_ff1': w(ks[10], (DEPTH, D_MODEL, D_FF), D_MODEL),
        'w_ff2': w(ks[11], (DEPTH, D_FF, D_MODEL), D_FF),
        'norm_final': gain(ks[12], (D_MODEL,)),
    }

def first_block(x, norm_mix, w_in, w_gate_up, b_gate_up, gla_norm, w_proj_sb, w_proj_gla,
              w_out, norm_mlp, w_ff1, w_ff2, norm_final):
    f32 = jnp.float32
    bsz, s_len, _ = x.shape
    split_points = np.cumsum(SPLIT_SIZES)[:-1].tolist()
    for layer in range(DEPTH):
        h = rms_norm(x, norm_mix[layer])
        proj = h @ w_in[layer]
        (sb_q, sb_k, sb_v, g_q, g_k, g_v, g_out, g_low, gate_sb, gate_gla) = jnp.split(
            proj, split_points, axis=-1)

        o_sb = stick_breaking_attention(split_heads(sb_q, SB_HEADS).astype(f32),
                                        split_heads(sb_k, SB_HEADS).astype(f32),
                                        split_heads(sb_v, SB_HEADS).astype(f32))
        o_sb = merge_heads(o_sb).astype(x.dtype)

        log_a = jax.nn.log_sigmoid((g_low @ w_gate_up[layer] + b_gate_up[layer]).astype(f32)) / GLA_GATE_TAU
        o_gla = gla_chunked(split_heads(g_q, GLA_HEADS).astype(f32),
                            split_heads(g_k, GLA_HEADS).astype(f32),
                            split_heads(g_v, GLA_HEADS).astype(f32),
                            split_heads(log_a, GLA_HEADS))
        o_gla = o_gla.transpose(0, 2, 1, 3)
        o_gla = rms_norm(o_gla, gla_norm[layer])
        o_gla = o_gla * jax.nn.silu(g_out.astype(f32).reshape(bsz, s_len, GLA_HEADS, GLA_DV))
        o_gla = o_gla.reshape(bsz, s_len, GLA_VALUE_WIDTH).astype(x.dtype)

        mix = (jax.nn.sigmoid(gate_sb) * (o_sb @ w_proj_sb[layer])
               + jax.nn.sigmoid(gate_gla) * (o_gla @ w_proj_gla[layer]))
        x = x + mix @ w_out[layer]

        h2 = rms_norm(x, norm_mlp[layer])
        x = x + jnp.square(jax.nn.relu(h2 @ w_ff1[layer])) @ w_ff2[layer]
    return rms_norm(x, norm_final)


DEPTH_2 = 2

N_MIXERS = 2
HEAD_DIM = 64
V_DIM = 2 * HEAD_DIM
N_HEADS = D_MODEL // V_DIM
QK_WIDTH = N_HEADS * 2 * HEAD_DIM
V_WIDTH = N_HEADS * V_DIM
ROT_DIM = HEAD_DIM // 4
ROPE_THETA = 500000.0
CONV_WIDTH = 3
CONV_DIM = D_MODEL
D_FF_2 = 4 * D_MODEL
N_ATTN = (DEPTH_2 + 1) // 2
N_CONV = DEPTH_2 // 2


def rmsnorm(x, g):
    xf = x.astype(jnp.float32)
    y = xf * lax.rsqrt(jnp.mean(xf * xf, axis=-1, keepdims=True) + EPS)
    return (y * g.astype(jnp.float32)).astype(x.dtype)

def rope_tables(seq_len):
    pos = jnp.arange(seq_len, dtype=jnp.float32)
    inv_freq = ROPE_THETA ** (-jnp.arange(0, ROT_DIM, 2, dtype=jnp.float32) / ROT_DIM)
    ang = pos[:, None] * inv_freq[None, :]
    return jnp.cos(ang), jnp.sin(ang)

def apply_partial_rope(t, cos, sin):
    half = ROT_DIM // 2
    x1 = t[..., :half].astype(jnp.float32)
    x2 = t[..., half:ROT_DIM].astype(jnp.float32)
    c = cos[None, :, None, None, :]
    s = sin[None, :, None, None, :]
    rot = jnp.concatenate([x1 * c - x2 * s, x2 * c + x1 * s], axis=-1).astype(t.dtype)
    return jnp.concatenate([rot, t[..., ROT_DIM:]], axis=-1)

def lambda_init_fn(layer_idx):
    return 0.8 - 0.6 * math.exp(-0.3 * layer_idx)

def diff_attention(x, w_qkv, w_o, lq1, lk1, lq2, lk2, subln_g, lambda_init):
    B, S, _ = x.shape
    qkv = x @ w_qkv
    q = qkv[..., :QK_WIDTH].reshape(B, S, N_HEADS, 2, HEAD_DIM)
    k = qkv[..., QK_WIDTH:2 * QK_WIDTH].reshape(B, S, N_HEADS, 2, HEAD_DIM)
    v = qkv[..., 2 * QK_WIDTH:].reshape(B, S, N_HEADS, V_DIM)
    cos, sin = rope_tables(S)
    q = apply_partial_rope(q, cos, sin) * (HEAD_DIM ** -0.5)
    k = apply_partial_rope(k, cos, sin)
    lam = (jnp.exp(jnp.sum(lq1.astype(jnp.float32) * lk1.astype(jnp.float32)))
           - jnp.exp(jnp.sum(lq2.astype(jnp.float32) * lk2.astype(jnp.float32)))
           + lambda_init)
    n_blocks = S // Q_BLOCK
    qb = q.reshape(B, n_blocks, Q_BLOCK, N_HEADS, 2, HEAD_DIM).transpose(1, 0, 2, 3, 4, 5)
    k32 = k.astype(jnp.float32)
    key_pos = jnp.arange(S)

    def block(args):
        q_i, i = args
        s = jnp.einsum('bqhcd,bkhcd->bhcqk', q_i.astype(jnp.float32), k32)
        q_pos = i * Q_BLOCK + jnp.arange(Q_BLOCK)
        mask = key_pos[None, :] <= q_pos[:, None]
        s = jnp.where(mask, s, -jnp.inf)
        p = jax.nn.softmax(s, axis=-1)
        a = p[:, :, 0] - lam * p[:, :, 1]
        return jnp.einsum('bhqk,bkhe->bqhe', a.astype(v.dtype), v)

    o = lax.map(block, (qb, jnp.arange(n_blocks)))
    o = o.transpose(1, 0, 2, 3, 4).reshape(B, S, N_HEADS, V_DIM)
    o = rmsnorm(o, subln_g) * (1.0 - lambda_init)
    return o.reshape(B, S, V_WIDTH) @ w_o

def short_conv(x, w_in, conv_w, w_out):
    h = x @ w_in
    b_gate = h[..., :CONV_DIM]
    c_gate = h[..., CONV_DIM:2 * CONV_DIM]
    u = c_gate * h[..., 2 * CONV_DIM:]
    up = jnp.pad(u, ((0, 0), (CONV_WIDTH - 1, 0), (0, 0)))
    S = x.shape[1]
    y = (conv_w[0] * up[:, 0:S] + conv_w[1] * up[:, 1:S + 1] + conv_w[2] * up[:, 2:S + 2])
    return (b_gate * y) @ w_out

def sq_relu_mlp(x, w_up, w_down):
    return jnp.square(jax.nn.relu(x @ w_up)) @ w_down

def second_inputs(seed: int = 0) -> dict:
    key = jax.random.key(seed)
    ks = jax.random.split(key, 20)
    f32 = jnp.float32
    D = D_MODEL

    def nrm(k, shape, scale):
        return jax.random.normal(k, shape, f32) * scale

    return {
        "x": nrm(ks[0], (BATCH, SEQ, D), 1.0),
        "attn_w_qkv": nrm(ks[1], (N_ATTN, D, 2 * QK_WIDTH + V_WIDTH), D ** -0.5),
        "attn_w_o": nrm(ks[2], (N_ATTN, V_WIDTH, D), V_WIDTH ** -0.5),
        "attn_lambda_q1": nrm(ks[3], (N_ATTN, HEAD_DIM), 0.1),
        "attn_lambda_k1": nrm(ks[4], (N_ATTN, HEAD_DIM), 0.1),
        "attn_lambda_q2": nrm(ks[5], (N_ATTN, HEAD_DIM), 0.1),
        "attn_lambda_k2": nrm(ks[6], (N_ATTN, HEAD_DIM), 0.1),
        "attn_subln_g": 1.0 + nrm(ks[7], (N_ATTN, V_DIM), 0.02),
        "conv_w_in": nrm(ks[8], (N_CONV, D, 3 * CONV_DIM), D ** -0.5),
        "conv_w": nrm(ks[9], (N_CONV, CONV_WIDTH, CONV_DIM), CONV_WIDTH ** -0.5),
        "conv_w_out": nrm(ks[10], (N_CONV, CONV_DIM, D), CONV_DIM ** -0.5),
        "mlp_w_up": nrm(ks[11], (DEPTH_2, D, D_FF_2), D ** -0.5),
        "mlp_w_down": nrm(ks[12], (DEPTH_2, D_FF_2, D), D_FF_2 ** -0.5),
        "norm_mixer_pre": 1.0 + nrm(ks[13], (DEPTH_2, D), 0.02),
        "norm_mixer_post": 1.0 + nrm(ks[14], (DEPTH_2, D), 0.02),
        "norm_mlp_pre": 1.0 + nrm(ks[15], (DEPTH_2, D), 0.02),
        "norm_mlp_post": 1.0 + nrm(ks[16], (DEPTH_2, D), 0.02),
    }

def second_block(x, attn_w_qkv, attn_w_o, attn_lambda_q1, attn_lambda_k1, attn_lambda_q2,
              attn_lambda_k2, attn_subln_g, conv_w_in, conv_w, conv_w_out, mlp_w_up,
              mlp_w_down, norm_mixer_pre, norm_mixer_post, norm_mlp_pre, norm_mlp_post):
    for i in range(DEPTH_2):
        h = rmsnorm(x, norm_mixer_pre[i])
        j = i // N_MIXERS
        if i % N_MIXERS == 0:
            m = diff_attention(h, attn_w_qkv[j], attn_w_o[j], attn_lambda_q1[j],
                               attn_lambda_k1[j], attn_lambda_q2[j], attn_lambda_k2[j],
                               attn_subln_g[j], lambda_init_fn(i))
        else:
            m = short_conv(h, conv_w_in[j], conv_w[j], conv_w_out[j])
        x = x + rmsnorm(m, norm_mixer_post[i])
        h = rmsnorm(x, norm_mlp_pre[i])
        x = x + rmsnorm(sq_relu_mlp(h, mlp_w_up[i], mlp_w_down[i]), norm_mlp_post[i])
    return x


def setup_inputs(seed=0):
    out = dict(first_inputs(seed))
    for name, value in second_inputs(seed + 1).items():
        if name != "x":
            out[name + "_2"] = value
    return out


def reference(
    x, norm_mix, w_in, w_gate_up, b_gate_up, gla_norm, w_proj_sb, w_proj_gla, w_out, norm_mlp,
    w_ff1, w_ff2, norm_final, attn_w_qkv_2, attn_w_o_2, attn_lambda_q1_2, attn_lambda_k1_2,
    attn_lambda_q2_2, attn_lambda_k2_2, attn_subln_g_2, conv_w_in_2, conv_w_2, conv_w_out_2,
    mlp_w_up_2, mlp_w_down_2, norm_mixer_pre_2, norm_mixer_post_2, norm_mlp_pre_2,
    norm_mlp_post_2,
):
    x = first_block(
        x, norm_mix, w_in, w_gate_up, b_gate_up, gla_norm, w_proj_sb, w_proj_gla, w_out,
        norm_mlp, w_ff1, w_ff2, norm_final,
    )
    return second_block(
        x, attn_w_qkv_2, attn_w_o_2, attn_lambda_q1_2, attn_lambda_k1_2, attn_lambda_q2_2,
        attn_lambda_k2_2, attn_subln_g_2, conv_w_in_2, conv_w_2, conv_w_out_2, mlp_w_up_2,
        mlp_w_down_2, norm_mixer_pre_2, norm_mixer_post_2, norm_mlp_pre_2, norm_mlp_post_2,
    )


_drawn_inputs = setup_inputs


def setup_inputs(seed=0):
    import zlib

    import numpy as np

    out = dict(_drawn_inputs(seed))
    spreads = {}
    factors = {'norm_mix': 2.86,
     'b_gate_up': 3.639,
     'gla_norm': 21.0,
     'norm_mlp': 25.29,
     'attn_lambda_q2_2': 8.0,
     'attn_lambda_k2_2': 7.622,
     'attn_subln_g_2': 11.337,
     'norm_mlp_pre_2': 2.909,
     'norm_mlp_post_2': 3.159,
     'attn_lambda_q1_2': 64.0,
     'attn_lambda_k1_2': 8.0,
     'norm_mixer_post_2': 2.866}
    for name, (base, spread) in spreads.items():
        noise = np.random.default_rng([zlib.crc32(name.encode()), seed]).standard_normal(out[name].shape)
        drawn = base * np.exp(spread * noise) if base else spread * noise
        out[name] = __import__('jax').numpy.asarray(drawn.astype(out[name].dtype))
    for name, factor in factors.items():
        out[name] = (out[name] * factor).astype(out[name].dtype)
    return out
```

```python
from contextlib import ExitStack

import numpy as np

import concourse.bass as bass
from concourse import mybir

F32 = mybir.dt.float32
F32R = mybir.dt.float32r
BF16 = mybir.dt.bfloat16
U8 = mybir.dt.uint8
ALU = mybir.AluOpType
ACT = mybir.ActivationFunctionType
AX = mybir.AxisListType

P = 128
SEQ = 512
D = 1024
TT = SEQ // P
KT = D // P
NBLK = 512
QUAD = 4
EPS = 1e-6

SB_HEADS, SB_DIM = 8, 64
GLA_HEADS, GLA_DK, GLA_DV, GLA_RANK, GLA_TAU = 4, 128, 256, 16, 16.0
DIFF_HEADS, DIFF_DIM, DIFF_V = 8, 64, 128
N_GAINS = 6 * KT + 2 + 1 + GLA_HEADS + 3 * KT
ROT, THETA = 16, 500000.0
LAMBDA_INIT = 0.8 - 0.6
D_FF = 4096
ROUNDS = D_FF // D
LEVELS = 7

C_SBQ, C_SBK, C_SBV = 0, 512, 1024
C_GQ, C_GK, C_GV, C_GOUT, C_LOW = 1536, 2048, 2560, 3584, 4608
C_GATE_SB, C_GATE_GLA = 4624, 5648

K_ID, K_NTRI, K_NONE, K_STRICT, K_CAUSAL, K_COS, K_SIN, K_MASKS = 0, 128, 256, 384, 512, 640, 1152, 1664
K_ALL = K_MASKS + (LEVELS + 1) * P

TRI = 10 * P
REST = {0: 512, 2: 896, 1: 1024}
ROW = {3: 0, 2: 512, 0: 896, 1: 1024}


def sb_col(j, i):
    return P * j if i == j else REST[j] + P * (i - j - 1)


class Phase:

    def __init__(self, name, blocks, quads=2):
        self.name, self.blocks, self.quads = name, blocks, quads
        self.q = self.b = 0


def plan():
    names = [Phase("sb_qk", 2), Phase("sb_v", 1), Phase("g_qk", 2), Phase("g_v", 2), Phase("g_out", 2),
             Phase("gate_sb", 2), Phase("gate_gla", 2), Phase("proj_sb", 2, 1), Phase("proj_gla", 2),
             Phase("w_out", 2), Phase("mlp0", 4 * ROUNDS), Phase("qk", 4), Phase("v", 2), Phase("w_o", 2),
             Phase("mlp1", 4 * ROUNDS), Phase("conv_in", 6), Phase("conv_out", 2), Phase("mlp2", 4 * ROUNDS)]
    q = b = 0
    for ph in names:
        ph.q, ph.b = q, b
        q += ph.blocks * ph.quads
        b += ph.blocks
    return {ph.name: ph for ph in names}, q, b


def shape_constants():
    c = np.zeros((P, K_ALL), np.float32)
    r, s = np.arange(P)[:, None], np.arange(P)[None, :]
    c[:, K_ID:K_ID + P] = r == s
    c[:, K_NTRI:K_NTRI + P] = np.where(r >= s, -1.0, 0.0)
    c[:, K_NONE:K_NONE + P] = -1.0
    c[:, K_STRICT:K_STRICT + P] = s > r
    c[:, K_CAUSAL:K_CAUSAL + P] = np.where(s > r, -1e30, 0.0)
    half = ROT // 2
    inv = np.float32(THETA) ** (-np.arange(0, ROT, 2, dtype=np.float32) / np.float32(ROT))
    ang = np.arange(SEQ, dtype=np.float32)[None, :] * inv[:, None].astype(np.float32)
    cos, sin = np.ones((P, SEQ), np.float32), np.zeros((P, SEQ), np.float32)
    for base in (0, DIFF_DIM):
        for part, sign in ((0, -1.0), (half, 1.0)):
            cos[base + part:base + part + half] = np.cos(ang)
            sin[base + part:base + part + half] = sign * np.sin(ang)
    c[:, K_COS:K_COS + SEQ] = cos
    c[:, K_SIN:K_SIN + SEQ] = sin
    c[:, K_MASKS:K_MASKS + P] = r == s
    for n in range(LEVELS):
        h = 1 << n
        m = K_MASKS + P * (n + 1)
        c[:, m:m + P] = (r // (2 * h) == s // (2 * h)) & (r % (2 * h) < h) & (s % (2 * h) >= h)
    return c


def build(nc, w, out, stop=99):
    ph, n_quads, n_blocks = plan()
    ctx = ExitStack()
    with ctx:
        def sb(name, shape, dt=F32):
            return ctx.enter_context(nc.sbuf_tensor(name, shape, dt))

        sems = {}

        def sem(name):
            sems[name] = ctx.enter_context(nc.semaphore(name))
            return sems[name]

        x_tm = sb("x_tm", [P, TT, D])
        a_hi = sb("a_hi", [P, KT, SEQ], F32R)
        a_lo = sb("a_lo", [P, KT, SEQ], F32R)
        h_hi = sb("h_hi", [P, KT, SEQ], F32R)
        h_lo = sb("h_lo", [P, KT, SEQ], F32R)
        w_raw = sb("w_raw", [P, 2, QUAD, NBLK])
        w_hi = sb("w_hi", [P, 2, QUAD, NBLK], F32R)
        w_lo = sb("w_lo", [P, 2, QUAD, NBLK], F32R)
        y_tm = sb("y_tm", [P, TT, D])
        qk = sb("qk", [P, 16, SEQ])
        arena = sb("arena", [P, 6144])
        consts = sb("consts", [P, K_STRICT + P])
        masks = sb("masks", [P, LEVELS + 1, P], U8)
        ntri = sb("ntri", [P, P], F32R)
        nones = sb("nones", [P, P], F32R)
        ident_b = sb("ident_b", [P, P], BF16)
        causal_b = sb("causal_b", [P, P], BF16)
        gains = sb("gains", [P, N_GAINS + 1])
        b_gate = gains[:, 51:55]
        convw = gains[:, 55:79].rearrange("p (a b) -> p a b", a=3)
        small = sb("small", [P, 256])
        stat = sb("stat", [P, 5, DIFF_HEADS * TT])
        ps = ctx.enter_context(nc.psum_tensor("ps", [P, 8, 512], F32))
        psf = ps[:].rearrange("p b n -> p (b n)")

        xf = x_tm[:].rearrange("p a b -> p (a b)")
        yf = y_tm[:].rearrange("p a b -> p (a b)")
        hhf = h_hi[:].rearrange("p a b -> p (a b)")
        hlf = h_lo[:].rearrange("p a b -> p (a b)")
        qkf = qk[:].rearrange("p a b -> p (a b)")
        y_fm = yf.rearrange("p (a b) -> p a b", a=KT)
        ident = consts[:, K_ID:K_ID + P]
        strict = consts[:, K_STRICT:K_STRICT + P]
        v_sb = arena[:, 0:2048].rearrange("p (a b) -> p a b", a=TT)
        b_cum = arena[:, 2048:4096]
        tmp = arena[:, 4096:6144]
        w_up16 = arena[0:GLA_RANK, 0:GLA_HEADS * GLA_DK]
        lam_in = tmp[:, 2 * SEQ:2 * SEQ + 4 * DIFF_DIM].rearrange("p (a b) -> p a b", a=4)
        masks_f = arena[:, 0:(LEVELS + 1) * P]
        gain_rows = tmp[:, P:2 * P]
        tmp4 = tmp.rearrange("p (a b) -> p a b", a=4)

        junk = qkf[:, 0:1024]
        g_row = qkf[:, 7168:8192]
        sb_t = [xf[:, 2560:3840], yf[:, 2560:3840]]
        sb_sp = [xf[:, 0:1280], xf[:, 1280:2560]]
        sb_w = [yf[:, 0:1280], yf[:, 1280:2560]]
        sb_hi = [hhf[:, 0:1280], hhf[:, 1280:2560]]
        sb_lo = [hlf[:, 0:1280], hlf[:, 1280:2560]]
        o_sb = tmp4
        g_q, g_k = qkf[:, 4096:6144], qkf[:, 6144:8192]
        g_f = [qkf[:, 0:2048], qkf[:, 2048:4096]]
        g_at = arena[:, 0:2048]
        g_kt = tmp[:, 0:1536]
        g_state = [arena[:, 2048:3072], arena[:, 3072:4096], tmp[:, 0:1024]]
        g_o = qkf[:, 0:4096]
        ahf = a_hi[:].rearrange("p a b -> p (a b)")
        alf = a_lo[:].rearrange("p a b -> p (a b)")
        d_p = [[arena[:, 2560 * u + 1280 * c:2560 * u + 1280 * (c + 1)] for c in range(2)] for u in range(2)]
        d_sq = [arena[:, 5120:5632], arena[:, 5632:6144]]
        rot = [arena[:, 0:2048], arena[:, 2048:4096]]
        cos_t, sin_t = tmp[:, 0:SEQ], tmp[:, SEQ:2 * SEQ]
        gates_sb, gates_gla = qkf[:, 0:4096], qkf[:, 4096:8192]

        sumsq, var, rsq0, rsq1, rstd = (small[:, 4 * n:4 * n + 4] for n in range(5))
        gss, gvar, grs0, grs1, grstd = (small[:, 20 + 16 * n:36 + 16 * n] for n in range(5))
        elast = small[:, 100:116]
        nmax = small[:, 116:132].rearrange("p (u c i) -> p u c i", u=2, c=2)
        dsum = small[:, 132:148].rearrange("p (u c i) -> p u c i", u=2, c=2)
        drec = small[:, 148:164].rearrange("p (u c i) -> p u c i", u=2, c=2)
        lam = small[:, 164:170]
        dss, dvar, drs0, drs1, drstd = (stat[:, n] for n in range(5))

        raw_full = [sem("raw_full0"), sem("raw_full1")]
        x_in = [sem(f"x_in{i}") for i in range(TT)]
        consts_in = sem("consts_in")
        gains_in = sem("gains_in")
        low_in = sem("low_in")
        x_again = sem("x_again")
        tables_in = sem("tables_in")
        swapped = [sem(f"swapped{i}") for i in range(2)]
        grow_in = sem("grow_in")
        y_clear, up_in = sem("y_clear"), sem("up_in")
        consts_r = sem("consts_r")
        out_sent = sem("out_sent")
        quad_done = sem("quad_done")
        turned = sem("turned")
        hi_ready = sem("hi_ready")
        exp_ready = sem("exp_ready")
        chunk_hi = sem("chunk_hi")
        turned_hi = sem("turned_hi")
        sumsq_ready = sem("sumsq_ready")
        guess_ready = sem("guess_ready")
        act_step = sem("act_step")
        lo_ready = sem("lo_ready")
        banks_free = sem("banks_free")
        chunk_f32 = sem("chunk_f32")
        chunk_lo = sem("chunk_lo")
        turned_lo = sem("turned_lo")
        var_ready = sem("var_ready")
        rstd_ready = sem("rstd_ready")
        normed = sem("normed")
        normed_act = sem("normed_act")
        resid_ready = sem("resid_ready")
        dve_step = sem("dve_step")
        z_ready, sb_abs, sb_exp, soft_log = sem("z_ready"), sem("sb_abs"), sem("sb_exp"), sem("soft_log")
        sp_made, sp_masked, sp_hi, sp_lo = sem("sp_made"), sem("sp_masked"), sem("sp_hi"), sem("sp_lo")
        c_ready, w_exp, w_masked = sem("c_ready"), sem("w_exp"), sem("w_masked")
        sb_pv, osb_out = sem("sb_pv"), sem("osb_out")
        low_split, low_mm, low_out, up_mm = sem("low_split"), sem("low_mm"), sem("low_out"), sem("up_mm")
        gate_log, b_ready = sem("gate_log"), sem("b_ready")
        g_diff, g_exp, g_fac, g_mm, g_sel = sem("g_diff"), sem("g_exp"), sem("g_fac"), sem("g_mm"), sem("g_sel")
        kd_ready, kd_turned, kd_out = sem("kd_ready"), sem("kd_turned"), sem("kd_out")
        st_mm, st_ready, go_mm, go_act, go_dve = sem("st_mm"), sem("st_ready"), sem("go_mm"), sem("go_act"), sem("go_dve")
        gss_ready, gvar_ready, ggs_ready, gout_ready = sem("gss_ready"), sem("gvar_ready"), sem("ggs_ready"), sem("gout_ready")
        rope_src, rope_done, lam_sum, lam_exp = sem("rope_src"), sem("rope_done"), sem("lam_sum"), sem("lam_exp")
        v_hi, v_lo = sem("v_hi"), sem("v_lo")
        s_mm = [sem("s_mm0"), sem("s_mm1")]
        s_max = [sem("s_max0"), sem("s_max1")]
        s_exp = [sem("s_exp0"), sem("s_exp1")]
        rec_made, ratio_made, p_mixed = sem("rec_made"), sem("ratio_made"), sem("p_mixed")
        p_turned, pt_hi, pt_lo, o_mm, o_out = sem("p_turned"), sem("pt_hi"), sem("pt_lo"), sem("o_mm"), sem("o_out")
        o_sq, o_ss, ovar_ready, ogs_ready, o_normed = sem("o_sq"), sem("o_ss"), sem("ovar_ready"), sem("ogs_ready"), sem("o_normed")

        norm_kinds = "TTFTPTPTPTP"
        turns = {"h": 8, "o_sb": 4, "o_gla": 8, "h_mlp0": 8, "h_mix1": 8, "o_diff": 8, "h_mlp1": 8,
                 "h_conv": 8, "h_mlp2": 8}
        turn_base, n = {}, 0
        for name, k in turns.items():
            turn_base[name] = n
            n += k
        turn_banks = {"h": 0, "o_sb": ph["g_qk"].b % 2, "o_gla": ph["proj_sb"].b % 2, "h_mlp0": ph["mlp0"].b % 2,
                      "h_mix1": ph["qk"].b % 2, "o_diff": ph["w_o"].b % 2, "h_mlp1": ph["mlp1"].b % 2,
                      "h_conv": ph["conv_in"].b % 2, "h_mlp2": ph["mlp2"].b % 2}
        gain_of = {"h": 0, "h_mlp0": 1, "h_mix1": 2, "h_mlp1": 3, "h_conv": 4, "h_mlp2": 5}
        G_GLA, G_SUBLN = 48, 50

        GAIN_LOADS = 10
        EXPS = 4 + 4 + 4
        len_batch = (512, 512, 256)
        low_bank = 4 * (ph["g_out"].b % 2)
        up_bank = 4 * ((ph["g_out"].b + 1) % 2)
        m_min, u_abs = qkf[:, 0:2048], qkf[:, 2048:4096]
        gate_u = sem("gate_u")
        low_t = qkf[0:GLA_RANK, 0:SEQ]
        gains_turned, gains_out = sem("gains_turned"), sem("gains_out")
        low_split_hi, sem_grstd, sem_orstd = sem("low_split_hi"), sem("gla_rstd_ready"), sem("o_rstd_ready")

        class Steps:

            def __init__(self, eng, sm):
                self.eng, self.sm, self.n = eng, sm, 0

            def __call__(self, ins):
                self.n += 1
                ins.then_inc(self.sm, 1)
                self.eng.wait_ge(self.sm, self.n)

        def slot_fill(p, blk, qi):
            if p.quads == 1:
                return (p.q + blk + 2) // 2 + 1
            assert p.q % 2 == 0
            return p.q // 2 + blk + 2

        def tok_block(dst, blk):
            return dst[:, :, bass.ds(blk * NBLK, NBLK)]

        def tok_cols(dst, blk, c):
            return dst[:, 2 * c:2 * c + 2, NBLK * blk:NBLK * (blk + 1)]

        def fm_tiles(dst, blk, c):
            return dst.rearrange("p (a b) -> p a b", a=8)[:, 4 * blk + 2 * c:4 * blk + 2 * c + 2]

        def clear_y(eng):
            nc.vector.memset(yf, 0.0).then_inc(y_clear, 1)

        def gemm_low_up(pe, mm):
            pe.wait_ge(low_out, 1)
            pe.wait_ge(up_in, 16)
            for h in range(GLA_HEADS):
                last = mm(ps[:, up_bank + h], w_up16[:, GLA_DK * h:GLA_DK * (h + 1)], low_t, start=True, stop=True)
            last.then_inc(up_mm, 1)
            pe.wait_ge(gate_u, 1)

        def turn_bank(name, k):
            return (4 * turn_banks[name] + k) % 8

        def quad_at(p, blk, qi):
            return p.q + blk * p.quads + qi

        def slot_of(p, u, qi):
            return (p.q + u * p.quads + qi) % 2

        def pairs(eng, p, blocks=None, peel=0):
            blocks = p.blocks if blocks is None else blocks
            assert blocks % 2 == 0
            for n in range(0, min(peel, blocks), 2):
                yield n
            left = blocks - peel
            if left == 2:
                yield peel
            elif left > 2:
                with eng.Fori(peel // 2, blocks // 2) as i:
                    yield i * 2

        block = ctx.enter_context(nc.Block())

        @block.sync
        def _(sp):
            def load(p, blk, u, src):
                for qi in range(p.quads):
                    n = quad_at(p, blk, qi)
                    s = slot_of(p, u, qi)
                    if not (isinstance(n, int) and n < 2):
                        sp.wait_ge(lo_ready, n - 1)
                    sp.dma_start(w_raw[:, s], src(blk, qi).rearrange("(a p) n -> p a n", p=P)).then_inc(raw_full[s], 16)

            def stream(name, src):
                p = ph[name]
                if p.blocks % 2:
                    return load(p, 0, 0, src)
                for blk in pairs(sp, p):
                    for u in range(2):
                        load(p, blk + u, u, src)

            def cols(wt, c0=0):
                return lambda blk, qi: wt[QUAD * P * qi:QUAD * P * (qi + 1), bass.ds(c0 + blk * NBLK, NBLK)]

            def mlp(name, up, down):
                p = ph[name]
                with sp.Fori(0, ROUNDS) as r:
                    for u in range(2):
                        load(p, r * 4 + u, u, lambda blk, qi: up[QUAD * P * qi:QUAD * P * (qi + 1),
                                                                 bass.ds(r * D + u * NBLK, NBLK)])
                    for u in range(2):
                        load(p, r * 4 + 2 + u, u, lambda blk, qi: down[bass.ds(r * D + qi * QUAD * P, QUAD * P),
                                                                       u * NBLK:(u + 1) * NBLK])

            w_in = w["w_in"][0]
            for i in range(TT):
                sp.dma_start(x_tm[:, i], w["x"][0, P * i:P * (i + 1), :]).then_inc(x_in[i], 16)
            stream("sb_qk", cols(w_in, C_SBQ))
            stream("sb_v", cols(w_in, C_SBV))
            stream("g_qk", cols(w_in, C_GQ))
            stream("g_v", cols(w_in, C_GV))
            stream("g_out", cols(w_in, C_GOUT))
            stream("gate_sb", cols(w_in, C_GATE_SB))
            stream("gate_gla", cols(w_in, C_GATE_GLA))
            stream("proj_sb", cols(w["w_proj_sb"][0]))
            stream("proj_gla", cols(w["w_proj_gla"][0]))
            stream("w_out", cols(w["w_out"][0]))
            mlp("mlp0", w["w_ff1"][0], w["w_ff2"][0])
            stream("qk", cols(w["attn_w_qkv_2"][0]))
            stream("v", cols(w["attn_w_qkv_2"][0], 2 * D))
            stream("w_o", cols(w["attn_w_o_2"][0]))
            mlp("mlp1", w["mlp_w_up_2"][0], w["mlp_w_down_2"][0])
            stream("conv_in", cols(w["conv_w_in_2"][0]))
            stream("conv_out", cols(w["conv_w_out_2"][0]))
            mlp("mlp2", w["mlp_w_up_2"][1], w["mlp_w_down_2"][1])
            for i in range(TT):
                sp.wait_ge(resid_ready, 4 * 4 + i + 1)
                sp.dma_start(out[0, P * i:P * (i + 1), :], x_tm[:, i]).then_inc(out_sent, 16)
            sp.wait_ge(out_sent, 16 * TT)

        @block.gpsimd
        def _(pool):
            dma = pool.dma_start
            dma(consts[:], w["shape_consts"][:, 0:K_STRICT + P]).then_inc(consts_in, 16)
            dma(tmp[:, 0:P], w["shape_consts"][:, K_CAUSAL:K_CAUSAL + P]).then_inc(consts_in, 16)
            dma(masks_f, w["shape_consts"][:, K_MASKS:K_ALL]).then_inc(consts_in, 16)
            rows = [(w[name][row].rearrange("(k p) -> k p", p=P), KT) for name, row in (
                ("norm_mix", 0), ("norm_mlp", 0), ("norm_mixer_pre_2", 0), ("norm_mlp_pre_2", 0),
                ("norm_mixer_pre_2", 1), ("norm_mlp_pre_2", 1))]
            rows += [(w["gla_norm"][0].rearrange("(k p) -> k p", p=P), 2), (w["attn_subln_g_2"], 1),
                     (w["b_gate_up"][0].rearrange("(k p) -> k p", p=P), GLA_HEADS),
                     (w["conv_w_2"][0].rearrange("c (k p) -> (c k) p", p=P), 3 * KT)]
            r = 0
            for src, n in rows:
                dma(gain_rows[r:r + n], src).then_inc(gains_in, 16)
                r += n
            assert r == N_GAINS

            def sb_mask(t, u):
                pool.wait_ge(w_exp, t + 1)
                diag = sb_w[u][:, 0:512].rearrange("p (a b) -> p a b", a=TT)
                nc.gpsimd.affine_select(out=diag, in_=diag, compare_op=ALU.is_gt, fill=0.0, base=0,
                                        pattern=[[0, TT], [1, P]], channel_multiplier=-1).then_inc(w_masked, 1)

            for t in range(SB_HEADS):
                sb_mask(t, t % 2)

            pool.wait_ge(turned_lo, turn_base["o_sb"] + turns["o_sb"])
            dma(tmp[:, 0:KT * P].rearrange("p (a b) -> p a b", a=KT),
                w["w_in"][0][:, C_LOW:C_LOW + P].rearrange("(a p) n -> p a n", p=P)).then_inc(low_in, 16)
            dma(w_up16, w["w_gate_up"][0]).then_inc(up_in, 16)

            pool.wait_ge(go_mm, 4)
            dma(x_tm[:], w["x"][0].rearrange("(i p) n -> p i n", p=P)).then_inc(x_again, 16)

            def gain_row(name, row):
                src = w[name][row] if row is not None else w[name]
                dma(g_row, src.rearrange("(a n) -> a n", a=1).partition_broadcast(P)).then_inc(grow_in, 16)

            pool.wait_ge(chunk_lo, 4)
            gain_row("norm_final", None)
            pool.wait_ge(turned_lo, turn_base["h_mix1"] + KT)
            dma(tmp[:, 0:2 * SEQ], w["shape_consts"][:, K_COS:K_MASKS]).then_inc(tables_in, 16)
            for n, name in enumerate(("q1", "k1", "q2", "k2")):
                dma(lam_in[:, n], w[f"attn_lambda_{name}_2"].partition_broadcast(P)).then_inc(tables_in, 16)
            half = ROT // 2
            for blk in range(4):
                pool.wait_ge(rope_src, blk + 1)
                r4 = rot[blk % 2].rearrange("p (a b) -> p a b", a=4)
                for base in (0, DIFF_DIM):
                    for a, b in ((0, half), (half, 0)):
                        dma(r4[base + a:base + a + half], qk[base + b:base + b + half, 4 * blk:4 * blk + 4]).then_inc(swapped[blk % 2], 16)
            def o_square(t, u):
                pool.wait_ge(o_out, t + 1)
                if not (isinstance(t, int) and t < 2):
                    pool.wait_ge(o_ss, t - 1)
                nc.gpsimd.tensor_tensor(d_sq[u], qk[:, bass.ds(t, 1)].rearrange("p a b -> p (a b)"),
                                        qk[:, bass.ds(t, 1)].rearrange("p a b -> p (a b)"), ALU.mult).then_inc(o_sq, 1)

            for u in range(2):
                o_square(u, u)
            with pool.Fori(1, DIFF_HEADS // 2) as i:
                for u in range(2):
                    o_square(i * 2 + u, u)
            pool.wait_ge(turned_lo, turn_base["o_diff"] + KT)
            gain_row("norm_mixer_post_2", 0)
            pool.wait_ge(resid_ready, 8)
            gain_row("norm_mlp_post_2", 0)
            pool.wait_ge(resid_ready, 12)
            pool.wait_ge(chunk_lo, 4 + 2 * 16 + 8)
            gain_row("norm_mixer_post_2", 1)
            pool.wait_ge(resid_ready, 16)
            gain_row("norm_mlp_post_2", 1)

        @block.tensor
        def _(pe):
            mm = nc.tensor.matmul

            def gemm(name, operand, token_major, waits=None):
                p = ph[name]
                hi, lo = operand

                def one(blk, u):
                    blk_no = p.b + blk
                    bank0 = 4 * ((p.b + u) % 2)
                    if not (isinstance(blk_no, int) and blk_no < 2):
                        pe.wait_ge(banks_free, blk_no - 1)
                    for qi in range(p.quads):
                        n, s = quad_at(p, blk, qi), slot_of(p, u, qi)
                        pe.wait_ge(lo_ready, n + 1)
                        for sm, value in (waits(blk, qi) if waits else ()):
                            pe.wait_ge(sm, value)
                        multiply(hi, lo, s, qi, bank0, p.quads, token_major).then_inc(quad_done, 1)

                if p.blocks % 2:
                    return one(0, 0)
                for blk in pairs(pe, p):
                    for u in range(2):
                        one(blk + u, u)

            def multiply(hi, lo, s, qi, bank0, quads, token_major):
                for a in range(QUAD):
                    k = QUAD * qi + a
                    for j in range(4):
                        js = slice(P * j, P * (j + 1))
                        if token_major:
                            parts = ((hi[:, k, js], w_hi[:, s, a]), (hi[:, k, js], w_lo[:, s, a]), (lo[:, k, js], w_hi[:, s, a]))
                        else:
                            parts = ((w_hi[:, s, a, js], hi[:, k]), (w_hi[:, s, a, js], lo[:, k]), (w_lo[:, s, a, js], hi[:, k]))
                        for x, (left, right) in enumerate(parts):
                            last = mm(ps[:, bank0 + j], left, right, start=(k == 0 and x == 0),
                                      stop=(k == QUAD * quads - 1 and x == 2))
                return last

            def turn(name, src, wait):
                for k in range(turns[name]):
                    for i in range(TT):
                        for sm, value in wait(k, i):
                            pe.wait_ge(sm, value)
                        last = nc.tensor.transpose(ps[:, turn_bank(name, k), P * i:P * (i + 1)], src(i, k), ident)
                    last.then_inc(turned, 1)

            def turn_normed(name, n):
                turn(name, lambda i, k: y_tm[:, i, P * k:P * (k + 1)],
                     lambda k, i: () if k else ([(normed, 3 * n + i + 1)] if i < 3 else [(normed_act, n + 1)]))

            def turned_waits(name):
                return lambda blk, qi: [(turned_lo, turn_base[name] + 4 * qi + 4)]

            A, H = (a_hi, a_lo), (h_hi, h_lo)

            def mlp(name, turned_name, chunks):
                p = ph[name]
                b0 = 4 * (p.b % 2)
                with pe.Fori(0, ROUNDS) as r:
                    for u in range(4):
                        blk = r * 4 + u
                        bank0 = 4 * ((p.b + u) % 2)
                        pe.wait_ge(banks_free, p.b + blk - 1)
                        for qi in range(2):
                            n, s = quad_at(p, blk, qi), slot_of(p, u, qi)
                            pe.wait_ge(lo_ready, n + 1)
                            if u < 2:
                                pe.wait_ge(turned_lo, turn_base[turned_name] + 4 * qi + 4)
                            else:
                                pe.wait_ge(chunk_lo, chunks + r * 4 + 2 * qi + 2)
                            hi, lo = A if u < 2 else H
                            multiply(hi, lo, s, qi, bank0, 2, u >= 2).then_inc(quad_done, 1)

            pe.wait_ge(consts_in, 48)
            pe.wait_ge(gains_in, GAIN_LOADS * 16)
            nc.tensor.transpose(ps[:, 7, 0:N_GAINS], gain_rows[0:N_GAINS], ident[0:N_GAINS, 0:N_GAINS]).then_inc(gains_turned, 1)
            pe.wait_ge(gains_out, 1)
            turn_normed("h", 0)
            gemm("sb_qk", A, False, turned_waits("h"))
            gemm("sb_v", A, True)
            if stop < 1:
                return

            pe.wait_ge(banks_free, ph["g_qk"].b)

            def sb_region(t):
                return psf[:, 1536 * (t % 2):1536 * (t % 2) + TRI]

            def sb_scores(t):
                z = sb_region(t)
                rows = slice(SB_DIM * (t % 2), SB_DIM * (t % 2) + SB_DIM)
                q, k = qk[rows, t // 2], qk[rows, 4 + t // 2]
                if t >= 2:
                    pe.wait_ge(w_exp, t - 1)
                for j in range(TT):
                    last = mm(z[:, P * j:P * (j + 1)], k[:, P * j:P * (j + 1)], q[:, P * j:P * (j + 1)],
                              start=(j == 0), stop=True, skip_group_check=True)
                for j in (0, 2, 1):
                    c = REST[j]
                    last = mm(z[:, c:c + SEQ - P * (j + 1)], k[:, P * j:P * (j + 1)], q[:, P * (j + 1):],
                              start=(j != 2), stop=True, skip_group_check=True)
                last.then_inc(z_ready, 1)

            def sb_sums(t):
                z = sb_region(t)
                pe.wait_ge(sp_lo, t + 1)
                for j in range(TT):
                    for part in (sb_hi[t % 2], sb_lo[t % 2]):
                        last = mm(z[:, P * j:P * (j + 1)], ntri[:], part[:, P * j:P * (j + 1)], start=False, stop=True,
                                  skip_group_check=True)
                        if j == TT - 1:
                            continue
                        n = SEQ - P * (j + 1)
                        c = REST[j]
                        last = mm(z[:, c:c + n], ntri[:], part[:, c:c + n], start=False, stop=True, skip_group_check=True)
                        for jj in range(j + 1, TT):
                            o = c + P * (jj - j - 1)
                            last = mm(z[:, o:o + P], nones[:], part[:, P * jj:P * (jj + 1)], start=False, stop=True,
                                      skip_group_check=True)
                            if jj < TT - 1:
                                m = SEQ - P * (jj + 1)
                                last = mm(z[:, o + P:o + P + m], nones[:], part[:, REST[jj]:REST[jj] + m], start=False,
                                          stop=True, skip_group_check=True)
                last.then_inc(c_ready, 1)

            def sb_values(t):
                pe.wait_ge(w_masked, t + 1)
                if t >= 2:
                    pe.wait_ge(osb_out, t - 1)
                for i in range(TT):
                    for j in range(i + 1):
                        c = sb_col(j, i)
                        last = mm(ps[:, 6 + t % 2, SB_DIM * i:SB_DIM * (i + 1)], sb_w[t % 2][:, c:c + P],
                                  v_sb[:, j, SB_DIM * t:SB_DIM * (t + 1)], start=(i == 0 and j == 0), stop=True,
                                  skip_group_check=True)
                last.then_inc(sb_pv, 1)

            for t in range(SB_HEADS + 2):
                if t < SB_HEADS:
                    sb_scores(t)
                if 1 <= t <= SB_HEADS:
                    sb_sums(t - 1)
                if t >= 2:
                    sb_values(t - 2)
            turn("o_sb", lambda i, k: o_sb[:, i, P * k:P * (k + 1)], lambda k, i: [] if k or i else [(osb_out, SB_HEADS)])
            if stop < 2:
                return

            pe.wait_ge(turned_lo, turn_base["o_sb"] + 4)
            gemm("g_qk", A, False)
            gemm("g_v", A, True)

            low_bank = 4 * (ph["g_out"].b % 2)
            pe.wait_ge(banks_free, ph["g_out"].b)
            pe.wait_ge(low_split, 1)
            low_hi = hhf[:, 2048:3072].rearrange("p (a b) -> p a b", a=KT)
            low_lo = hlf[:, 2048:3072].rearrange("p (a b) -> p a b", a=KT)
            for k in range(KT):
                for x, (left, right) in enumerate(((low_hi, a_hi), (low_hi, a_lo), (low_lo, a_hi))):
                    last = mm(ps[:, low_bank], left[:, k], right[:, k], start=(k == 0 and x == 0), stop=(k == KT - 1 and x == 2))
            last.then_inc(low_mm, 1)
            gemm_low_up(pe, mm)
            gemm("g_out", A, True)
            if stop < 3:
                return

            pe.wait_ge(banks_free, ph["gate_sb"].b)
            for n in range(LEVELS + 1):
                pe.wait_ge(g_fac, n) if n else pe.wait_ge(b_ready, 1)
                if n >= 2:
                    pe.wait_ge(g_sel, n - 1)
                left, right = (g_k, g_q) if n == 0 else (g_f[(n - 1) % 2], g_f[(n - 1) % 2])
                for m in range(16):
                    ms = slice(P * m, P * (m + 1))
                    last = mm(psf[:, 2048 * (n % 2) + P * m:2048 * (n % 2) + P * (m + 1)], left[:, ms], right[:, ms],
                              start=True, stop=True)
                last.then_inc(g_mm, 1)
            pe.wait_ge(kd_ready, 1)
            pe.wait_ge(g_sel, LEVELS + 1)
            for m in range(12):
                h, c = m // 3, m % 3
                col = SEQ * h + P * c
                last = nc.tensor.transpose(psf[:, P * m:P * (m + 1)], g_k[:, col:col + P], ident)
            last.then_inc(kd_turned, 1)
            pe.wait_ge(kd_out, 1)
            for m in range(12):
                h, c = m // 3, m % 3
                dst = psf[:, 1024 + GLA_DV * (4 * c + h):1024 + GLA_DV * (4 * c + h + 1)]
                last = mm(dst, g_kt[:, P * m:P * (m + 1)], x_tm[:, c, GLA_DV * h:GLA_DV * (h + 1)], start=True, stop=True)
            last.then_inc(st_mm, 1)
            pe.wait_ge(st_ready, 3)
            for c in range(TT):
                for h in range(GLA_HEADS):
                    dst = ps[:, 2 * c + h // 2, GLA_DV * (h % 2):GLA_DV * (h % 2 + 1)]
                    col = SEQ * h + P * c
                    last = mm(dst, g_at[:, col:col + P], x_tm[:, c, GLA_DV * h:GLA_DV * (h + 1)], start=True, stop=(c == 0))
                    if c:
                        last = mm(dst, g_q[:, col:col + P], g_state[c - 1][:, GLA_DV * h:GLA_DV * (h + 1)], start=False, stop=True)
                last.then_inc(go_mm, 1)
            pe.wait_ge(go_act, 2)
            pe.wait_ge(go_dve, 2)
            if stop < 4:
                return
            gemm("gate_sb", A, False)
            gemm("gate_gla", A, False)
            pe.wait_ge(banks_free, ph["proj_sb"].b)
            turn("o_gla", lambda i, k: y_tm[:, i, P * k:P * (k + 1)], lambda k, i: [] if k else [(gout_ready, i + 1)])
            pe.wait_ge(turned_lo, turn_base["o_gla"] + 4)
            gemm("proj_sb", H, False, lambda blk, qi: [(turned_lo, turn_base["o_gla"] + 4 * blk + 4)])
            gemm("proj_gla", A, False, turned_waits("o_gla"))
            gemm("w_out", H, True, lambda blk, qi: [(chunk_lo, 2 * qi + 2)])
            if stop < 5:
                return
            turn_normed("h_mlp0", 1)
            mlp("mlp0", "h_mlp0", 4)
            if stop < 6:
                return
            turn_normed("h_mix1", 2)
            gemm("qk", A, False, turned_waits("h_mix1"))
            gemm("v", A, True)

            pe.wait_ge(banks_free, ph["w_o"].b)
            pe.wait_ge(rope_done, 4)

            def diff_scores(t, c):
                rows = slice(DIFF_DIM * c, DIFF_DIM * (c + 1))
                q, k = qk[rows, t], qk[rows, 8 + t]
                if t:
                    pe.wait_ge(s_exp[c], t)
                s = psf[:, 1536 * c:1536 * c + TRI]
                for i in (3, 2, 0, 1):
                    n = P * (i + 1)
                    mm(s[:, ROW[i]:ROW[i] + n], q[:, P * i:P * (i + 1)], k[:, 0:n], start=(i != 0), stop=True,
                       skip_group_check=True)
                    last = mm(s[:, ROW[i] + n - P:ROW[i] + n], ident_b[:], causal_b[:], start=False, stop=True,
                              skip_group_check=True)
                last.then_inc(s_mm[c], 1)

            batches = (((3, 0), (3, 1), (3, 2), (3, 3)), ((2, 0), (2, 1), (2, 2), (0, 0)), ((1, 0), (1, 1)))

            def diff_turn(t, b):
                pe.wait_ge(p_mixed, t + 1)
                if 3 * t + b:
                    pe.wait_ge(pt_lo, 3 * t + b)
                for n, (i, j) in enumerate(batches[b]):
                    c = ROW[i] + P * j
                    last = nc.tensor.transpose(ps[:, 6, P * n:P * (n + 1)], d_p[t % 2][0][:, c:c + P], ident)
                last.then_inc(p_turned, 1)

            def diff_values(t):
                pe.wait_ge(pt_lo, 3 * t + 3)
                if t:
                    pe.wait_ge(o_out, t)
                else:
                    pe.wait_ge(v_lo, 1)
                for i in range(TT):
                    for j in range(i + 1):
                        c = ROW[i] + P * j
                        o = ps[:, 7, P * i:P * (i + 1)]
                        ph_, pl_ = sb_hi[t % 2][:, c:c + P], sb_lo[t % 2][:, c:c + P]
                        vs = slice(D * j + P * t, D * j + P * (t + 1))
                        for x, (left, right) in enumerate(((ph_, ahf[:, vs]), (ph_, alf[:, vs]), (pl_, ahf[:, vs]))):
                            last = mm(o, left, right, start=(j == 0 and x == 0), stop=(j == i and x == 2))
                last.then_inc(o_mm, 1)

            for t in range(DIFF_HEADS + 1):
                if t < DIFF_HEADS:
                    diff_scores(t, 0)
                if t:
                    diff_turn(t - 1, 0)
                if t < DIFF_HEADS:
                    diff_scores(t, 1)
                if t:
                    diff_turn(t - 1, 1)
                    diff_turn(t - 1, 2)
                    diff_values(t - 1)
            pe.wait_ge(o_out, DIFF_HEADS)
            turn("o_diff", lambda i, k: qk[:, k, P * i:P * (i + 1)], lambda k, i: [] if i else [(o_normed, k // 2 + 1)])
            if stop < 7:
                return
            gemm("w_o", A, True, turned_waits("o_diff"))
            turn_normed("h_mlp1", 3)
            mlp("mlp1", "h_mlp1", 4 + 16)
            if stop < 8:
                return
            turn_normed("h_conv", 4)
            gemm("conv_in", A, False, turned_waits("h_conv"))
            gemm("conv_out", H, True, lambda blk, qi: [(chunk_lo, 4 + 32 + 4 * qi + 4)])
            if stop < 9:
                return
            turn_normed("h_mlp2", 5)
            mlp("mlp2", "h_mlp2", 4 + 32 + 8)

        @block.scalar
        def _(act):
            step = Steps(act, act_step)

            def split(p, blk, u, qi):
                n, s = quad_at(p, blk, qi) + 2, slot_of(p, u, qi)
                if isinstance(n, int) and n >= n_quads:
                    return
                act.wait_ge(raw_full[s], slot_fill(p, blk, qi) * 16)
                act.wait_ge(quad_done, n - 1)
                nc.scalar.activation(w_hi[:, s], w_raw[:, s], ACT.Copy).then_inc(hi_ready, 1)

            def first_splits():
                for s in range(2):
                    act.wait_ge(raw_full[s], 16)
                    nc.scalar.activation(w_hi[:, s], w_raw[:, s], ACT.Copy).then_inc(hi_ready, 1)

            def body(p, blk, u, evac=None):
                for qi in range(p.quads):
                    split(p, blk, u, qi)
                if evac:
                    act.wait_ge(quad_done, quad_at(p, blk, p.quads))
                    evac(blk, 4 * ((p.b + u) % 2))

            def phase(name, evac=None):
                p = ph[name]
                if p.blocks % 2:
                    return body(p, 0, 0, evac)
                for blk in pairs(act, p):
                    for u in range(2):
                        body(p, blk + u, u, evac)

            def gate_exp(dst, free=None):
                def evac(blk, bank0):
                    if free:
                        act.wait_ge(*free)
                    for c in range(2):
                        nc.scalar.activation(dst(blk, c), ps[:, bank0 + 2 * c:bank0 + 2 * c + 2], ACT.Exp,
                                             scale=-1.0).then_inc(exp_ready, 1)
                return evac

            def round_chunk(n, src, dst):
                act.wait_ge(chunk_f32, n)
                nc.scalar.activation(dst, src, ACT.Copy).then_inc(chunk_hi, 1)

            def mlp(name, chunks, last=False):
                p = ph[name]

                def rounds(r, tail=False):
                    for u in range(4):
                        blk = r * 4 + u
                        if not (tail and u == 3):
                            for qi in range(2):
                                split(p, blk, u, qi)
                        if u < 2:
                            bank0 = 4 * ((p.b + u) % 2)
                            act.wait_ge(quad_done, quad_at(p, blk, 2))
                            for c in range(2):
                                g = chunks + r * 4 + 2 * u + c
                                act.wait_ge(chunk_lo, g - 1)
                                nc.scalar.activation(tmp4[:, 2 * c:2 * c + 2], ps[:, bank0 + 2 * c:bank0 + 2 * c + 2],
                                                     ACT.Relu).then_inc(exp_ready, 1)
                            for c in range(2):
                                g = chunks + r * 4 + 2 * u + c
                                round_chunk(g + 1, tmp4[:, 2 * c:2 * c + 2], h_hi[:, 4 * u + 2 * c:4 * u + 2 * c + 2])

                with act.Fori(0, ROUNDS - 1 if last else ROUNDS) as r:
                    rounds(r)
                if last:
                    rounds(ROUNDS - 1, True)

            def squares(n, src, waits):
                for i in range(TT):
                    act.wait_ge(*waits(i))
                    step(nc.scalar.activation(junk, src[:, i], ACT.Square, accum_out=sumsq[:, i:i + 1]))
                    if i == TT - 1:
                        nc.scalar.activation(small[:, 250:251], sumsq[:, 0:1], ACT.Copy).then_inc(sumsq_ready, 1)

            def guess(n, v, dst0, dst, made, sm=guess_ready):
                act.wait_ge(*made)
                step(nc.scalar.activation(dst0, v, ACT.Ln))
                nc.scalar.activation(dst, dst0, ACT.Exp, scale=-0.5).then_inc(sm, 1)

            def norm(n, src, waits):
                squares(n, src, waits)
                guess(n, var, rsq0, rsq1, (var_ready, n + 1))

            def norm_to_y(n, t, waits):
                norm(n, x_tm, waits)
                act.wait_ge(rstd_ready, n + 1)
                nc.scalar.activation(y_tm[:, 3], x_tm[:, 3], ACT.Copy, scale=rstd[:, 3:4]).then_inc(normed_act, 1)

            def turned_out(name, gain, dst):
                for k in range(turns[name]):
                    act.wait_ge(turned, turn_base[name] + k + 1)
                    src = ps[:, turn_bank(name, k)]
                    g = gain(k)
                    if g is None:
                        last = nc.scalar.activation(dst[:, k], src, ACT.Copy)
                    else:
                        last = nc.scalar.activation(dst[:, k], src, ACT.Copy, scale=g)
                    last.then_inc(turned_hi, 1)

            def feature_gain(name):
                return lambda k: gains[:, 8 * gain_of[name] + k:8 * gain_of[name] + k + 1]

            nc.scalar.preload_act_table_set("natural_log_exp_and_others")
            norm_to_y(0, 0, lambda i: (x_in[i], 16))
            act.wait_ge(gains_out, 1)
            turned_out("h", feature_gain("h"), a_hi)
            first_splits()
            phase("sb_qk")
            phase("sb_v")
            if stop < 1:
                return

            def sb_soft(t, u):
                z = psf[:, 1536 * u:1536 * u + TRI]
                act.wait_ge(z_ready, t + 1)
                if not (isinstance(t, int) and t < 2):
                    act.wait_ge(sp_made, t - 1)
                nc.scalar.activation(sb_t[u], z, ACT.Abs).then_inc(sb_abs, 1)
                act.wait_ge(sb_abs, t + 1)
                nc.scalar.activation(sb_t[u], sb_t[u], ACT.Exp, scale=-1.0).then_inc(sb_exp, 1)
                act.wait_ge(sb_exp, t + 1)
                nc.scalar.activation(sb_t[u], sb_t[u], ACT.Ln, bias=1.0).then_inc(soft_log, 1)

            def sb_weights(t, u):
                act.wait_ge(c_ready, t + 1)
                if not (isinstance(t, int) and t < 2):
                    act.wait_ge(sb_pv, t - 1)
                nc.scalar.activation(sb_w[u], psf[:, 1536 * u:1536 * u + TRI], ACT.Exp).then_inc(w_exp, 1)

            def sb_round(t, u):
                act.wait_ge(sp_masked, t + 1)
                if not (isinstance(t, int) and t < 2):
                    act.wait_ge(c_ready, t - 1)
                nc.scalar.activation(sb_hi[u], sb_sp[u], ACT.Copy).then_inc(sp_hi, 1)

            sb_soft(0, 0)
            sb_round(0, 0)
            sb_soft(1, 1)
            sb_weights(0, 0)
            sb_round(1, 1)
            with act.Fori(1, SB_HEADS // 2) as i:
                for u in range(2):
                    t = i * 2 + u
                    sb_soft(t, u)
                    sb_weights(t - 1, 1 - u)
                    sb_round(t, u)
            sb_weights(SB_HEADS - 1, 1)
            turned_out("o_sb", lambda k: None, h_hi)
            if stop < 2:
                return
            phase("g_qk")
            act.wait_ge(low_in, 16)
            nc.scalar.activation(hhf[:, 2048:3072], tmp[:, 0:1024], ACT.Copy).then_inc(low_split_hi, 1)
            phase("g_v")
            act.wait_ge(up_mm, 1)
            for h in range(GLA_HEADS):
                last = nc.scalar.activation(tmp4[:, h], ps[:, up_bank + h], ACT.Identity, bias=b_gate[:, h:h + 1])
            last.then_inc(gate_u, 1)
            act.wait_ge(gate_u, 1)
            step(nc.scalar.activation(u_abs, tmp, ACT.Abs))
            step(nc.scalar.activation(u_abs, u_abs, ACT.Exp, scale=-1.0))
            nc.scalar.activation(u_abs, u_abs, ACT.Ln, bias=1.0).then_inc(gate_log, 1)
            phase("g_out", gate_exp(lambda blk, c: tok_cols(y_tm, blk, c)))
            if stop < 3:
                return
            for n in range(LEVELS + 2):
                act.wait_ge(g_diff, n + 1)
                nc.scalar.activation(g_f[n % 2], g_f[n % 2], ACT.Exp).then_inc(g_exp, 1)
            nc.scalar.activation(elast, b_cum.rearrange("p (m n) -> p m n", n=P)[:, :, P - 1], ACT.Exp).then_inc(g_exp, 1)
            for c in range(2):
                act.wait_ge(go_mm, c + 1)
                nc.scalar.activation(g_o[:, 1024 * c:1024 * (c + 1)], psf[:, 1024 * c:1024 * (c + 1)], ACT.Copy).then_inc(go_act, 1)
            act.wait_ge(go_dve, 2)
            act.wait_ge(go_act, 2)
            for m in range(16):
                step(nc.scalar.activation(tmp[:, 1024:1024 + GLA_DV], g_o[:, GLA_DV * m:GLA_DV * (m + 1)], ACT.Square,
                                          accum_out=gss[:, m:m + 1]))
            nc.scalar.activation(small[:, 251:252], gss[:, 0:1], ACT.Copy).then_inc(gss_ready, 1)
            guess(0, gvar, grs0, grs1, (gvar_ready, 1), ggs_ready)
            if stop < 4:
                return
            phase("gate_sb", gate_exp(lambda blk, c: fm_tiles(gates_sb, blk, c), (gout_ready, 4)))
            phase("gate_gla", gate_exp(lambda blk, c: fm_tiles(gates_gla, blk, c)))
            turned_out("o_gla", lambda k: gains[:, G_GLA + k % 2:G_GLA + k % 2 + 1], a_hi)
            phase("proj_sb")

            def mix_hi(blk, bank0):
                for c in range(2):
                    round_chunk(2 * blk + c + 1, tmp4[:, 2 * c:2 * c + 2], h_hi[:, bass.ds(4 * blk + 2 * c, 2)])
            phase("proj_gla", mix_hi)
            phase("w_out")
            if stop < 5:
                return
            norm_to_y(1, 1, lambda i: (banks_free, ph["mlp0"].b))
            turned_out("h_mlp0", feature_gain("h_mlp0"), a_hi)
            mlp("mlp0", 4)
            norm(2, x_tm, lambda i: (banks_free, ph["qk"].b))
            norm_to_y(3, 2, lambda i: (resid_ready, i + 1))
            if stop < 6:
                return
            turned_out("h_mix1", feature_gain("h_mix1"), a_hi)
            phase("qk")
            phase("v")
            act.wait_ge(lam_sum, 1)
            nc.scalar.activation(lam[:, 2:4], lam[:, 0:2], ACT.Exp).then_inc(lam_exp, 1)
            act.wait_ge(banks_free, ph["w_o"].b)
            nc.scalar.activation(ahf, yf, ACT.Copy).then_inc(v_hi, 1)

            def diff_exp(t, u, c):
                act.wait_ge(s_max[c], t + 1)
                if not (isinstance(t, int) and t < 2):
                    if c == 0:
                        act.wait_ge(p_turned, 3 * t - 3)
                    else:
                        act.wait_ge(p_mixed, t - 1)
                for i in range(TT):
                    n = P * (i + 1)
                    last = nc.scalar.activation(d_p[u][c][:, ROW[i]:ROW[i] + n], psf[:, 1536 * c + ROW[i]:1536 * c + ROW[i] + n],
                                                ACT.Exp, bias=nmax[:, u, c, i:i + 1], accum_out=dsum[:, u, c, i:i + 1])
                last.then_inc(s_exp[c], 1)

            def diff_round(t, u, b):
                n = len_batch[b]
                act.wait_ge(p_turned, 3 * t + b + 1)
                if b == 0 and not (isinstance(t, int) and t < 2):
                    act.wait_ge(o_mm, t - 1)
                nc.scalar.activation(sb_hi[u][:, 512 * b:512 * b + n], ps[:, 6, 0:n], ACT.Copy).then_inc(pt_hi, 1)

            def diff_out(t, u):
                act.wait_ge(o_mm, t + 1)
                for i in range(TT):
                    last = nc.scalar.activation(qk[:, bass.ds(t, 1), P * i:P * (i + 1)].rearrange("p a b -> p (a b)"), ps[:, 7, P * i:P * (i + 1)],
                                                ACT.Copy, scale=drec[:, u, 0, i:i + 1])
                last.then_inc(o_out, 1)

            def diff_tail(t, u):
                diff_round(t, u, 1)
                diff_round(t, u, 2)
                diff_out(t, u)

            diff_exp(0, 0, 0)
            diff_exp(0, 0, 1)
            diff_exp(1, 1, 0)
            diff_round(0, 0, 0)
            diff_exp(1, 1, 1)
            diff_tail(0, 0)
            with act.Fori(1, DIFF_HEADS // 2) as i:
                for u in range(2):
                    t = i * 2 + u
                    diff_exp(t, u, 0)
                    diff_round(t - 1, 1 - u, 0)
                    diff_exp(t, u, 1)
                    diff_tail(t - 1, 1 - u)
            diff_round(DIFF_HEADS - 1, 1, 0)
            diff_tail(DIFF_HEADS - 1, 1)
            guess(0, dvar, drs0, drs1, (ovar_ready, 1), ogs_ready)
            turned_out("o_diff", lambda k: gains[:, N_GAINS:N_GAINS + 1], a_hi)
            if stop < 7:
                return
            phase("w_o")
            norm(4, y_tm, lambda i: (banks_free, ph["mlp1"].b))
            norm_to_y(5, 3, lambda i: (resid_ready, 4 + i + 1))
            turned_out("h_mlp1", feature_gain("h_mlp1"), a_hi)
            mlp("mlp1", 4 + 16)
            norm(6, y_tm, lambda i: (banks_free, ph["conv_in"].b))
            norm_to_y(7, 4, lambda i: (resid_ready, 8 + i + 1))
            if stop < 8:
                return
            turned_out("h_conv", feature_gain("h_conv"), a_hi)

            def conv_hi(blk, bank0):
                if blk >= 4:
                    for a in range(4):
                        k = 4 * (blk - 4) + a
                        round_chunk(4 + 32 + k + 1, qk[:, k], h_hi[:, k])
            p = ph["conv_in"]
            for blk in range(p.blocks):
                body(p, blk, blk % 2, conv_hi)
            phase("conv_out")
            norm(8, y_tm, lambda i: (banks_free, ph["mlp2"].b))
            norm_to_y(9, 5, lambda i: (resid_ready, 12 + i + 1))
            if stop < 9:
                return
            turned_out("h_mlp2", feature_gain("h_mlp2"), a_hi)
            mlp("mlp2", 4 + 32 + 8, True)
            norm(10, y_tm, lambda i: (banks_free, n_blocks))

        @block.vector
        def _(dve):
            step = Steps(dve, dve_step)
            tt, ts, stt = nc.vector.tensor_tensor, nc.vector.tensor_scalar, nc.vector.scalar_tensor_tensor

            def split(p, blk, u, qi):
                n, s = quad_at(p, blk, qi) + 2, slot_of(p, u, qi)
                if isinstance(n, int) and n >= n_quads:
                    return
                dve.wait_ge(hi_ready, n + 1)
                tt(w_lo[:, s], w_raw[:, s], w_hi[:, s].bitcast(F32), ALU.subtract).then_inc(lo_ready, 1)

            def first_splits():
                for s in range(2):
                    dve.wait_ge(hi_ready, s + 1)
                    tt(w_lo[:, s], w_raw[:, s], w_hi[:, s].bitcast(F32), ALU.subtract).then_inc(lo_ready, 1)

            def body(p, blk, u, evac):
                for qi in range(p.quads):
                    split(p, blk, u, qi)
                dve.wait_ge(quad_done, quad_at(p, blk, p.quads))
                evac(blk, 4 * ((p.b + u) % 2))

            def phase(name, evac):
                p = ph[name]
                if p.blocks % 2:
                    return body(p, 0, 0, evac)
                for blk in pairs(dve, p):
                    for u in range(2):
                        body(p, blk + u, u, evac)

            def to_tiles(first, scale=None):
                def evac(blk, bank0):
                    dst = qk[:, bass.ds(first + 4 * blk, 4)]
                    src = ps[:, bank0:bank0 + 4]
                    if scale is None or blk:
                        nc.vector.tensor_copy(dst, src).then_inc(banks_free, 1)
                    else:
                        ts(dst, src, scale, None, ALU.mult).then_inc(banks_free, 1)
                return evac

            def to_tokens(dst):
                def evac(blk, bank0):
                    nc.vector.tensor_copy(tok_block(dst, blk), ps[:, bank0:bank0 + 4]).then_inc(banks_free, 1)
                return evac

            def add_tokens(dst):
                def evac(blk, bank0):
                    d = tok_block(dst, blk)
                    tt(d, ps[:, bank0:bank0 + 4], d, ALU.add).then_inc(banks_free, 1)
                return evac

            def lo_chunk(n, src, hi, dst):
                dve.wait_ge(chunk_hi, n)
                tt(dst, src, hi.bitcast(F32), ALU.subtract).then_inc(chunk_lo, 1)

            def mlp(name, chunks, exps, acc, last=False):
                p = ph[name]

                def rounds(r, tail=False):
                    for u in range(4):
                        blk = r * 4 + u
                        bank0 = 4 * ((p.b + u) % 2)
                        if not (tail and u == 3):
                            for qi in range(2):
                                split(p, blk, u, qi)
                        if u >= 2:
                            dve.wait_ge(quad_done, quad_at(p, blk, 2))
                            d = acc[:, :, NBLK * (u - 2):NBLK * (u - 1)]
                            tt(d, ps[:, bank0:bank0 + 4], d, ALU.add).then_inc(banks_free, 1)
                            continue
                        for c in range(2):
                            dve.wait_ge(exp_ready, exps + r * 4 + 2 * u + c + 1)
                            f = tmp4[:, 2 * c:2 * c + 2]
                            last = stt(f.rearrange("p a b -> p (a b)"), psf[:, 512 * (bank0 + 2 * c):512 * (bank0 + 2 * c + 2)], 0.0,
                                       f.rearrange("p a b -> p (a b)"), ALU.max, ALU.mult)
                            last.then_inc(chunk_f32, 1)
                        for c in range(2):
                            g = chunks + r * 4 + 2 * u + c
                            ks = slice(4 * u + 2 * c, 4 * u + 2 * c + 2)
                            dve.wait_ge(chunk_hi, g + 1)
                            tt(h_lo[:, ks], tmp4[:, 2 * c:2 * c + 2], h_hi[:, ks].bitcast(F32), ALU.subtract).then_inc(chunk_lo, 1)
                            if c == 0:
                                dve.wait_ge(chunk_f32, g + 2)
                                nc.vector.memset(small[:, 252:253], 0.0).then_inc(banks_free, 1)

                with dve.Fori(0, ROUNDS - 1 if last else ROUNDS) as r:
                    rounds(r)
                if last:
                    rounds(ROUNDS - 1, True)

            def refine(n_cols, v, y0, y1, out_, count, denom, sums, ready, v_done, guessed, done):
                dve.wait_ge(*ready)
                ts(v, sums, 1.0 / denom, EPS, ALU.mult, ALU.add).then_inc(v_done, 1)
                dve.wait_ge(*guessed)
                step(tt(y0, y1, y1, ALU.mult))
                step(tt(y0, y0, v, ALU.mult))
                step(ts(y0, y0, -0.5, 1.5, ALU.mult, ALU.add))
                tt(out_, y0, y1, ALU.mult).then_inc(done, 1)

            def rms(n):
                refine(4, var, rsq0, rsq1, rstd, n, D, sumsq, (sumsq_ready, n + 1), var_ready, (guess_ready, n + 1), rstd_ready)
                dve.wait_ge(rstd_ready, n + 1)

            def norm_to_y(n):
                rms(n)
                for i in range(3):
                    ts(y_tm[:, i], x_tm[:, i], rstd[:, i:i + 1], None, ALU.mult).then_inc(normed, 1)

            def norm_add(n, rows):
                rms(n)
                dve.wait_ge(grow_in, 16 * rows)
                for i in range(TT):
                    step(stt(y_tm[:, i], y_tm[:, i], rstd[:, i:i + 1], g_row, ALU.mult, ALU.mult))
                    tt(x_tm[:, i], x_tm[:, i], y_tm[:, i], ALU.add).then_inc(resid_ready, 1)

            def turned_out(name, gain, hi, lo):
                for k in range(turns[name]):
                    dve.wait_ge(turned_hi, turn_base[name] + k + 1)
                    src = ps[:, turn_bank(name, k)]
                    g = gain(k)
                    if g is None:
                        last = tt(lo[:, k], src, hi[:, k].bitcast(F32), ALU.subtract)
                    else:
                        last = stt(lo[:, k], src, g, hi[:, k].bitcast(F32), ALU.mult, ALU.subtract)
                    last.then_inc(turned_lo, 1)

            def feature_gain(name):
                return lambda k: gains[:, 8 * gain_of[name] + k:8 * gain_of[name] + k + 1]

            dve.wait_ge(consts_in, 48)
            nc.vector.tensor_copy(ntri[:], consts[:, K_NTRI:K_NTRI + P]).then_inc(consts_r, 1)
            nc.vector.tensor_copy(nones[:], consts[:, K_NONE:K_NONE + P]).then_inc(consts_r, 1)
            nc.vector.tensor_copy(ident_b[:], ident).then_inc(consts_r, 1)
            nc.vector.tensor_copy(causal_b[:], tmp[:, 0:P]).then_inc(consts_r, 1)
            step(nc.vector.tensor_copy(masks[:].rearrange("p a b -> p (a b)"), masks_f))
            dve.wait_ge(gains_turned, 1)
            nc.vector.tensor_copy(gains[:, 0:N_GAINS], ps[:, 7, 0:N_GAINS]).then_inc(gains_out, 1)
            dve.wait_ge(gains_out, 1)
            norm_to_y(0)
            step(ts(gains[:, N_GAINS:N_GAINS + 1], gains[:, G_SUBLN:G_SUBLN + 1], 1.0 - LAMBDA_INIT, None, ALU.mult))
            turned_out("h", feature_gain("h"), a_hi, a_lo)
            first_splits()
            phase("sb_qk", to_tiles(0, SB_DIM ** -0.5))
            phase("sb_v", lambda blk, bank0: nc.vector.tensor_copy(v_sb, ps[:, bank0:bank0 + 4]).then_inc(banks_free, 1))
            if stop < 1:
                return

            def sb_softplus(t, u):
                dve.wait_ge(soft_log, t + 1)
                if not (isinstance(t, int) and t < 2):
                    dve.wait_ge(sp_lo, t - 1)
                stt(sb_sp[u], psf[:, 1536 * u:1536 * u + TRI], 0.0, sb_t[u], ALU.max, ALU.add).then_inc(sp_made, 1)
                dve.wait_ge(sp_made, t + 1)
                diag = sb_sp[u][:, 0:512].rearrange("p (a b) -> p a b", a=TT)
                tt(diag, diag, strict.rearrange("p (a b) -> p a b", a=1).to_broadcast([P, TT, P]), ALU.mult).then_inc(sp_masked, 1)
                dve.wait_ge(sp_hi, t + 1)
                tt(sb_lo[u], sb_sp[u], sb_hi[u].bitcast(F32), ALU.subtract).then_inc(sp_lo, 1)

            def sb_out(t, u):
                dve.wait_ge(sb_pv, t + 1)
                nc.vector.tensor_copy(o_sb[:, :, bass.ds(SB_DIM * t, SB_DIM)],
                                      ps[:, 6 + u, 0:SB_DIM * TT].rearrange("p (a b) -> p a b", a=TT)).then_inc(osb_out, 1)

            for t in range(2):
                sb_softplus(t, t)
            with dve.Fori(1, SB_HEADS // 2) as i:
                for u in range(2):
                    t = i * 2 + u
                    sb_softplus(t, u)
                    sb_out(t - 2, u)
            for u in range(2):
                sb_out(SB_HEADS - 2 + u, u)
            turned_out("o_sb", lambda k: None, h_hi, h_lo)
            if stop < 2:
                return
            phase("g_qk", to_tiles(8, GLA_DK ** -0.5))
            dve.wait_ge(low_split_hi, 1)
            tt(hlf[:, 2048:3072], tmp[:, 0:1024], hhf[:, 2048:3072].bitcast(F32), ALU.subtract).then_inc(low_split, 1)
            phase("g_v", to_tokens(x_tm))

            dve.wait_ge(low_mm, 1)
            nc.vector.tensor_copy(low_t, ps[0:GLA_RANK, low_bank]).then_inc(low_out, 1)
            dve.wait_ge(gate_u, 1)
            step(ts(m_min, tmp, 0.0, None, ALU.min))
            dve.wait_ge(gate_log, 1)
            step(tt(m_min, m_min, u_abs, ALU.subtract))
            step(ts(m_min, m_min, 1.0 / GLA_TAU, None, ALU.mult))
            keep = arena[:, 0:2048]
            step(nc.vector.memset(keep, 1.0))
            step(nc.vector.memset(keep.rearrange("p (m n) -> p m n", n=P)[:, :, 0:1], 0.0))
            nc.vector.tensor_tensor_scan(b_cum, keep, m_min, 0.0, ALU.mult, ALU.add).then_inc(b_ready, 1)

            def silu(blk, bank0):
                for c in range(2):
                    d = tok_cols(y_tm, blk, c)
                    dve.wait_ge(exp_ready, 2 * blk + c + 1)
                    step(ts(d, d, 1.0, None, ALU.add))
                    step(nc.vector.reciprocal(d, d))
                    last = tt(d, ps[:, bank0 + 2 * c:bank0 + 2 * c + 2], d, ALU.mult)
                    step(last) if c == 0 else last.then_inc(banks_free, 1)
            phase("g_out", silu)
            if stop < 3:
                return

            step(nc.vector.memset(g_at, 0.0))
            dve.wait_ge(b_ready, 1)
            b_chunk = b_cum.rearrange("p (m n) -> p m n", n=P)

            def level_diff(n):
                h = 1 << n
                if n >= 2:
                    dve.wait_ge(g_mm, n)
                b2 = b_cum.rearrange("p (m two n) -> p m two n", two=2, n=h)
                f2 = g_f[n % 2].rearrange("p (m two n) -> p m two n", two=2, n=h)
                mid = b2[:, :, 0, h - 1:h].to_broadcast([P, 2048 // (2 * h), h])
                tt(f2[:, :, 1], b2[:, :, 1], mid, ALU.subtract)
                tt(f2[:, :, 0], mid, b2[:, :, 0], ALU.subtract).then_inc(g_diff, 1)

            def level_factor(n):
                h = 1 << n
                dve.wait_ge(g_exp, n + 1)
                f2, q2, k2 = (z.rearrange("p (m two n) -> p m two n", two=2, n=h) for z in (g_f[n % 2], g_q, g_k))
                tt(f2[:, :, 1], f2[:, :, 1], q2[:, :, 1], ALU.mult)
                tt(f2[:, :, 0], f2[:, :, 0], k2[:, :, 0], ALU.mult).then_inc(g_fac, 1)

            def level_select(n):
                dve.wait_ge(g_mm, n + 1)
                if n:
                    dve.wait_ge(g_sel, n)
                nc.vector.copy_predicated(g_at.rearrange("p (m n) -> p m n", n=P),
                                          masks[:, n:n + 1].to_broadcast([P, 16, P]),
                                          psf[:, 2048 * (n % 2):2048 * (n % 2 + 1)].rearrange("p (m n) -> p m n", n=P)).then_inc(g_sel, 1)

            level_diff(0)
            level_diff(1)
            level_factor(0)
            for n in range(2, LEVELS):
                level_select(n - 2)
                level_factor(n - 1)
                level_diff(n)
            level_select(LEVELS - 2)
            level_factor(LEVELS - 1)
            dve.wait_ge(g_mm, LEVELS)
            step(nc.vector.tensor_copy(g_f[LEVELS % 2], b_cum))
            nc.vector.memset(small[:, 253:254], 0.0).then_inc(g_diff, 1)
            level_select(LEVELS - 1)
            dve.wait_ge(g_mm, LEVELS + 1)
            tt(g_f[(LEVELS + 1) % 2].rearrange("p (m n) -> p m n", n=P), b_chunk[:, :, P - 1:P].to_broadcast([P, 16, P]), b_chunk,
               ALU.subtract).then_inc(g_diff, 1)
            level_select(LEVELS)
            dve.wait_ge(g_exp, LEVELS + 2)
            tt(g_k, g_k, g_f[(LEVELS + 1) % 2], ALU.mult).then_inc(kd_ready, 1)
            step(tt(g_q, g_q, g_f[LEVELS % 2], ALU.mult))
            dve.wait_ge(kd_turned, 1)
            nc.vector.tensor_copy(g_kt, psf[:, 0:1536]).then_inc(kd_out, 1)
            dve.wait_ge(st_mm, 1)
            dve.wait_ge(g_exp, LEVELS + 3)
            step(nc.vector.tensor_copy(g_state[0], psf[:, 1024:2048]))
            nc.vector.memset(small[:, 254:255], 0.0).then_inc(st_ready, 1)
            for c in range(1, 3):
                for h in range(GLA_HEADS):
                    hs = slice(GLA_DV * h, GLA_DV * (h + 1))
                    last = stt(g_state[c][:, hs], g_state[c - 1][:, hs], elast[:, 4 * h + c:4 * h + c + 1],
                               psf[:, 1024 * (c + 1) + GLA_DV * h:1024 * (c + 1) + GLA_DV * (h + 1)], ALU.mult, ALU.add)
                step(last)
                nc.vector.memset(small[:, 254:255], 0.0).then_inc(st_ready, 1)
            for c in range(2, 4):
                dve.wait_ge(go_mm, c + 1)
                nc.vector.tensor_copy(g_o[:, 1024 * c:1024 * (c + 1)], psf[:, 1024 * c:1024 * (c + 1)]).then_inc(go_dve, 1)
            refine(16, gvar, grs0, grs1, grstd, 0, GLA_DV, gss, (gss_ready, 1), gvar_ready, (ggs_ready, 1), sem_grstd)
            dve.wait_ge(sem_grstd, 1)
            for m in range(16):
                i, h = m // 4, m % 4
                ys = y_tm[:, i, GLA_DV * h:GLA_DV * (h + 1)]
                last = stt(ys, g_o[:, GLA_DV * m:GLA_DV * (m + 1)], grstd[:, m:m + 1], ys, ALU.mult, ALU.mult)
                if h == 3:
                    last.then_inc(gout_ready, 1)
            if stop < 4:
                return

            def sigmoid(tiles, base):
                def evac(blk, bank0):
                    for c in range(2):
                        d = fm_tiles(tiles, blk, c)
                        dve.wait_ge(exp_ready, base + 2 * blk + c + 1)
                        step(ts(d, d, 1.0, None, ALU.add))
                        last = nc.vector.reciprocal(d, d)
                        if c:
                            last.then_inc(banks_free, 1)
                return evac
            dve.wait_ge(gout_ready, 4)
            phase("gate_sb", sigmoid(gates_sb, 4))
            phase("gate_gla", sigmoid(gates_gla, 8))
            turned_out("o_gla", lambda k: gains[:, G_GLA + k % 2:G_GLA + k % 2 + 1], a_hi, a_lo)

            def mix_sb(blk, bank0):
                d = gates_sb.rearrange("p (a b) -> p a b", a=8)[:, 4 * blk:4 * blk + 4]
                tt(d, ps[:, bank0:bank0 + 4], d, ALU.mult).then_inc(banks_free, 1)

            def mix_gla(blk, bank0):
                for c in range(2):
                    f = tmp4[:, 2 * c:2 * c + 2]
                    last = tt(f, ps[:, bank0 + 2 * c:bank0 + 2 * c + 2], fm_tiles(gates_gla, blk, c), ALU.mult)
                    if c:
                        last.then_inc(banks_free, 1)
                step(nc.vector.memset(small[:, 255:256], 0.0))
                for c in range(2):
                    f = tmp4[:, 2 * c:2 * c + 2]
                    tt(f, f, fm_tiles(gates_sb, blk, c), ALU.add).then_inc(chunk_f32, 1)
                for c in range(2):
                    ks = slice(4 * blk + 2 * c, 4 * blk + 2 * c + 2)
                    lo_chunk(2 * blk + c + 1, tmp4[:, 2 * c:2 * c + 2], h_hi[:, ks], h_lo[:, ks])
                dve.wait_ge(chunk_lo, 2 * blk + 2)
            phase("proj_sb", mix_sb)
            dve.wait_ge(banks_free, ph["proj_gla"].b)
            phase("proj_gla", mix_gla)
            dve.wait_ge(x_again, 16)
            phase("w_out", add_tokens(x_tm))
            if stop < 5:
                return
            norm_to_y(1)
            turned_out("h_mlp0", feature_gain("h_mlp0"), a_hi, a_lo)
            mlp("mlp0", 4, EXPS, x_tm)
            rms(2)
            dve.wait_ge(grow_in, 16)
            for i in range(TT):
                stt(x_tm[:, i], x_tm[:, i], rstd[:, i:i + 1], g_row, ALU.mult, ALU.mult).then_inc(resid_ready, 1)
            norm_to_y(3)
            if stop < 6:
                return
            turned_out("h_mix1", feature_gain("h_mix1"), a_hi, a_lo)

            for u in range(2):
                step(nc.vector.memset(rot[u], 0.0))
            dve.wait_ge(tables_in, 80)
            prod = stat[:, 0:4].rearrange("p a b -> p (a b)")
            step(tt(prod.rearrange("p (a b) -> p a b", a=2), lam_in[:, 0:4:2], lam_in[:, 1:4:2], ALU.mult))
            nc.vector.tensor_reduce(lam[:, 0:2], prod.rearrange("p (a b) -> p a b", a=2), AX.X, ALU.add).then_inc(lam_sum, 1)

            def rope(blk):
                sw = rot[blk % 2].rearrange("p (a b) -> p a b", a=4)
                tiles = qk[:, 4 * blk:4 * blk + 4]
                dve.wait_ge(swapped[blk % 2], 64 * (blk // 2 + 1))
                step(tt(sw, sw, sin_t.rearrange("p (a b) -> p a b", a=1).to_broadcast([P, 4, SEQ]), ALU.mult))
                step(tt(tiles, tiles, cos_t.rearrange("p (a b) -> p a b", a=1).to_broadcast([P, 4, SEQ]), ALU.mult))
                tt(tiles, tiles, sw, ALU.add).then_inc(rope_done, 1)

            p = ph["qk"]
            for blk in range(4):
                for qi in range(2):
                    split(p, blk, blk % 2, qi)
                dve.wait_ge(quad_done, quad_at(p, blk, 2))
                bank0 = 4 * ((p.b + blk) % 2)
                dst, src = qk[:, 4 * blk:4 * blk + 4], ps[:, bank0:bank0 + 4]
                if blk < 2:
                    step(ts(dst, src, DIFF_DIM ** -0.5, None, ALU.mult))
                else:
                    step(nc.vector.tensor_copy(dst, src))
                if blk >= 2:
                    dve.wait_ge(rope_done, blk - 1)
                nc.vector.memset(small[:, 248:249], 0.0).then_inc(banks_free, 1)
                nc.vector.memset(small[:, 249:250], 0.0).then_inc(rope_src, 1)
                if blk:
                    rope(blk - 1)
            rope(3)
            phase("v", to_tokens(y_tm))
            dve.wait_ge(v_hi, 1)
            tt(alf, yf, ahf.bitcast(F32), ALU.subtract).then_inc(v_lo, 1)
            dve.wait_ge(lam_exp, 1)
            step(tt(lam[:, 4:5], lam[:, 3:4], lam[:, 2:3], ALU.subtract))
            step(ts(lam[:, 5:6], lam[:, 4:5], LAMBDA_INIT, None, ALU.subtract))

            def diff_max(t, u, c):
                dve.wait_ge(s_mm[c], t + 1)
                if not (isinstance(t, int) and t < 2):
                    dve.wait_ge(s_exp[c], t - 1)
                for i in range(TT):
                    n = P * (i + 1)
                    last = nc.vector.tensor_reduce(nmax[:, u, c, i:i + 1], psf[:, 1536 * c + ROW[i]:1536 * c + ROW[i] + n],
                                                   AX.X, ALU.max, negate=True)
                last.then_inc(s_max[c], 1)

            def diff_mix(t, u):
                dve.wait_ge(s_exp[0], t + 1)
                dve.wait_ge(s_exp[1], t + 1)
                if not (isinstance(t, int) and t < 2):
                    dve.wait_ge(o_out, t - 1)
                nc.vector.reciprocal(drec[:, u], dsum[:, u]).then_inc(rec_made, 1)
                dve.wait_ge(rec_made, t + 1)
                stt(nmax[:, u, 1], drec[:, u, 1], lam[:, 5:6], dsum[:, u, 0], ALU.mult, ALU.mult).then_inc(ratio_made, 1)
                dve.wait_ge(ratio_made, t + 1)
                for i in range(TT):
                    n = P * (i + 1)
                    cs = slice(ROW[i], ROW[i] + n)
                    last = stt(d_p[u][0][:, cs], d_p[u][1][:, cs], nmax[:, u, 1, i:i + 1], d_p[u][0][:, cs], ALU.mult, ALU.add)
                last.then_inc(p_mixed, 1)

            def diff_lo(t, u, b):
                n = len_batch[b]
                dve.wait_ge(pt_hi, 3 * t + b + 1)
                cs = slice(512 * b, 512 * b + n)
                tt(sb_lo[u][:, cs], ps[:, 6, 0:n], sb_hi[u][:, cs].bitcast(F32), ALU.subtract).then_inc(pt_lo, 1)

            def diff_sumsq(t, u):
                dve.wait_ge(o_sq, t + 1)
                nc.vector.tensor_reduce(dss[:, bass.ds(TT * t, TT)], d_sq[u].rearrange("p (a b) -> p a b", a=TT), AX.X, ALU.add).then_inc(o_ss, 1)

            diff_max(0, 0, 0)
            diff_max(0, 0, 1)
            diff_mix(0, 0)
            diff_max(1, 1, 0)
            diff_lo(0, 0, 0)
            diff_max(1, 1, 1)
            diff_lo(0, 0, 1)
            diff_lo(0, 0, 2)
            diff_mix(1, 1)
            with dve.Fori(1, DIFF_HEADS // 2) as i:
                for u in range(2):
                    t = i * 2 + u
                    diff_max(t, u, 0)
                    diff_lo(t - 1, 1 - u, 0)
                    diff_max(t, u, 1)
                    diff_lo(t - 1, 1 - u, 1)
                    diff_lo(t - 1, 1 - u, 2)
                    diff_mix(t, u)
                    diff_sumsq(t - 2, u)
            for b in range(3):
                diff_lo(DIFF_HEADS - 1, 1, b)
            for u in range(2):
                diff_sumsq(DIFF_HEADS - 2 + u, u)
            dve.wait_ge(o_ss, DIFF_HEADS)
            refine(32, dvar, drs0, drs1, drstd, 0, DIFF_V, dss, (o_ss, DIFF_HEADS), ovar_ready, (ogs_ready, 1), sem_orstd)
            dve.wait_ge(sem_orstd, 1)
            for g in range(4):
                o = qk[:, 2 * g:2 * g + 2].rearrange("p a (i e) -> p (a i) e", e=P)
                r = drstd[:, 8 * g:8 * g + 8].rearrange("p (n one) -> p n one", one=1).to_broadcast([P, 8, P])
                tt(o, o, r, ALU.mult).then_inc(o_normed, 1)
            turned_out("o_diff", lambda k: gains[:, N_GAINS:N_GAINS + 1], a_hi, a_lo)
            if stop < 7:
                return
            phase("w_o", to_tokens(y_tm))
            norm_add(4, 2)
            norm_to_y(5)
            turned_out("h_mlp1", feature_gain("h_mlp1"), a_hi, a_lo)
            clear_y(dve)
            mlp("mlp1", 4 + 16, EXPS + 16, y_tm)
            norm_add(6, 3)
            norm_to_y(7)
            if stop < 8:
                return
            turned_out("h_conv", feature_gain("h_conv"), a_hi, a_lo)

            def conv(k):
                u_, y_ = y_fm[:, k], qk[:, 8 + k]
                step(ts(y_, u_, convw[:, 2, k:k + 1], None, ALU.mult))
                step(stt(y_[:, 1:SEQ], u_[:, 0:SEQ - 1], convw[:, 1, k:k + 1], y_[:, 1:SEQ], ALU.mult, ALU.add))
                step(stt(y_[:, 2:SEQ], u_[:, 0:SEQ - 2], convw[:, 0, k:k + 1], y_[:, 2:SEQ], ALU.mult, ALU.add))
                tt(qk[:, k], qk[:, k], y_, ALU.mult).then_inc(chunk_f32, 1)
                lo_chunk(4 + 32 + k + 1, qk[:, k], h_hi[:, k], h_lo[:, k])

            p = ph["conv_in"]
            for blk in range(p.blocks):
                for qi in range(2):
                    split(p, blk, blk % 2, qi)
                dve.wait_ge(quad_done, quad_at(p, blk, 2))
                bank0 = 4 * ((p.b + blk) % 2)
                src = ps[:, bank0:bank0 + 4]
                if blk < 4:
                    nc.vector.tensor_copy(qk[:, 4 * blk:4 * blk + 4], src).then_inc(banks_free, 1)
                    continue
                g = 4 * (blk - 4)
                dve.wait_ge(banks_free, p.b + blk)
                tt(y_fm[:, g:g + 4], src, qk[:, 8 + g:12 + g], ALU.mult).then_inc(banks_free, 1)
                dve.wait_ge(banks_free, p.b + blk + 1)
                for a in range(4):
                    conv(g + a)
            phase("conv_out", to_tokens(y_tm))
            norm_add(8, 4)
            norm_to_y(9)
            if stop < 9:
                return
            turned_out("h_mlp2", feature_gain("h_mlp2"), a_hi, a_lo)
            clear_y(dve)
            mlp("mlp2", 4 + 32 + 8, EXPS + 32, y_tm, True)
            norm_add(10, 5)


_OUT = ((1, SEQ, D), "float32")
_INS = ["x", "norm_mix", "w_in", "w_gate_up", "b_gate_up", "gla_norm", "w_proj_sb", "w_proj_gla", "w_out", "norm_mlp",
        "w_ff1", "w_ff2", "norm_final", "attn_w_qkv_2", "attn_w_o_2", "attn_lambda_q1_2", "attn_lambda_k1_2",
        "attn_lambda_q2_2", "attn_lambda_k2_2", "attn_subln_g_2", "conv_w_in_2", "conv_w_2", "conv_w_out_2",
        "mlp_w_up_2", "mlp_w_down_2", "norm_mixer_pre_2", "norm_mixer_post_2", "norm_mlp_pre_2", "norm_mlp_post_2"]


def kernel(**inputs):
    import concourse.bacc as bacc
    from concourse.bass_utils import run_bass_kernel_spmd

    nc = bacc.Bacc("TRN2", target_bir_lowering=False, num_devices=1)
    arrays, args = {}, {}
    for name, a in [(n, np.ascontiguousarray(inputs[n])) for n in _INS] + [("shape_consts", shape_constants())]:
        arrays[f"in_{name}"] = a
        args[name] = nc.dram_tensor(f"in_{name}", a.shape, mybir.dt.from_np(a.dtype), kind="ExternalInput").ap()
    out = nc.dram_tensor("out", _OUT[0], mybir.dt.from_np(np.dtype(_OUT[1])), kind="ExternalOutput").ap()
    build(nc, args, out)
    result = run_bass_kernel_spmd(nc, [arrays], core_ids=[0])
    return result.results[0]["out"]
```

```python
from contextlib import ExitStack

import numpy as np

import concourse.bass as bass
from concourse import mybir

F32 = mybir.dt.float32
F32R = mybir.dt.float32r
BF16 = mybir.dt.bfloat16
U8 = mybir.dt.uint8
ALU = mybir.AluOpType
ACT = mybir.ActivationFunctionType
AX = mybir.AxisListType

P = 128
SEQ = 512
D = 1024
TT = SEQ // P
KT = D // P
NBLK = 512
QUAD = 4
EPS = 1e-6
GATE_MIN = -43.0

SB_HEADS, SB_DIM = 8, 64
GLA_HEADS, GLA_DK, GLA_DV, GLA_RANK, GLA_TAU = 4, 128, 256, 16, 16.0
DIFF_HEADS, DIFF_DIM, DIFF_V = 8, 64, 128
N_GAINS = 2 + 1 + GLA_HEADS + 3 * KT
ROT, THETA = 16, 500000.0
LAMBDA_INIT = 0.8 - 0.6
D_FF = 4096
ROUNDS = D_FF // D
LEVELS = 7

C_SBQ, C_SBK, C_SBV = 0, 512, 1024
C_GQ, C_GK, C_GV, C_GOUT, C_LOW = 1536, 2048, 2560, 3584, 4608
C_GATE_SB, C_GATE_GLA = 4624, 5648

K_ID, K_NTRI, K_NONE, K_STRICT, K_CAUSAL, K_COS, K_SIN, K_MASKS = 0, 128, 256, 384, 512, 640, 1152, 1664
K_ALL = K_MASKS + (LEVELS + 1) * P

TRI = 10 * P
COL = {0: 0, 1: 512, 3: 896, 2: 1024}
AFTER = {0: TRI, 1: TRI + 3 * P, 2: TRI + 5 * P}
TRI_AFTER = TRI + 6 * P
ROW = {3: 0, 2: 512, 0: 896, 1: 1024}


class Phase:

    def __init__(self, name, blocks, quads=2):
        self.name, self.blocks, self.quads = name, blocks, quads
        self.q = self.b = 0


def plan():
    names = [Phase("sb_qk", 2), Phase("sb_v", 1), Phase("g_qk", 2), Phase("g_v", 2), Phase("g_out", 2),
             Phase("gate_sb", 2), Phase("gate_gla", 2), Phase("proj_sb", 2, 1), Phase("proj_gla", 2),
             Phase("w_out", 2), Phase("mlp0", 4 * ROUNDS), Phase("qk", 4), Phase("v", 2), Phase("w_o", 2),
             Phase("mlp1", 4 * ROUNDS), Phase("conv_in", 6), Phase("conv_out", 2), Phase("mlp2", 4 * ROUNDS)]
    q = b = 0
    for ph in names:
        ph.q, ph.b = q, b
        q += ph.blocks * ph.quads
        b += ph.blocks
    return {ph.name: ph for ph in names}, q, b


def shape_constants():
    c = np.zeros((P, K_ALL), np.float32)
    r, s = np.arange(P)[:, None], np.arange(P)[None, :]
    c[:, K_ID:K_ID + P] = r == s
    c[:, K_NTRI:K_NTRI + P] = np.where(r >= s, -1.0, 0.0)
    c[:, K_NONE:K_NONE + P] = -1.0
    c[:, K_STRICT:K_STRICT + P] = s > r
    c[:, K_CAUSAL:K_CAUSAL + P] = np.where(s > r, -1e30, 0.0)
    half = ROT // 2
    inv = np.float32(THETA) ** (-np.arange(0, ROT, 2, dtype=np.float32) / np.float32(ROT))
    ang = np.arange(SEQ, dtype=np.float32)[None, :] * inv[:, None].astype(np.float32)
    cos, sin = np.ones((P, SEQ), np.float32), np.zeros((P, SEQ), np.float32)
    for base in (0, DIFF_DIM):
        for part, sign in ((0, -1.0), (half, 1.0)):
            cos[base + part:base + part + half] = np.cos(ang)
            sin[base + part:base + part + half] = sign * np.sin(ang)
    c[:, K_COS:K_COS + SEQ] = cos
    c[:, K_SIN:K_SIN + SEQ] = sin
    c[:, K_MASKS:K_MASKS + P] = r == s
    for n in range(LEVELS):
        h = 1 << n
        m = K_MASKS + P * (n + 1)
        c[:, m:m + P] = (r // (2 * h) == s // (2 * h)) & (r % (2 * h) < h) & (s % (2 * h) >= h)
    return c


def build(nc, w, out, stop=99):
    ph, n_quads, n_blocks = plan()
    ctx = ExitStack()
    with ctx:
        def sb(name, shape, dt=F32):
            return ctx.enter_context(nc.sbuf_tensor(name, shape, dt))

        def twin(name, shape, dt):
            return nc.alloc_sbuf_tensor_at(name, shape, dt, offset=-(-nc.sbuf_base // 32) * 32)

        sems = {}

        def sem(name):
            sems[name] = ctx.enter_context(nc.semaphore(name))
            return sems[name]

        x_r = twin("x_r", [P, TT * D], F32R)
        x_tm = sb("x_tm", [P, TT, D])
        a_hi = sb("a_hi", [P, KT, SEQ], F32R)
        a_lo = sb("a_lo", [P, KT, SEQ], F32R)
        h_hi = sb("h_hi", [P, KT, SEQ], F32R)
        h_lo_f = twin("h_lo_f", [P, KT * SEQ], F32)
        h_lo = sb("h_lo", [P, KT, SEQ], F32R)
        w_raw = sb("w_raw", [P, 2, QUAD, NBLK])
        w_hi = sb("w_hi", [P, 2, QUAD, NBLK], F32R)
        w_lo = sb("w_lo", [P, 2, QUAD, NBLK], F32R)
        y_r = twin("y_r", [P, TT * D], F32R)
        y_tm = sb("y_tm", [P, TT, D])
        qk_r = twin("qk_r", [P, 16, SEQ], F32R)
        qk = sb("qk", [P, 16, SEQ])
        arena_r = twin("arena_r", [P, 6144], F32R)
        arena = sb("arena", [P, 6144])
        consts = sb("consts", [P, K_STRICT + P])
        masks = sb("masks", [P, LEVELS + 1, P], U8)
        ntri = sb("ntri", [P, P], F32R)
        nones = sb("nones", [P, P], F32R)
        ident_b = sb("ident_b", [P, P], BF16)
        causal_b = sb("causal_b", [P, P], BF16)
        strict_b = sb("strict_b", [P, P], BF16)
        gains = sb("gains", [P, N_GAINS + 1])
        b_gate = gains[:, 3:7]
        convw = gains[:, 7:31].rearrange("p (a b) -> p a b", a=3)
        small = sb("small", [P, 256])
        stat = sb("stat", [P, 7, DIFF_HEADS * TT])
        ps = ctx.enter_context(nc.psum_tensor("ps", [P, 8, 512], F32))
        psf = ps[:].rearrange("p b n -> p (b n)")

        xf = x_tm[:].rearrange("p a b -> p (a b)")
        yf = y_tm[:].rearrange("p a b -> p (a b)")
        hhf = h_hi[:].rearrange("p a b -> p (a b)")
        hlf = h_lo[:].rearrange("p a b -> p (a b)")
        qkf = qk[:].rearrange("p a b -> p (a b)")
        y_fm = yf.rearrange("p (a b) -> p a b", a=KT)
        ident = consts[:, K_ID:K_ID + P]
        strict = consts[:, K_STRICT:K_STRICT + P]
        b_cum = arena[:, 2048:4096]
        tmp = arena[:, 4096:6144]
        w_up16 = arena[0:GLA_RANK, 0:GLA_HEADS * GLA_DK]
        lam_in = tmp[:, 2 * SEQ:2 * SEQ + 4 * DIFF_DIM].rearrange("p (a b) -> p a b", a=4)
        masks_f = arena[:, 0:(LEVELS + 1) * P]
        gain_rows = tmp[:, P:2 * P]
        tmp4 = tmp.rearrange("p (a b) -> p a b", a=4)

        junk = qkf[:, 0:1024]
        g_add, g_turn = qkf[:, 7168:8192], qkf[:, 6144:7168]
        sb_t = [yf[:, 1280 * u:1280 * (u + 1)] for u in range(2)]
        sb_sp = [h_lo_f[:, 2048 * u:2048 * (u + 1)] for u in range(2)]
        sb_lo = [hlf[:, 2048 * u:2048 * (u + 1)] for u in range(2)]
        sb_hi = [hhf[:, 2048 * u:2048 * (u + 1)] for u in range(2)]
        sb_w = [xf[:, 1280 * u:1280 * (u + 1)] for u in range(2)]
        sb_wlo = [x_r[:, 1280 * u:1280 * (u + 1)] for u in range(2)]
        sb_whi = [x_r[:, 2560:3840], y_r[:, 2560:3840]]
        sbq_hi, sbq_lo = qk_r[:, 0:8], qk_r[:, 8:16]
        sbv_hi = arena_r[:, 0:2048].rearrange("p (a b) -> p a b", a=TT)
        sbv_lo = arena_r[:, 2048:4096].rearrange("p (a b) -> p a b", a=TT)
        o_sb = tmp4
        g_q, g_k = qkf[:, 4096:6144], qkf[:, 6144:8192]
        g_f = [qkf[:, 0:2048], qkf[:, 2048:4096]]
        g_at = arena[:, 0:2048]
        g_kt = tmp[:, 0:1536]
        g_state = [arena[:, 2048:3072], arena[:, 3072:4096], tmp[:, 0:1024]]
        g_o = qkf[:, 0:4096]
        ahf = a_hi[:].rearrange("p a b -> p (a b)")
        alf = a_lo[:].rearrange("p a b -> p (a b)")
        d_p = [[arena[:, 2560 * u + 1280 * c:2560 * u + 1280 * (c + 1)] for c in range(2)] for u in range(2)]
        d_hi = [y_r[:, 0:1280], y_r[:, 1280:2560]]

        def d_lo(u, c, n):
            if u == 0:
                return y_r[:, 2560 + c:2560 + c + n]
            return arena_r[:, 5120 + c:5120 + c + n] if c < 1024 else y_r[:, 2816 + c:2816 + c + n]

        diff_qk_hi = (h_hi, h_lo)
        rot = [arena[:, 0:2048], arena[:, 2048:4096]]
        cos_t, sin_t = tmp[:, 0:SEQ], tmp[:, SEQ:2 * SEQ]
        gates_sb, gates_gla = qkf[:, 0:4096], qkf[:, 4096:8192]

        sumsq, var, log_var, guess0, newton, rstd = (
            [small[:, 170 + 8 * n + 4 * u:174 + 8 * n + 4 * u] for u in range(2)] for n in range(6))
        eps_col = small[:, 0:1]
        gss, gvar, grs0, grs1, grstd = (small[:, 20 + 16 * n:36 + 16 * n] for n in range(5))
        elast = small[:, 100:116]
        nmax = small[:, 116:132].rearrange("p (u c i) -> p u c i", u=2, c=2)
        dsum = small[:, 132:148].rearrange("p (u c i) -> p u c i", u=2, c=2)
        drec = stat[:, 5:7]
        lam = small[:, 164:170]
        dss, dvar, drs0, drs1, drstd = (stat[:, n] for n in range(5))

        raw_full = [sem("raw_full0"), sem("raw_full1")]
        x_in = [sem(f"x_in{i}") for i in range(TT)]
        consts_in = sem("consts_in")
        gains_in = sem("gains_in")
        low_in = sem("low_in")
        x_again = sem("x_again")
        tables_in = sem("tables_in")
        swapped = [sem(f"swapped{i}") for i in range(2)]
        grow_in = sem("grow_in")
        y_clear, up_in = sem("y_clear"), sem("up_in")
        consts_r = sem("consts_r")
        out_sent = sem("out_sent")
        quad_done = sem("quad_done")
        turned = sem("turned")
        hi_ready = sem("hi_ready")
        exp_ready = sem("exp_ready")
        chunk_hi = sem("chunk_hi")
        turned_hi = sem("turned_hi")
        sumsq_ready = sem("sumsq_ready")
        guess_ready = sem("guess_ready")
        act_step = sem("act_step")
        lo_ready = sem("lo_ready")
        banks_free = sem("banks_free")
        chunk_f32 = sem("chunk_f32")
        chunk_lo = sem("chunk_lo")
        turned_lo = sem("turned_lo")
        rstd_ready = sem("rstd_ready")
        normed = sem("normed")
        resid_ready = sem("resid_ready")
        tile_done = sem("tile_done")
        tile_out = sem("tile_out")
        eps_set = sem("eps_set")
        pool_step = sem("pool_step")
        dve_step = sem("dve_step")
        z_ready, sb_abs, sb_exp, soft_log = sem("z_ready"), sem("sb_abs"), sem("sb_exp"), sem("soft_log")
        sp_made, sp_summed, sp_hi, sp_lo = sem("sp_made"), sem("sp_summed"), sem("sp_hi"), sem("sp_lo")
        c_ready, w_exp, sbw_lo = sem("c_ready"), sem("w_exp"), sem("sbw_lo")
        sp_pair, sp_after = sem("sp_pair"), sem("sp_after")
        qkv_hi, osb_hi, osb_lo = sem("qkv_hi"), sem("osb_hi"), sem("osb_lo")
        sb_pv, osb_out = sem("sb_pv"), sem("osb_out")
        low_split, low_mm, low_out, up_mm = sem("low_split"), sem("low_mm"), sem("low_out"), sem("up_mm")
        gate_log, b_ready = sem("gate_log"), sem("b_ready")
        g_diff, g_exp, g_fac, g_mm, g_sel = sem("g_diff"), sem("g_exp"), sem("g_fac"), sem("g_mm"), sem("g_sel")
        kd_ready, kd_turned, kd_out = sem("kd_ready"), sem("kd_turned"), sem("kd_out")
        st_mm, st_ready, go_mm, go_act, go_dve = sem("st_mm"), sem("st_ready"), sem("go_mm"), sem("go_act"), sem("go_dve")
        gss_ready, gvar_ready, ggs_ready, gout_ready = sem("gss_ready"), sem("gvar_ready"), sem("ggs_ready"), sem("gout_ready")
        rope_src, rope_done, lam_sum, lam_exp = sem("rope_src"), sem("rope_done"), sem("lam_sum"), sem("lam_exp")
        v_hi, v_lo, qk_hi, qk_lo = sem("v_hi"), sem("v_lo"), sem("qk_hi"), sem("qk_lo")
        s_mm = [sem("s_mm0"), sem("s_mm1")]
        s_max = [sem("s_max0"), sem("s_max1")]
        s_exp = [sem("s_exp0"), sem("s_exp1")]
        rec_made, ratio_made, p_mixed = sem("rec_made"), sem("ratio_made"), sem("p_mixed")
        p_turned, pt_hi, pt_lo, o_mm, o_out = sem("p_turned"), sem("pt_hi"), sem("pt_lo"), sem("o_mm"), sem("o_out")
        ovar_ready, ogs_ready, o_normed = sem("ovar_ready"), sem("ogs_ready"), sem("o_normed")

        junctions = {"h": (None, None, None, 0, 0, 0), "h_mlp0": (0, None, None, 0, 1, 1),
                     "h_mix1": (3 * 4, "F", 2, 0, 3, 2), "h_mlp1": (3 * 5, "P", 4, 1, 5, 3),
                     "h_conv": (3 * 9, "P", 6, 2, 7, 4), "h_mlp2": (3 * 10, "P", 8, 3, 9, 5),
                     "out": (3 * 14, "P", 10, 4, None, 6)}
        after_block = {"h": 0, "h_mlp0": ph["mlp0"].b, "h_mix1": ph["qk"].b, "h_mlp1": ph["mlp1"].b,
                       "h_conv": ph["conv_in"].b, "h_mlp2": ph["mlp2"].b, "out": n_blocks}
        turns = {"h": 8, "o_gla": 8, "h_mlp0": 8, "h_mix1": 8, "o_diff": 8, "h_mlp1": 8,
                 "h_conv": 8, "h_mlp2": 8}
        turn_base, n = {}, 0
        for name, k in turns.items():
            turn_base[name] = n
            n += k
        turn_banks = {"h": 0, "o_gla": ph["proj_sb"].b % 2, "h_mlp0": ph["mlp0"].b % 2,
                      "h_mix1": ph["qk"].b % 2, "o_diff": ph["w_o"].b % 2, "h_mlp1": ph["mlp1"].b % 2,
                      "h_conv": ph["conv_in"].b % 2, "h_mlp2": ph["mlp2"].b % 2}
        G_GLA, G_SUBLN = 0, 2

        GAIN_LOADS = 4
        EXPS = 0
        len_batch = (512, 512, 256)
        low_bank = 4 * (ph["g_out"].b % 2)
        up_bank = 4 * ((ph["g_out"].b + 1) % 2)
        m_min, u_abs = qkf[:, 0:2048], qkf[:, 2048:4096]
        gate_u = sem("gate_u")
        clamped = sem("clamped")
        gates_made = sem("gates_made")
        low_t = qkf[0:GLA_RANK, 0:SEQ]
        gains_turned, gains_out = sem("gains_turned"), sem("gains_out")
        low_split_hi, sem_grstd, sem_orstd = sem("low_split_hi"), sem("gla_rstd_ready"), sem("o_rstd_ready")

        class Steps:

            def __init__(self, eng, sm):
                self.eng, self.sm, self.n = eng, sm, 0

            def __call__(self, ins):
                self.n += 1
                ins.then_inc(self.sm, 1)
                self.eng.wait_ge(self.sm, self.n)

        def slot_fill(p, blk, qi):
            if p.quads == 1:
                return (p.q + blk + 2) // 2 + 1
            assert p.q % 2 == 0
            return p.q // 2 + blk + 2

        def tok_block(dst, blk):
            return dst[:, :, bass.ds(blk * NBLK, NBLK)]

        def tok_cols(dst, blk, c):
            return dst[:, 2 * c:2 * c + 2, NBLK * blk:NBLK * (blk + 1)]

        def fm_tiles(dst, blk, c):
            return dst.rearrange("p (a b) -> p a b", a=8)[:, 4 * blk + 2 * c:4 * blk + 2 * c + 2]

        def fm_block(dst, blk):
            return dst.rearrange("p (a b) -> p a b", a=8)[:, 4 * blk:4 * blk + 4]

        def clear_y(eng):
            nc.vector.memset(yf, 0.0).then_inc(y_clear, 1)

        def gemm_low_up(pe, mm):
            pe.wait_ge(low_out, 1)
            pe.wait_ge(up_in, 16)
            for h in range(GLA_HEADS):
                last = mm(ps[:, up_bank + h], w_up16[:, GLA_DK * h:GLA_DK * (h + 1)], low_t, start=True, stop=True)
            last.then_inc(up_mm, 1)
            pe.wait_ge(gate_u, 1)

        def turn_bank(name, k):
            return (4 * turn_banks[name] + k) % 8

        def tile_bank(name, i, half):
            return (4 * (after_block[name] % 2) + 2 * i + half) % 8

        def tile_lo(name, quad):
            return turn_base[name] + 7 + quad

        def stat_count(name, n, i):
            _, _, add, _, turn_, _ = junctions[name]
            if add is None:
                return 4 * n + i + 1
            first = 4 * add
            if turn_ is None:
                return first + i + 1
            if n == add:
                return first + (1 if i == 0 else 2 * i)
            return first + (2 * i + 3 if i < TT - 1 else 2 * TT)

        def quad_at(p, blk, qi):
            return p.q + blk * p.quads + qi

        def slot_of(p, u, qi):
            return (p.q + u * p.quads + qi) % 2

        def pairs(eng, p, blocks=None, peel=0):
            blocks = p.blocks if blocks is None else blocks
            assert blocks % 2 == 0
            for n in range(0, min(peel, blocks), 2):
                yield n
            left = blocks - peel
            if left == 2:
                yield peel
            elif left > 2:
                with eng.Fori(peel // 2, blocks // 2) as i:
                    yield i * 2

        block = ctx.enter_context(nc.Block())

        @block.sync
        def _(sp):
            def load(p, blk, u, src):
                for qi in range(p.quads):
                    n = quad_at(p, blk, qi)
                    s = slot_of(p, u, qi)
                    if not (isinstance(n, int) and n < 2):
                        sp.wait_ge(lo_ready, n - 1)
                    sp.dma_start(w_raw[:, s], src(blk, qi).rearrange("(a p) n -> p a n", p=P)).then_inc(raw_full[s], 16)

            def stream(name, src):
                p = ph[name]
                if p.blocks % 2:
                    return load(p, 0, 0, src)
                for blk in pairs(sp, p):
                    for u in range(2):
                        load(p, blk + u, u, src)

            def cols(wt, c0=0):
                return lambda blk, qi: wt[QUAD * P * qi:QUAD * P * (qi + 1), bass.ds(c0 + blk * NBLK, NBLK)]

            def mlp(name, up, down):
                p = ph[name]
                with sp.Fori(0, ROUNDS) as r:
                    for u in range(2):
                        load(p, r * 4 + u, u, lambda blk, qi: up[QUAD * P * qi:QUAD * P * (qi + 1),
                                                                 bass.ds(r * D + u * NBLK, NBLK)])
                    for u in range(2):
                        load(p, r * 4 + 2 + u, u, lambda blk, qi: down[bass.ds(r * D + qi * QUAD * P, QUAD * P),
                                                                       u * NBLK:(u + 1) * NBLK])

            w_in = w["w_in"][0]
            for i in range(TT):
                sp.dma_start(x_tm[:, i], w["x"][0, P * i:P * (i + 1), :]).then_inc(x_in[i], 16)
            stream("sb_qk", cols(w_in, C_SBQ))
            stream("sb_v", cols(w_in, C_SBV))
            stream("g_qk", cols(w_in, C_GQ))
            stream("g_v", cols(w_in, C_GV))
            stream("g_out", cols(w_in, C_GOUT))
            stream("gate_sb", cols(w_in, C_GATE_SB))
            stream("gate_gla", cols(w_in, C_GATE_GLA))
            stream("proj_sb", cols(w["w_proj_sb"][0]))
            stream("proj_gla", cols(w["w_proj_gla"][0]))
            stream("w_out", cols(w["w_out"][0]))
            mlp("mlp0", w["w_ff1"][0], w["w_ff2"][0])
            stream("qk", cols(w["attn_w_qkv_2"][0]))
            stream("v", cols(w["attn_w_qkv_2"][0], 2 * D))
            stream("w_o", cols(w["attn_w_o_2"][0]))
            mlp("mlp1", w["mlp_w_up_2"][0], w["mlp_w_down_2"][0])
            stream("conv_in", cols(w["conv_w_in_2"][0]))
            stream("conv_out", cols(w["conv_w_out_2"][0]))
            mlp("mlp2", w["mlp_w_up_2"][1], w["mlp_w_down_2"][1])
            for i in range(TT):
                sp.wait_ge(resid_ready, 4 * 4 + i + 1)
                sp.dma_start(out[0, P * i:P * (i + 1), :], x_tm[:, i]).then_inc(out_sent, 16)
            sp.wait_ge(out_sent, 16 * TT)

        @block.gpsimd
        def _(pool):
            dma = pool.dma_start
            pstep = Steps(pool, pool_step)

            def gain_row(dst, name, row=None):
                src = w[name] if row is None else w[name][row]
                dma(dst, src.rearrange("(a n) -> a n", a=1).partition_broadcast(P)).then_inc(grow_in, 16)

            def refine(name, n, i):
                pool.wait_ge(sumsq_ready, stat_count(name, n, i))
                v, y, t, r, ss = (z[n % 2][:, i:i + 1] for z in (var, guess0, newton, rstd, sumsq))
                pstep(nc.gpsimd.tensor_scalar(v, ss, 1.0 / D, EPS, ALU.mult, ALU.add))
                pool.wait_ge(guess_ready, stat_count(name, n, i))
                pstep(nc.gpsimd.tensor_tensor(t, y, y, ALU.mult))
                pstep(nc.gpsimd.tensor_tensor(t, t, v, ALU.mult))
                pstep(nc.gpsimd.tensor_scalar(t, t, -0.5, 1.5, ALU.mult, ALU.add))
                nc.gpsimd.tensor_tensor(r, t, y, ALU.mult).then_inc(rstd_ready, 1)

            def refine_tiles(name):
                _, _, add, _, turn_, _ = junctions[name]
                for s_ in range(TT + 1):
                    if add is not None and s_ < TT:
                        refine(name, add, s_)
                    if turn_ is not None and s_ > 0:
                        refine(name, turn_, s_ - 1)

            nc.gpsimd.memset(eps_col, EPS).then_inc(eps_set, 1)
            gain_row(g_turn, "norm_mix", 0)
            dma(consts[:], w["shape_consts"][:, 0:K_STRICT + P]).then_inc(consts_in, 16)
            dma(tmp[:, 0:P], w["shape_consts"][:, K_CAUSAL:K_CAUSAL + P]).then_inc(consts_in, 16)
            dma(masks_f, w["shape_consts"][:, K_MASKS:K_ALL]).then_inc(consts_in, 16)
            rows = [(w["gla_norm"][0].rearrange("(k p) -> k p", p=P), 2), (w["attn_subln_g_2"], 1),
                    (w["b_gate_up"][0].rearrange("(k p) -> k p", p=P), GLA_HEADS),
                    (w["conv_w_2"][0].rearrange("c (k p) -> (c k) p", p=P), 3 * KT)]
            r = 0
            for src, n in rows:
                dma(gain_rows[r:r + n], src).then_inc(gains_in, 16)
                r += n
            assert r == N_GAINS

            refine_tiles("h")
            def sb_after(t, u):
                pool.wait_ge(sp_made, t + 1)
                sp = sb_sp[u]
                nc.gpsimd.tensor_tensor(sp[:, AFTER[0] + P:AFTER[0] + 2 * P], sp[:, COL[1] + P:COL[1] + 2 * P],
                                        sp[:, COL[2]:COL[2] + P], ALU.add)
                for j in range(3):
                    last = nc.gpsimd.tensor_copy(sp[:, AFTER[j]:AFTER[j] + P], sp[:, COL[j + 1]:COL[j + 1] + P])
                last.then_inc(sp_after, 1)

            with pool.Fori(0, SB_HEADS // 2) as i:
                for u in range(2):
                    sb_after(i * 2 + u, u)

            pool.wait_ge(osb_lo, 1)
            dma(tmp[:, 0:KT * P].rearrange("p (a b) -> p a b", a=KT),
                w["w_in"][0][:, C_LOW:C_LOW + P].rearrange("(a p) n -> p a n", p=P)).then_inc(low_in, 16)
            dma(w_up16, w["w_gate_up"][0]).then_inc(up_in, 16)

            pool.wait_ge(go_mm, 4)
            dma(x_tm[:], w["x"][0].rearrange("(i p) n -> p i n", p=P)).then_inc(x_again, 16)
            pool.wait_ge(chunk_lo, 4)
            gain_row(g_turn, "norm_mlp", 0)
            refine_tiles("h_mlp0")
            pool.wait_ge(normed, 8)
            gain_row(g_add, "norm_final")
            gain_row(g_turn, "norm_mixer_pre_2", 0)
            refine_tiles("h_mix1")
            pool.wait_ge(resid_ready, 4)
            dma(tmp[:, 0:2 * SEQ], w["shape_consts"][:, K_COS:K_MASKS]).then_inc(tables_in, 16)
            for n, name in enumerate(("q1", "k1", "q2", "k2")):
                dma(lam_in[:, n], w[f"attn_lambda_{name}_2"].partition_broadcast(P)).then_inc(tables_in, 16)
            half = ROT // 2
            for blk in range(4):
                pool.wait_ge(rope_src, blk + 1)
                r4 = rot[blk % 2].rearrange("p (a b) -> p a b", a=4)
                for base in (0, DIFF_DIM):
                    for a, b in ((0, half), (half, 0)):
                        dma(r4[base + a:base + a + half], qk[base + b:base + b + half, 4 * blk:4 * blk + 4]).then_inc(swapped[blk % 2], 16)
            pool.wait_ge(turned_lo, turn_base["o_diff"] + KT)
            gain_row(g_add, "norm_mixer_post_2", 0)
            gain_row(g_turn, "norm_mlp_pre_2", 0)
            refine_tiles("h_mlp1")
            pool.wait_ge(normed, 16)
            gain_row(g_add, "norm_mlp_post_2", 0)
            gain_row(g_turn, "norm_mixer_pre_2", 1)
            refine_tiles("h_conv")
            pool.wait_ge(chunk_lo, 4 + 2 * 16 + 8)
            gain_row(g_add, "norm_mixer_post_2", 1)
            gain_row(g_turn, "norm_mlp_pre_2", 1)
            refine_tiles("h_mlp2")
            pool.wait_ge(normed, 24)
            gain_row(g_add, "norm_mlp_post_2", 1)
            refine_tiles("out")

        @block.tensor
        def _(pe):
            mm = nc.tensor.matmul

            def gemm(name, operand, token_major, waits=None, ordered=False):
                p = ph[name]
                hi, lo = operand

                def one(blk, u):
                    blk_no = p.b + blk
                    bank0 = 4 * ((p.b + u) % 2)
                    if not (isinstance(blk_no, int) and blk_no < 2):
                        pe.wait_ge(banks_free, blk_no - 1)
                    for qi in range(p.quads):
                        n, s = quad_at(p, blk, qi), slot_of(p, u, qi)
                        pe.wait_ge(lo_ready, n + 1)
                        for sm, value in (waits(blk, qi) if waits else ()):
                            pe.wait_ge(sm, value)
                        if ordered and blk == 1 and qi == 1:
                            multiply_ordered(hi, lo, s, bank0).then_inc(quad_done, 1)
                        else:
                            multiply(hi, lo, s, qi, bank0, p.quads, token_major).then_inc(quad_done, 1)

                if p.blocks % 2:
                    return one(0, 0)
                for blk in pairs(pe, p):
                    for u in range(2):
                        one(blk + u, u)

            def multiply(hi, lo, s, qi, bank0, quads, token_major):
                for a in range(QUAD):
                    k = QUAD * qi + a
                    for j in range(4):
                        js = slice(P * j, P * (j + 1))
                        if token_major:
                            parts = ((hi[:, k, js], w_hi[:, s, a]), (hi[:, k, js], w_lo[:, s, a]), (lo[:, k, js], w_hi[:, s, a]))
                        else:
                            parts = ((w_hi[:, s, a, js], hi[:, k]), (w_hi[:, s, a, js], lo[:, k]), (w_lo[:, s, a, js], hi[:, k]))
                        for x, (left, right) in enumerate(parts):
                            last = mm(ps[:, bank0 + j], left, right, start=(k == 0 and x == 0),
                                      stop=(k == QUAD * quads - 1 and x == 2))
                return last

            def multiply_ordered(hi, lo, s, bank0):
                for j in range(TT):
                    js = slice(P * j, P * (j + 1))
                    for a in range(QUAD):
                        k = QUAD + a
                        for x, (left, right) in enumerate(((hi[:, k, js], w_hi[:, s, a]), (hi[:, k, js], w_lo[:, s, a]),
                                                           (lo[:, k, js], w_hi[:, s, a]))):
                            last = mm(ps[:, bank0 + j], left, right, start=False, stop=(a == QUAD - 1 and x == 2))
                    if j < TT - 1:
                        last.then_inc(tile_done, 1)
                return last

            def turn(name, src, wait):
                for k in range(turns[name]):
                    for i in range(TT):
                        for sm, value in wait(k, i):
                            pe.wait_ge(sm, value)
                        last = nc.tensor.transpose(ps[:, turn_bank(name, k), P * i:P * (i + 1)], src(i, k), ident)
                    last.then_inc(turned, 1)

            def turn_tiles(name):
                before = junctions[name][5]
                if after_block[name]:
                    pe.wait_ge(banks_free, after_block[name] - 1)
                for i in range(TT):
                    pe.wait_ge(normed, 4 * before + i + 1)
                    for half in range(2):
                        for a in range(4):
                            k = 4 * half + a
                            last = nc.tensor.transpose(ps[:, tile_bank(name, i, half), P * a:P * (a + 1)],
                                                       y_tm[:, i, P * k:P * (k + 1)], ident)
                        last.then_inc(turned, 1)

            def turned_waits(name):
                if name in junctions:
                    return lambda blk, qi: [(turned_lo, tile_lo(name, qi))]
                return lambda blk, qi: [(turned_lo, turn_base[name] + 4 * qi + 4)]

            A, H = (a_hi, a_lo), (h_hi, h_lo)

            def mlp(name, turned_name, chunks):
                p = ph[name]
                b0 = 4 * (p.b % 2)
                with pe.Fori(0, ROUNDS) as r:
                    for u in range(4):
                        blk = r * 4 + u
                        bank0 = 4 * ((p.b + u) % 2)
                        pe.wait_ge(banks_free, p.b + blk - 1)
                        for qi in range(2):
                            n, s = quad_at(p, blk, qi), slot_of(p, u, qi)
                            pe.wait_ge(lo_ready, n + 1)
                            if u < 2:
                                pe.wait_ge(turned_lo, tile_lo(turned_name, qi))
                            else:
                                pe.wait_ge(chunk_lo, chunks + r * 4 + 2 * qi + 2)
                            hi, lo = A if u < 2 else H
                            if u == 3 and qi == 1:
                                multiply_ordered(hi, lo, s, bank0).then_inc(quad_done, 1)
                            else:
                                multiply(hi, lo, s, qi, bank0, 2, u >= 2).then_inc(quad_done, 1)

            pe.wait_ge(consts_in, 48)
            turn_tiles("h")
            gemm("sb_qk", A, False, turned_waits("h"))
            gemm("sb_v", A, True)
            pe.wait_ge(banks_free, ph["sb_v"].b + 1)
            pe.wait_ge(gains_in, GAIN_LOADS * 16)
            nc.tensor.transpose(ps[:, 7, 0:N_GAINS], gain_rows[0:N_GAINS], ident[0:N_GAINS, 0:N_GAINS]).then_inc(gains_turned, 1)
            pe.wait_ge(gains_out, 1)
            if stop < 1:
                return

            pe.wait_ge(banks_free, ph["g_qk"].b)

            def sb_region(t):
                return psf[:, 1536 * (t % 2):1536 * (t % 2) + TRI]

            def sb_scores(t):
                z = sb_region(t)
                rows = slice(SB_DIM * (t % 2), SB_DIM * (t % 2) + SB_DIM)
                (qh, kh), (ql, kl) = ((z_[rows, t // 2], z_[rows, 4 + t // 2]) for z_ in (sbq_hi, sbq_lo))
                if t >= 2:
                    pe.wait_ge(w_exp, t - 1)
                for j in (0, 1, 3, 2):
                    out_ = z[:, COL[j]:COL[j] + SEQ - P * j]
                    js = slice(P * j, P * (j + 1))
                    for x, (k_, q_) in enumerate(((kh, qh), (kh, ql), (kl, qh))):
                        mm(out_, k_[:, js], q_[:, P * j:], start=(x == 0 and j != 3), stop=True, skip_group_check=True)
                    last = mm(out_[:, 0:P], ident_b[:], strict_b[:], start=False, stop=True, skip_group_check=True)
                last.then_inc(z_ready, 1)

            def sb_sums(t):
                z = sb_region(t)
                pe.wait_ge(sp_lo, t + 1)
                for part in (sb_hi[t % 2], sb_lo[t % 2]):
                    for c, n in ((0, 512), (512, 512), (1024, 256)):
                        mm(z[:, c:c + n], ntri[:], part[:, c:c + n], start=False, stop=True, skip_group_check=True)
                    for j in range(3):
                        n, c = SEQ - P * (j + 1), COL[j] + P
                        last = mm(z[:, c:c + n], nones[:], part[:, AFTER[j]:AFTER[j] + n], start=False, stop=True,
                                  skip_group_check=True)
                last.then_inc(c_ready, 1)

            def sb_values(t):
                pe.wait_ge(sbw_lo, t + 1)
                if t >= 2:
                    pe.wait_ge(osb_out, t - 1)
                vs = slice(P * (t // 2), P * (t // 2 + 1))
                w_h, w_l = sb_whi[t % 2], sb_wlo[t % 2]
                for j in range(TT):
                    ws = slice(COL[j], COL[j] + SEQ - P * j)
                    for x, (v_, w_) in enumerate(((sbv_hi, w_h), (sbv_hi, w_l), (sbv_lo, w_h))):
                        last = mm(ps[:, 6 + t % 2, P * j:], v_[:, j, vs], w_[:, ws], start=(j == 0 and x == 0), stop=True,
                                  skip_group_check=True)
                last.then_inc(sb_pv, 1)

            for t in range(SB_HEADS + 2):
                if t < SB_HEADS:
                    sb_scores(t)
                if 1 <= t <= SB_HEADS:
                    sb_sums(t - 1)
                if t >= 2:
                    sb_values(t - 2)
            if stop < 2:
                return
            pe.wait_ge(osb_out, SB_HEADS)
            gemm("g_qk", A, False)
            gemm("g_v", A, True)

            low_bank = 4 * (ph["g_out"].b % 2)
            pe.wait_ge(banks_free, ph["g_out"].b)
            pe.wait_ge(low_split, 1)
            low_hi = hhf[:, 2048:3072].rearrange("p (a b) -> p a b", a=KT)
            low_lo = hlf[:, 2048:3072].rearrange("p (a b) -> p a b", a=KT)
            for k in range(KT):
                for x, (left, right) in enumerate(((low_hi, a_hi), (low_hi, a_lo), (low_lo, a_hi))):
                    last = mm(ps[:, low_bank], left[:, k], right[:, k], start=(k == 0 and x == 0), stop=(k == KT - 1 and x == 2))
            last.then_inc(low_mm, 1)
            gemm_low_up(pe, mm)
            gemm("g_out", A, True)
            if stop < 3:
                return

            pe.wait_ge(banks_free, ph["gate_sb"].b)
            for n in range(LEVELS + 1):
                pe.wait_ge(g_fac, n) if n else pe.wait_ge(b_ready, 1)
                if n >= 2:
                    pe.wait_ge(g_sel, n - 1)
                left, right = (g_k, g_q) if n == 0 else (g_f[(n - 1) % 2], g_f[(n - 1) % 2])
                for m in range(16):
                    ms = slice(P * m, P * (m + 1))
                    last = mm(psf[:, 2048 * (n % 2) + P * m:2048 * (n % 2) + P * (m + 1)], left[:, ms], right[:, ms],
                              start=True, stop=True)
                last.then_inc(g_mm, 1)
            pe.wait_ge(kd_ready, 1)
            pe.wait_ge(g_sel, LEVELS + 1)
            for m in range(12):
                h, c = m // 3, m % 3
                col = SEQ * h + P * c
                last = nc.tensor.transpose(psf[:, P * m:P * (m + 1)], g_k[:, col:col + P], ident)
            last.then_inc(kd_turned, 1)
            pe.wait_ge(kd_out, 1)
            for m in range(12):
                h, c = m // 3, m % 3
                dst = psf[:, 1024 + GLA_DV * (4 * c + h):1024 + GLA_DV * (4 * c + h + 1)]
                last = mm(dst, g_kt[:, P * m:P * (m + 1)], x_tm[:, c, GLA_DV * h:GLA_DV * (h + 1)], start=True, stop=True)
            last.then_inc(st_mm, 1)
            pe.wait_ge(st_ready, 3)
            for c in range(TT):
                for h in range(GLA_HEADS):
                    dst = ps[:, 2 * c + h // 2, GLA_DV * (h % 2):GLA_DV * (h % 2 + 1)]
                    col = SEQ * h + P * c
                    last = mm(dst, g_at[:, col:col + P], x_tm[:, c, GLA_DV * h:GLA_DV * (h + 1)], start=True, stop=(c == 0))
                    if c:
                        last = mm(dst, g_q[:, col:col + P], g_state[c - 1][:, GLA_DV * h:GLA_DV * (h + 1)], start=False, stop=True)
                last.then_inc(go_mm, 1)
            pe.wait_ge(go_act, 2)
            pe.wait_ge(go_dve, 2)
            if stop < 4:
                return
            gemm("gate_sb", A, False)
            gemm("gate_gla", A, False)
            pe.wait_ge(banks_free, ph["proj_sb"].b)
            turn("o_gla", lambda i, k: y_tm[:, i, P * k:P * (k + 1)], lambda k, i: [] if k else [(gout_ready, i + 1)])
            pe.wait_ge(turned_lo, turn_base["o_gla"] + 4)
            pe.wait_ge(osb_lo, 1)
            gemm("proj_sb", H, False, lambda blk, qi: [(turned_lo, turn_base["o_gla"] + 4 * blk + 4)])
            gemm("proj_gla", A, False, turned_waits("o_gla"))
            gemm("w_out", H, True, lambda blk, qi: [(chunk_lo, 2 * qi + 2)], True)
            if stop < 5:
                return
            turn_tiles("h_mlp0")
            mlp("mlp0", "h_mlp0", 4)
            if stop < 6:
                return
            turn_tiles("h_mix1")
            gemm("qk", A, False, turned_waits("h_mix1"))
            gemm("v", A, True)

            pe.wait_ge(banks_free, ph["w_o"].b)
            pe.wait_ge(qk_lo, 4)

            def diff_scores(t, c):
                rows = slice(DIFF_DIM * c, DIFF_DIM * (c + 1))
                (qh, kh), (ql, kl) = (z_[rows, t] for z_ in diff_qk_hi), (qk_r[rows, 8 * z_ + t] for z_ in range(2))
                if t:
                    pe.wait_ge(s_exp[c], t)
                s = psf[:, 1536 * c:1536 * c + TRI]
                for i in (3, 2, 0, 1):
                    n = P * (i + 1)
                    for x, (q_, k_) in enumerate(((qh, kh), (qh, kl), (ql, kh))):
                        mm(s[:, ROW[i]:ROW[i] + n], q_[:, P * i:P * (i + 1)], k_[:, 0:n], start=(i != 0 and x == 0), stop=True,
                           skip_group_check=True)
                    last = mm(s[:, ROW[i] + n - P:ROW[i] + n], ident_b[:], causal_b[:], start=False, stop=True,
                              skip_group_check=True)
                last.then_inc(s_mm[c], 1)

            batches = (((3, 0), (3, 1), (3, 2), (3, 3)), ((2, 0), (2, 1), (2, 2), (0, 0)), ((1, 0), (1, 1)))

            def diff_turn(t, b):
                pe.wait_ge(p_mixed, t + 1)
                if 3 * t + b:
                    pe.wait_ge(pt_lo, 3 * t + b)
                for n, (i, j) in enumerate(batches[b]):
                    c = ROW[i] + P * j
                    last = nc.tensor.transpose(ps[:, 6, P * n:P * (n + 1)], d_p[t % 2][0][:, c:c + P], ident)
                last.then_inc(p_turned, 1)

            def diff_values(t):
                pe.wait_ge(pt_lo, 3 * t + 3)
                if t:
                    pe.wait_ge(o_out, t)
                else:
                    pe.wait_ge(v_lo, 1)
                for i in range(TT):
                    for j in range(i + 1):
                        c = ROW[i] + P * j
                        o = ps[:, 7, P * i:P * (i + 1)]
                        ph_, pl_ = d_hi[t % 2][:, c:c + P], d_lo(t % 2, c, P)
                        vs = slice(D * j + P * t, D * j + P * (t + 1))
                        for x, (left, right) in enumerate(((ph_, ahf[:, vs]), (ph_, alf[:, vs]), (pl_, ahf[:, vs]))):
                            last = mm(o, left, right, start=(j == 0 and x == 0), stop=(j == i and x == 2))
                last.then_inc(o_mm, 1)

            for t in range(DIFF_HEADS + 2):
                for c in range(2):
                    if 1 <= t <= DIFF_HEADS:
                        diff_turn(t - 1, c)
                    if t < DIFF_HEADS:
                        diff_scores(t, c)
                if 1 <= t <= DIFF_HEADS:
                    diff_turn(t - 1, 2)
                if t >= 2:
                    diff_values(t - 2)
            pe.wait_ge(o_out, DIFF_HEADS)
            turn("o_diff", lambda i, k: qk[:, k, P * i:P * (i + 1)], lambda k, i: [] if i else [(o_normed, k // 2 + 1)])
            if stop < 7:
                return
            gemm("w_o", A, True, turned_waits("o_diff"), True)
            turn_tiles("h_mlp1")
            mlp("mlp1", "h_mlp1", 4 + 16)
            if stop < 8:
                return
            turn_tiles("h_conv")
            gemm("conv_in", A, False, turned_waits("h_conv"))
            gemm("conv_out", H, True, lambda blk, qi: [(chunk_lo, 4 + 32 + 4 * qi + 4)], True)
            if stop < 9:
                return
            turn_tiles("h_mlp2")
            mlp("mlp2", "h_mlp2", 4 + 32 + 8)

        @block.scalar
        def _(act):
            step = Steps(act, act_step)

            def split(p, blk, u, qi):
                n, s = quad_at(p, blk, qi) + 2, slot_of(p, u, qi)
                if isinstance(n, int) and n >= n_quads:
                    return
                act.wait_ge(raw_full[s], slot_fill(p, blk, qi) * 16)
                act.wait_ge(quad_done, n - 1)
                nc.scalar.activation(w_hi[:, s], w_raw[:, s], ACT.Copy).then_inc(hi_ready, 1)

            def first_split(s):
                act.wait_ge(raw_full[s], 16)
                nc.scalar.activation(w_hi[:, s], w_raw[:, s], ACT.Copy).then_inc(hi_ready, 1)

            def body(p, blk, u, evac=None):
                for qi in range(p.quads):
                    split(p, blk, u, qi)
                if evac:
                    act.wait_ge(quad_done, quad_at(p, blk, p.quads))
                    evac(blk, 4 * ((p.b + u) % 2))

            def phase(name, evac=None):
                p = ph[name]
                if p.blocks % 2:
                    return body(p, 0, 0, evac)
                for blk in pairs(act, p):
                    for u in range(2):
                        body(p, blk + u, u, evac)

            def gates(dst, moved, base):
                def evac(blk, bank0):
                    d = dst(blk)
                    act.wait_ge(moved, base + blk + 1)
                    step(nc.scalar.activation(d, d, ACT.Exp, scale=-1.0))
                    step(nc.scalar.activation(d, d, ACT.Ln, bias=1.0))
                    nc.scalar.activation(d, d, ACT.Exp, scale=-1.0).then_inc(gates_made, 1)
                return evac

            def round_chunk(n, src, dst):
                act.wait_ge(chunk_f32, n)
                nc.scalar.activation(dst, src, ACT.Copy).then_inc(chunk_hi, 1)

            def mlp(name, chunks):
                p = ph[name]

                def rounds(r, tail=False):
                    for u in range(4):
                        blk = r * 4 + u
                        for qi in range(1 if tail and u == 3 else 2):
                            split(p, blk, u, qi)
                        if u < 2:
                            bank0 = 4 * ((p.b + u) % 2)
                            act.wait_ge(quad_done, quad_at(p, blk, 2))
                            for c in range(2):
                                g = chunks + r * 4 + 2 * u + c
                                act.wait_ge(chunk_lo, g - 1)
                                nc.scalar.activation(tmp4[:, 2 * c:2 * c + 2], ps[:, bank0 + 2 * c:bank0 + 2 * c + 2],
                                                     ACT.Relu).then_inc(exp_ready, 1)
                            for c in range(2):
                                g = chunks + r * 4 + 2 * u + c
                                round_chunk(g + 1, tmp4[:, 2 * c:2 * c + 2], h_hi[:, 4 * u + 2 * c:4 * u + 2 * c + 2])

                with act.Fori(0, ROUNDS - 1) as r:
                    rounds(r)
                rounds(ROUNDS - 1, True)

            def square(name, n, i, src):
                ss, lv, y = (z[n % 2][:, i:i + 1] for z in (sumsq, log_var, guess0))
                count = stat_count(name, n, i)
                if count > 1:
                    act.wait_ge(sumsq_ready, count - 1)
                nc.scalar.activation(junk, src[:, i], ACT.Square, accum_out=ss).then_inc(sumsq_ready, 1)
                act.wait_ge(sumsq_ready, count)
                step(nc.scalar.activation(lv, ss, ACT.Ln, bias=eps_col, scale=1.0 / D))
                nc.scalar.activation(y, lv, ACT.Exp, scale=-0.5).then_inc(guess_ready, 1)

            def junction(name, last_split):
                tile0, kind, add, adds, turn_, _ = junctions[name]
                for s_ in range(TT + 3):
                    if s_ < TT:
                        if name == "h":
                            act.wait_ge(x_in[s_], 16)
                        elif s_ < 3:
                            act.wait_ge(tile_out, tile0 + s_ + 1)
                        else:
                            act.wait_ge(banks_free, after_block[name])
                        square(name, turn_ if add is None else add, s_, y_tm if kind == "P" else x_tm)
                    if turn_ is not None and add is not None and 1 <= s_ <= TT:
                        act.wait_ge(resid_ready, 4 * adds + s_)
                        square(name, turn_, s_ - 1, x_tm)
                    if turn_ is not None and s_ >= 3:
                        for half in range(2):
                            i = s_ - 3
                            act.wait_ge(turned, turn_base[name] + 2 * i + half + 1)
                            nc.scalar.activation(a_hi[:, 4 * half:4 * half + 4, P * i:P * (i + 1)],
                                                 ps[:, tile_bank(name, i, half)].rearrange("p (a b) -> p a b", a=4),
                                                 ACT.Copy).then_inc(turned_hi, 1)
                last_split()

            def guess(n, v, dst0, dst, made, sm):
                act.wait_ge(*made)
                step(nc.scalar.activation(dst0, v, ACT.Ln))
                nc.scalar.activation(dst, dst0, ACT.Exp, scale=-0.5).then_inc(sm, 1)

            def held_split(name, u=3):
                p = ph[name]
                return lambda: split(p, p.blocks - 1, 1, 1)

            def phase_to_junction(name):
                p = ph[name]
                body(p, 0, 0)
                split(p, 1, 1, 0)

            def turned_out(name, gain, dst):
                for k in range(turns[name]):
                    act.wait_ge(turned, turn_base[name] + k + 1)
                    src = ps[:, turn_bank(name, k)]
                    g = gain(k)
                    if g is None:
                        last = nc.scalar.activation(dst[:, k], src, ACT.Copy)
                    else:
                        last = nc.scalar.activation(dst[:, k], src, ACT.Copy, scale=g)
                    last.then_inc(turned_hi, 1)

            nc.scalar.preload_act_table_set("natural_log_exp_and_others")
            act.wait_ge(eps_set, 1)
            first_split(0)
            junction("h", lambda: first_split(1))
            def sbq_round(blk, bank0):
                nc.scalar.activation(sbq_hi[:, bass.ds(4 * blk, 4)], ps[:, bank0:bank0 + 4], ACT.Copy,
                                     scale=1.0 if blk else SB_DIM ** -0.5).then_inc(qkv_hi, 1)

            phase("sb_qk", sbq_round)
            phase("sb_v", lambda blk, bank0: nc.scalar.activation(sbv_hi, ps[:, bank0:bank0 + 4], ACT.Copy).then_inc(qkv_hi, 1))
            if stop < 1:
                return

            def sb_soft(t, u):
                z = psf[:, 1536 * u:1536 * u + TRI]
                act.wait_ge(z_ready, t + 1)
                if not (isinstance(t, int) and t < 2):
                    act.wait_ge(sp_made, t - 1)
                nc.scalar.activation(sb_t[u], z, ACT.Abs).then_inc(sb_abs, 1)
                act.wait_ge(sb_abs, t + 1)
                nc.scalar.activation(sb_t[u], sb_t[u], ACT.Exp, scale=-1.0).then_inc(sb_exp, 1)
                act.wait_ge(sb_exp, t + 1)
                nc.scalar.activation(sb_t[u], sb_t[u], ACT.Ln, bias=1.0).then_inc(soft_log, 1)

            def sb_weights(t, u):
                act.wait_ge(c_ready, t + 1)
                if not (isinstance(t, int) and t < 2):
                    act.wait_ge(sb_pv, t - 1)
                z = psf[:, 1536 * u:1536 * u + TRI]
                nc.scalar.activation(sb_w[u], z, ACT.Exp)
                nc.scalar.activation(sb_whi[u], z, ACT.Exp).then_inc(w_exp, 1)

            def sb_round(t, u):
                act.wait_ge(sp_summed, t + 1)
                act.wait_ge(sp_after, t + 1)
                if not (isinstance(t, int) and t < 2):
                    act.wait_ge(c_ready, t - 1)
                nc.scalar.activation(sb_hi[u], sb_sp[u], ACT.Copy).then_inc(sp_hi, 1)

            sb_soft(0, 0)
            sb_round(0, 0)
            sb_soft(1, 1)
            sb_weights(0, 0)
            sb_round(1, 1)
            with act.Fori(1, SB_HEADS // 2) as i:
                for u in range(2):
                    t = i * 2 + u
                    sb_soft(t, u)
                    sb_weights(t - 1, 1 - u)
                    sb_round(t, u)
            sb_weights(SB_HEADS - 1, 1)
            if stop < 2:
                return
            act.wait_ge(osb_out, SB_HEADS)
            nc.scalar.activation(h_hi[:, 0:4], o_sb, ACT.Copy).then_inc(osb_hi, 1)
            phase("g_qk")
            act.wait_ge(low_in, 16)
            nc.scalar.activation(hhf[:, 2048:3072], tmp[:, 0:1024], ACT.Copy).then_inc(low_split_hi, 1)
            phase("g_v")
            act.wait_ge(up_mm, 1)
            for h in range(GLA_HEADS):
                last = nc.scalar.activation(tmp4[:, h], ps[:, up_bank + h], ACT.Identity, bias=b_gate[:, h:h + 1])
            last.then_inc(gate_u, 1)
            act.wait_ge(gate_u, 1)
            step(nc.scalar.activation(u_abs, tmp, ACT.Abs))
            step(nc.scalar.activation(u_abs, u_abs, ACT.Exp, scale=-1.0))
            nc.scalar.activation(u_abs, u_abs, ACT.Ln, bias=1.0).then_inc(gate_log, 1)
            phase("g_out", gates(lambda blk: tok_block(y_tm, blk), clamped, 0))
            if stop < 3:
                return
            for n in range(LEVELS + 2):
                act.wait_ge(g_diff, n + 1)
                nc.scalar.activation(g_f[n % 2], g_f[n % 2], ACT.Exp).then_inc(g_exp, 1)
            nc.scalar.activation(elast, b_cum.rearrange("p (m n) -> p m n", n=P)[:, :, P - 1], ACT.Exp).then_inc(g_exp, 1)
            for c in range(2):
                act.wait_ge(go_mm, c + 1)
                nc.scalar.activation(g_o[:, 1024 * c:1024 * (c + 1)], psf[:, 1024 * c:1024 * (c + 1)], ACT.Copy).then_inc(go_act, 1)
            act.wait_ge(go_dve, 2)
            act.wait_ge(go_act, 2)
            for m in range(16):
                step(nc.scalar.activation(tmp[:, 1024:1024 + GLA_DV], g_o[:, GLA_DV * m:GLA_DV * (m + 1)], ACT.Square,
                                          accum_out=gss[:, m:m + 1]))
            nc.scalar.activation(small[:, 251:252], gss[:, 0:1], ACT.Copy).then_inc(gss_ready, 1)
            guess(0, gvar, grs0, grs1, (gvar_ready, 1), ggs_ready)
            if stop < 4:
                return
            phase("gate_sb", gates(lambda blk: fm_block(gates_sb, blk), banks_free, ph["gate_sb"].b))
            phase("gate_gla", gates(lambda blk: fm_block(gates_gla, blk), banks_free, ph["gate_gla"].b))
            turned_out("o_gla", lambda k: gains[:, G_GLA + k % 2:G_GLA + k % 2 + 1], a_hi)
            phase("proj_sb")

            def mix_hi(blk, bank0):
                for c in range(2):
                    round_chunk(2 * blk + c + 1, tmp4[:, 2 * c:2 * c + 2], h_hi[:, bass.ds(4 * blk + 2 * c, 2)])
            phase("proj_gla", mix_hi)
            phase_to_junction("w_out")
            if stop < 5:
                return
            junction("h_mlp0", held_split("w_out"))
            mlp("mlp0", 4)
            junction("h_mix1", held_split("mlp0"))
            if stop < 6:
                return
            def qk_round(blk):
                act.wait_ge(rope_done, blk + 1)
                nc.scalar.activation(diff_qk_hi[blk // 2][:, 4 * (blk % 2):4 * (blk % 2) + 4], qk[:, 4 * blk:4 * blk + 4],
                                     ACT.Copy).then_inc(qk_hi, 1)

            for p in (ph["qk"], ph["v"]):
                for blk in range(p.blocks):
                    split(p, blk, blk % 2, 0)
                    n = blk + p.b - ph["qk"].b
                    if n >= 2:
                        qk_round(n - 2)
                    split(p, blk, blk % 2, 1)
            act.wait_ge(lam_sum, 1)
            nc.scalar.activation(lam[:, 2:4], lam[:, 0:2], ACT.Exp).then_inc(lam_exp, 1)

            def diff_exp(t, u, c):
                act.wait_ge(s_max[c], t + 1)
                if not (isinstance(t, int) and t < 2):
                    if c == 0:
                        act.wait_ge(p_turned, 3 * t - 3)
                    else:
                        act.wait_ge(p_mixed, t - 1)
                for i in range(TT):
                    n = P * (i + 1)
                    last = nc.scalar.activation(d_p[u][c][:, ROW[i]:ROW[i] + n], psf[:, 1536 * c + ROW[i]:1536 * c + ROW[i] + n],
                                                ACT.Exp, bias=nmax[:, u, c, i:i + 1], accum_out=dsum[:, u, c, i:i + 1])
                last.then_inc(s_exp[c], 1)

            def diff_round(t, u, b):
                n = len_batch[b]
                act.wait_ge(p_turned, 3 * t + b + 1)
                if b == 0 and isinstance(t, int) and t == 0:
                    act.wait_ge(v_lo, 1)
                if b == 0 and not (isinstance(t, int) and t < 2):
                    act.wait_ge(o_mm, t - 1)
                nc.scalar.activation(d_hi[u][:, 512 * b:512 * b + n], ps[:, 6, 0:n], ACT.Copy).then_inc(pt_hi, 1)

            def diff_out(t, u):
                act.wait_ge(o_mm, t + 1)
                for i in range(TT):
                    o = ps[:, 7, P * i:P * (i + 1)]
                    rec = drec[:, 0, bass.ds(4 * t + i, 1)]
                    nc.scalar.activation(qk[:, bass.ds(t, 1), P * i:P * (i + 1)].rearrange("p a b -> p (a b)"), o, ACT.Copy, scale=rec)
                    last = nc.scalar.activation(o, o, ACT.Square, scale=rec, accum_out=dss[:, bass.ds(4 * t + i, 1)])
                last.then_inc(o_out, 1)

            def diff_step(t, u):
                for c in range(2):
                    diff_round(t - 1, 1 - u, c)
                    diff_exp(t, u, c)
                diff_round(t - 1, 1 - u, 2)

            diff_exp(0, 0, 0)
            diff_exp(0, 0, 1)
            act.wait_ge(banks_free, ph["w_o"].b)
            nc.scalar.activation(ahf, yf, ACT.Copy).then_inc(v_hi, 1)
            diff_step(1, 1)
            with act.Fori(1, DIFF_HEADS // 2) as i:
                for u in range(2):
                    t = i * 2 + u
                    diff_step(t, u)
                    diff_out(t - 2, u)
            for b in range(3):
                diff_round(DIFF_HEADS - 1, 1, b)
            for u in range(2):
                diff_out(DIFF_HEADS - 2 + u, u)
            guess(0, dvar, drs0, drs1, (ovar_ready, 1), ogs_ready)
            turned_out("o_diff", lambda k: gains[:, N_GAINS:N_GAINS + 1], a_hi)
            if stop < 7:
                return
            phase_to_junction("w_o")
            junction("h_mlp1", held_split("w_o"))
            mlp("mlp1", 4 + 16)
            junction("h_conv", held_split("mlp1"))
            if stop < 8:
                return

            def conv_hi(blk, bank0):
                if blk >= 4:
                    for a in range(4):
                        k = 4 * (blk - 4) + a
                        round_chunk(4 + 32 + k + 1, qk[:, k], h_hi[:, k])
            p = ph["conv_in"]
            for blk in range(p.blocks):
                body(p, blk, blk % 2, conv_hi)
            phase_to_junction("conv_out")
            junction("h_mlp2", held_split("conv_out"))
            if stop < 9:
                return
            mlp("mlp2", 4 + 32 + 8)
            junction("out", lambda: None)

        @block.vector
        def _(dve):
            step = Steps(dve, dve_step)
            tt, ts, stt = nc.vector.tensor_tensor, nc.vector.tensor_scalar, nc.vector.scalar_tensor_tensor

            def split(p, blk, u, qi):
                n, s = quad_at(p, blk, qi) + 2, slot_of(p, u, qi)
                if isinstance(n, int) and n >= n_quads:
                    return
                dve.wait_ge(hi_ready, n + 1)
                tt(w_lo[:, s], w_raw[:, s], w_hi[:, s].bitcast(F32), ALU.subtract).then_inc(lo_ready, 1)

            def first_split(s):
                dve.wait_ge(hi_ready, s + 1)
                tt(w_lo[:, s], w_raw[:, s], w_hi[:, s].bitcast(F32), ALU.subtract).then_inc(lo_ready, 1)

            def body(p, blk, u, evac):
                for qi in range(p.quads):
                    split(p, blk, u, qi)
                dve.wait_ge(quad_done, quad_at(p, blk, p.quads))
                evac(blk, 4 * ((p.b + u) % 2))

            def phase(name, evac):
                p = ph[name]
                if p.blocks % 2:
                    return body(p, 0, 0, evac)
                for blk in pairs(dve, p):
                    for u in range(2):
                        body(p, blk + u, u, evac)

            def to_tiles(first, scale=None):
                def evac(blk, bank0):
                    dst = qk[:, bass.ds(first + 4 * blk, 4)]
                    src = ps[:, bank0:bank0 + 4]
                    if scale is None or blk:
                        nc.vector.tensor_copy(dst, src).then_inc(banks_free, 1)
                    else:
                        ts(dst, src, scale, None, ALU.mult).then_inc(banks_free, 1)
                return evac

            def to_tokens(dst):
                def evac(blk, bank0):
                    nc.vector.tensor_copy(tok_block(dst, blk), ps[:, bank0:bank0 + 4]).then_inc(banks_free, 1)
                return evac

            def add_tokens(dst):
                def evac(blk, bank0):
                    d = tok_block(dst, blk)
                    tt(d, ps[:, bank0:bank0 + 4], d, ALU.add).then_inc(banks_free, 1)
                return evac

            def lo_chunk(n, src, hi, dst):
                dve.wait_ge(chunk_hi, n)
                tt(dst, src, hi.bitcast(F32), ALU.subtract).then_inc(chunk_lo, 1)

            def mlp(name, chunks, exps, acc, first_tile):
                p = ph[name]

                def rounds(r, tail=False):
                    for u in range(4):
                        blk = r * 4 + u
                        bank0 = 4 * ((p.b + u) % 2)
                        split(p, blk, u, 0)
                        if u == 3:
                            if tail:
                                return
                            for i in range(TT):
                                if i < TT - 1:
                                    dve.wait_ge(tile_done, first_tile + r * 3 + i + 1)
                                else:
                                    dve.wait_ge(quad_done, quad_at(p, blk, 2))
                                d = acc[:, i, NBLK:]
                                tt(d, ps[:, bank0 + i], d, ALU.add).then_inc(tile_out if i < TT - 1 else banks_free, 1)
                            split(p, blk, u, 1)
                            continue
                        split(p, blk, u, 1)
                        if u >= 2:
                            dve.wait_ge(quad_done, quad_at(p, blk, 2))
                            d = acc[:, :, NBLK * (u - 2):NBLK * (u - 1)]
                            tt(d, ps[:, bank0:bank0 + 4], d, ALU.add).then_inc(banks_free, 1)
                            continue
                        for c in range(2):
                            dve.wait_ge(exp_ready, exps + r * 4 + 2 * u + c + 1)
                            f = tmp4[:, 2 * c:2 * c + 2]
                            last = stt(f.rearrange("p a b -> p (a b)"), psf[:, 512 * (bank0 + 2 * c):512 * (bank0 + 2 * c + 2)], 0.0,
                                       f.rearrange("p a b -> p (a b)"), ALU.max, ALU.mult)
                            last.then_inc(chunk_f32, 1)
                        for c in range(2):
                            g = chunks + r * 4 + 2 * u + c
                            ks = slice(4 * u + 2 * c, 4 * u + 2 * c + 2)
                            dve.wait_ge(chunk_hi, g + 1)
                            tt(h_lo[:, ks], tmp4[:, 2 * c:2 * c + 2], h_hi[:, ks].bitcast(F32), ALU.subtract).then_inc(chunk_lo, 1)
                            if c == 0:
                                dve.wait_ge(chunk_f32, g + 2)
                                nc.vector.memset(small[:, 252:253], 0.0).then_inc(banks_free, 1)

                with dve.Fori(0, ROUNDS - 1) as r:
                    rounds(r)
                rounds(ROUNDS - 1, True)

            def refine(n_cols, v, y0, y1, out_, count, denom, sums, ready, v_done, guessed, done):
                dve.wait_ge(*ready)
                ts(v, sums, 1.0 / denom, EPS, ALU.mult, ALU.add).then_inc(v_done, 1)
                dve.wait_ge(*guessed)
                step(tt(y0, y1, y1, ALU.mult))
                step(tt(y0, y0, v, ALU.mult))
                step(ts(y0, y0, -0.5, 1.5, ALU.mult, ALU.add))
                tt(out_, y0, y1, ALU.mult).then_inc(done, 1)

            def junction(name, move, rows, last_split):
                tile0, kind, add, adds, turn_, turns_before = junctions[name]
                done = [False]
                for s_ in range(TT + 3):
                    if move and s_ < TT:
                        if s_ < TT - 1:
                            dve.wait_ge(tile_done, tile0 + s_ + 1)
                        else:
                            dve.wait_ge(quad_done, last_quad[name])
                        move(s_).then_inc(tile_out if s_ < TT - 1 else banks_free, 1)
                    if s_ == 0:
                        dve.wait_ge(grow_in, 16 * rows)
                    if add is not None and 1 <= s_ <= TT:
                        i = s_ - 1
                        dve.wait_ge(rstd_ready, stat_count(name, add, i))
                        r = rstd[add % 2][:, i:i + 1]
                        if kind == "F":
                            stt(x_tm[:, i], x_tm[:, i], r, g_add, ALU.mult, ALU.mult).then_inc(resid_ready, 1)
                        else:
                            step(stt(y_tm[:, i], y_tm[:, i], r, g_add, ALU.mult, ALU.mult))
                            tt(x_tm[:, i], x_tm[:, i], y_tm[:, i], ALU.add).then_inc(resid_ready, 1)
                    if turn_ is not None and 2 <= s_ <= TT + 1:
                        i = s_ - 2
                        dve.wait_ge(rstd_ready, stat_count(name, turn_, i))
                        stt(y_tm[:, i], x_tm[:, i], rstd[turn_ % 2][:, i:i + 1], g_turn, ALU.mult, ALU.mult).then_inc(normed, 1)
                    if turn_ is not None and s_ >= 3:
                        i = s_ - 3
                        for half in range(2):
                            dve.wait_ge(turned_hi, turn_base[name] + 2 * i + half + 1)
                            cs = (slice(None), slice(4 * half, 4 * half + 4), slice(P * i, P * (i + 1)))
                            tt(a_lo[cs], ps[:, tile_bank(name, i, half)].rearrange("p (a b) -> p a b", a=4),
                               a_hi[cs].bitcast(F32), ALU.subtract).then_inc(turned_lo, 1)
                last_split()

            last_quad = {"h_mlp0": ph["mlp0"].q, "h_mix1": ph["qk"].q, "h_mlp1": ph["mlp1"].q,
                         "h_conv": ph["conv_in"].q, "h_mlp2": ph["mlp2"].q, "out": n_quads}

            def held_split(name):
                p = ph[name]
                return lambda: split(p, p.blocks - 1, 1, 1)

            def phase_to_junction(name, evac):
                p = ph[name]
                body(p, 0, 0, evac)
                split(p, 1, 1, 0)

            def move_tile(name, dst):
                bank0 = 4 * ((ph[name].b + 1) % 2)
                return lambda i: nc.vector.tensor_copy(dst[:, i, NBLK:], ps[:, bank0 + i])

            def add_tile(name, dst):
                bank0 = 4 * ((ph[name].b + 1) % 2)
                return lambda i: tt(dst[:, i, NBLK:], ps[:, bank0 + i], dst[:, i, NBLK:], ALU.add)

            def turned_out(name, gain, hi, lo):
                for k in range(turns[name]):
                    dve.wait_ge(turned_hi, turn_base[name] + k + 1)
                    src = ps[:, turn_bank(name, k)]
                    g = gain(k)
                    if g is None:
                        last = tt(lo[:, k], src, hi[:, k].bitcast(F32), ALU.subtract)
                    else:
                        last = stt(lo[:, k], src, g, hi[:, k].bitcast(F32), ALU.mult, ALU.subtract)
                    last.then_inc(turned_lo, 1)

            dve.wait_ge(consts_in, 48)
            nc.vector.tensor_copy(ntri[:], consts[:, K_NTRI:K_NTRI + P]).then_inc(consts_r, 1)
            nc.vector.tensor_copy(nones[:], consts[:, K_NONE:K_NONE + P]).then_inc(consts_r, 1)
            nc.vector.tensor_copy(ident_b[:], ident).then_inc(consts_r, 1)
            nc.vector.tensor_copy(causal_b[:], tmp[:, 0:P]).then_inc(consts_r, 1)
            ts(strict_b[:], strict, 1.0, 1e30, ALU.subtract, ALU.mult).then_inc(consts_r, 1)
            step(nc.vector.tensor_copy(masks[:].rearrange("p a b -> p (a b)"), masks_f))
            first_split(0)
            for i in range(TT):
                dve.wait_ge(x_in[i], 16)
            junction("h", None, 1, lambda: first_split(1))

            def sbq_lo_part(blk, bank0):
                dve.wait_ge(qkv_hi, blk + 1)
                stt(sbq_lo[:, 4 * blk:4 * blk + 4].rearrange("p a b -> p (a b)"), psf[:, 512 * bank0:512 * bank0 + 2048],
                    1.0 if blk else SB_DIM ** -0.5, sbq_hi[:, 4 * blk:4 * blk + 4].bitcast(F32).rearrange("p a b -> p (a b)"),
                    ALU.mult, ALU.subtract).then_inc(banks_free, 1)

            def sbv_lo_part(blk, bank0):
                dve.wait_ge(qkv_hi, 3)
                tt(sbv_lo, ps[:, bank0:bank0 + 4], sbv_hi.bitcast(F32), ALU.subtract).then_inc(banks_free, 1)

            phase("sb_qk", sbq_lo_part)
            phase("sb_v", sbv_lo_part)
            dve.wait_ge(gains_turned, 1)
            nc.vector.tensor_copy(gains[:, 0:N_GAINS], ps[:, 7, 0:N_GAINS]).then_inc(gains_out, 1)
            dve.wait_ge(gains_out, 1)
            step(ts(gains[:, N_GAINS:N_GAINS + 1], gains[:, G_SUBLN:G_SUBLN + 1], 1.0 - LAMBDA_INIT, None, ALU.mult))
            if stop < 1:
                return

            def sb_softplus(t, u):
                dve.wait_ge(soft_log, t + 1)
                if not (isinstance(t, int) and t < 2):
                    dve.wait_ge(c_ready, t - 1)
                stt(sb_sp[u][:, 0:TRI], psf[:, 1536 * u:1536 * u + TRI], 0.0, sb_t[u], ALU.max, ALU.add).then_inc(sp_made, 1)
                dve.wait_ge(sp_made, t + 1)
                tile = lambda c: sb_sp[u][:, c:c + P]
                tt(tile(AFTER[1] + P), tile(COL[2] + P), tile(COL[3]), ALU.add).then_inc(sp_pair, 1)
                dve.wait_ge(sp_pair, t + 1)
                tt(tile(AFTER[0] + 2 * P), tile(COL[1] + 2 * P), tile(AFTER[1] + P), ALU.add).then_inc(sp_summed, 1)

            def sb_softplus_lo(t, u):
                dve.wait_ge(sp_hi, t + 1)
                tt(sb_lo[u], sb_sp[u], sb_hi[u].bitcast(F32), ALU.subtract).then_inc(sp_lo, 1)

            def sb_weights_lo(t, u):
                dve.wait_ge(w_exp, t + 1)
                tt(sb_wlo[u], sb_w[u], sb_whi[u].bitcast(F32), ALU.subtract).then_inc(sbw_lo, 1)

            def sb_out(t, u, pair):
                dve.wait_ge(sb_pv, t + 1)
                rows = slice(SB_DIM * u, SB_DIM * (u + 1))
                nc.vector.tensor_copy(o_sb[rows, bass.ds(pair, 1)].rearrange("p a b -> p (a b)"),
                                      ps[rows, 6 + u]).then_inc(osb_out, 1)

            sb_softplus(0, 0)
            sb_softplus_lo(0, 0)
            sb_softplus(1, 1)
            sb_weights_lo(0, 0)
            sb_softplus_lo(1, 1)
            with dve.Fori(1, SB_HEADS // 2) as i:
                for u in range(2):
                    t = i * 2 + u
                    sb_softplus(t, u)
                    sb_weights_lo(t - 1, 1 - u)
                    sb_softplus_lo(t, u)
                    sb_out(t - 2, u, i - 1)
            sb_weights_lo(SB_HEADS - 1, 1)
            for u in range(2):
                sb_out(SB_HEADS - 2 + u, u, SB_HEADS // 2 - 1)
            dve.wait_ge(osb_hi, 1)
            tt(h_lo[:, 0:4], o_sb, h_hi[:, 0:4].bitcast(F32), ALU.subtract).then_inc(osb_lo, 1)
            if stop < 2:
                return
            phase("g_qk", to_tiles(8, GLA_DK ** -0.5))
            dve.wait_ge(low_split_hi, 1)
            tt(hlf[:, 2048:3072], tmp[:, 0:1024], hhf[:, 2048:3072].bitcast(F32), ALU.subtract).then_inc(low_split, 1)
            phase("g_v", to_tokens(x_tm))

            dve.wait_ge(low_mm, 1)
            nc.vector.tensor_copy(low_t, ps[0:GLA_RANK, low_bank]).then_inc(low_out, 1)
            dve.wait_ge(gate_u, 1)
            step(ts(m_min, tmp, 0.0, None, ALU.min))
            dve.wait_ge(gate_log, 1)
            step(tt(m_min, m_min, u_abs, ALU.subtract))
            step(ts(m_min, m_min, 1.0 / GLA_TAU, None, ALU.mult))
            keep = arena[:, 0:2048]
            step(nc.vector.memset(keep, 1.0))
            step(nc.vector.memset(keep.rearrange("p (m n) -> p m n", n=P)[:, :, 0:1], 0.0))
            nc.vector.tensor_tensor_scan(b_cum, keep, m_min, 0.0, ALU.mult, ALU.add).then_inc(b_ready, 1)

            def silu(blk, bank0):
                d, src = tok_block(y_tm, blk), ps[:, bank0:bank0 + 4]
                ts(d, src, GATE_MIN, None, ALU.max).then_inc(clamped, 1)
                dve.wait_ge(gates_made, blk + 1)
                tt(d, src, d, ALU.mult).then_inc(banks_free, 1)
            phase("g_out", silu)
            if stop < 3:
                return

            step(nc.vector.memset(g_at, 0.0))
            dve.wait_ge(b_ready, 1)
            b_chunk = b_cum.rearrange("p (m n) -> p m n", n=P)

            def level_diff(n):
                h = 1 << n
                if n >= 2:
                    dve.wait_ge(g_mm, n)
                b2 = b_cum.rearrange("p (m two n) -> p m two n", two=2, n=h)
                f2 = g_f[n % 2].rearrange("p (m two n) -> p m two n", two=2, n=h)
                mid = b2[:, :, 0, h - 1:h].to_broadcast([P, 2048 // (2 * h), h])
                tt(f2[:, :, 1], b2[:, :, 1], mid, ALU.subtract)
                tt(f2[:, :, 0], mid, b2[:, :, 0], ALU.subtract).then_inc(g_diff, 1)

            def level_factor(n):
                h = 1 << n
                dve.wait_ge(g_exp, n + 1)
                f2, q2, k2 = (z.rearrange("p (m two n) -> p m two n", two=2, n=h) for z in (g_f[n % 2], g_q, g_k))
                tt(f2[:, :, 1], f2[:, :, 1], q2[:, :, 1], ALU.mult)
                tt(f2[:, :, 0], f2[:, :, 0], k2[:, :, 0], ALU.mult).then_inc(g_fac, 1)

            def level_select(n):
                dve.wait_ge(g_mm, n + 1)
                if n:
                    dve.wait_ge(g_sel, n)
                nc.vector.copy_predicated(g_at.rearrange("p (m n) -> p m n", n=P),
                                          masks[:, n:n + 1].to_broadcast([P, 16, P]),
                                          psf[:, 2048 * (n % 2):2048 * (n % 2 + 1)].rearrange("p (m n) -> p m n", n=P)).then_inc(g_sel, 1)

            level_diff(0)
            level_diff(1)
            level_factor(0)
            for n in range(2, LEVELS):
                level_select(n - 2)
                level_factor(n - 1)
                level_diff(n)
            level_select(LEVELS - 2)
            level_factor(LEVELS - 1)
            dve.wait_ge(g_mm, LEVELS)
            step(nc.vector.tensor_copy(g_f[LEVELS % 2], b_cum))
            nc.vector.memset(small[:, 253:254], 0.0).then_inc(g_diff, 1)
            level_select(LEVELS - 1)
            dve.wait_ge(g_mm, LEVELS + 1)
            tt(g_f[(LEVELS + 1) % 2].rearrange("p (m n) -> p m n", n=P), b_chunk[:, :, P - 1:P].to_broadcast([P, 16, P]), b_chunk,
               ALU.subtract).then_inc(g_diff, 1)
            level_select(LEVELS)
            dve.wait_ge(g_exp, LEVELS + 2)
            tt(g_k, g_k, g_f[(LEVELS + 1) % 2], ALU.mult).then_inc(kd_ready, 1)
            step(tt(g_q, g_q, g_f[LEVELS % 2], ALU.mult))
            dve.wait_ge(kd_turned, 1)
            nc.vector.tensor_copy(g_kt, psf[:, 0:1536]).then_inc(kd_out, 1)
            dve.wait_ge(st_mm, 1)
            dve.wait_ge(g_exp, LEVELS + 3)
            step(nc.vector.tensor_copy(g_state[0], psf[:, 1024:2048]))
            nc.vector.memset(small[:, 254:255], 0.0).then_inc(st_ready, 1)
            for c in range(1, 3):
                for h in range(GLA_HEADS):
                    hs = slice(GLA_DV * h, GLA_DV * (h + 1))
                    last = stt(g_state[c][:, hs], g_state[c - 1][:, hs], elast[:, 4 * h + c:4 * h + c + 1],
                               psf[:, 1024 * (c + 1) + GLA_DV * h:1024 * (c + 1) + GLA_DV * (h + 1)], ALU.mult, ALU.add)
                step(last)
                nc.vector.memset(small[:, 254:255], 0.0).then_inc(st_ready, 1)
            for c in range(2, 4):
                dve.wait_ge(go_mm, c + 1)
                nc.vector.tensor_copy(g_o[:, 1024 * c:1024 * (c + 1)], psf[:, 1024 * c:1024 * (c + 1)]).then_inc(go_dve, 1)
            refine(16, gvar, grs0, grs1, grstd, 0, GLA_DV, gss, (gss_ready, 1), gvar_ready, (ggs_ready, 1), sem_grstd)
            dve.wait_ge(sem_grstd, 1)
            for m in range(16):
                i, h = m // 4, m % 4
                ys = y_tm[:, i, GLA_DV * h:GLA_DV * (h + 1)]
                last = stt(ys, g_o[:, GLA_DV * m:GLA_DV * (m + 1)], grstd[:, m:m + 1], ys, ALU.mult, ALU.mult)
                if h == 3:
                    last.then_inc(gout_ready, 1)
            if stop < 4:
                return

            def move_gates(tiles):
                def evac(blk, bank0):
                    ts(fm_block(tiles, blk), ps[:, bank0:bank0 + 4], GATE_MIN, None, ALU.max).then_inc(banks_free, 1)
                return evac
            dve.wait_ge(gout_ready, 4)
            phase("gate_sb", move_gates(gates_sb))
            phase("gate_gla", move_gates(gates_gla))
            turned_out("o_gla", lambda k: gains[:, G_GLA + k % 2:G_GLA + k % 2 + 1], a_hi, a_lo)

            def mix_sb(blk, bank0):
                dve.wait_ge(gates_made, 2 + blk + 1)
                d = gates_sb.rearrange("p (a b) -> p a b", a=8)[:, 4 * blk:4 * blk + 4]
                tt(d, ps[:, bank0:bank0 + 4], d, ALU.mult).then_inc(banks_free, 1)

            def mix_gla(blk, bank0):
                dve.wait_ge(gates_made, 4 + blk + 1)
                for c in range(2):
                    f = tmp4[:, 2 * c:2 * c + 2]
                    last = tt(f, ps[:, bank0 + 2 * c:bank0 + 2 * c + 2], fm_tiles(gates_gla, blk, c), ALU.mult)
                    if c:
                        last.then_inc(banks_free, 1)
                step(nc.vector.memset(small[:, 255:256], 0.0))
                for c in range(2):
                    f = tmp4[:, 2 * c:2 * c + 2]
                    tt(f, f, fm_tiles(gates_sb, blk, c), ALU.add).then_inc(chunk_f32, 1)
                for c in range(2):
                    ks = slice(4 * blk + 2 * c, 4 * blk + 2 * c + 2)
                    lo_chunk(2 * blk + c + 1, tmp4[:, 2 * c:2 * c + 2], h_hi[:, ks], h_lo[:, ks])
                dve.wait_ge(chunk_lo, 2 * blk + 2)
            phase("proj_sb", mix_sb)
            dve.wait_ge(banks_free, ph["proj_gla"].b)
            phase("proj_gla", mix_gla)
            dve.wait_ge(x_again, 16)
            phase_to_junction("w_out", add_tokens(x_tm))
            if stop < 5:
                return
            junction("h_mlp0", add_tile("w_out", x_tm), 2, held_split("w_out"))
            mlp("mlp0", 4, EXPS, x_tm, 3)
            junction("h_mix1", add_tile("mlp0", x_tm), 4, held_split("mlp0"))
            if stop < 6:
                return

            for u in range(2):
                step(nc.vector.memset(rot[u], 0.0))
            dve.wait_ge(tables_in, 80)
            prod = stat[:, 0:4].rearrange("p a b -> p (a b)")
            step(tt(prod.rearrange("p (a b) -> p a b", a=2), lam_in[:, 0:4:2], lam_in[:, 1:4:2], ALU.mult))
            nc.vector.tensor_reduce(lam[:, 0:2], prod.rearrange("p (a b) -> p a b", a=2), AX.X, ALU.add).then_inc(lam_sum, 1)

            def rope(blk):
                sw = rot[blk % 2].rearrange("p (a b) -> p a b", a=4)
                tiles = qk[:, 4 * blk:4 * blk + 4]
                dve.wait_ge(swapped[blk % 2], 64 * (blk // 2 + 1))
                step(tt(sw, sw, sin_t.rearrange("p (a b) -> p a b", a=1).to_broadcast([P, 4, SEQ]), ALU.mult))
                step(tt(tiles, tiles, cos_t.rearrange("p (a b) -> p a b", a=1).to_broadcast([P, 4, SEQ]), ALU.mult))
                tt(tiles, tiles, sw, ALU.add).then_inc(rope_done, 1)

            p = ph["qk"]
            def qk_lo_part(blk):
                dve.wait_ge(qk_hi, blk + 1)
                d = qk[:, 4 * blk:4 * blk + 4]
                tt(qk_r[:, 4 * blk:4 * blk + 4], d, diff_qk_hi[blk // 2][:, 4 * (blk % 2):4 * (blk % 2) + 4].bitcast(F32), ALU.subtract).then_inc(qk_lo, 1)

            for blk in range(4):
                split(p, blk, blk % 2, 0)
                if blk >= 2:
                    qk_lo_part(blk - 2)
                split(p, blk, blk % 2, 1)
                dve.wait_ge(quad_done, quad_at(p, blk, 2))
                bank0 = 4 * ((p.b + blk) % 2)
                dst, src = qk[:, 4 * blk:4 * blk + 4], ps[:, bank0:bank0 + 4]
                if blk < 2:
                    step(ts(dst, src, DIFF_DIM ** -0.5, None, ALU.mult))
                else:
                    step(nc.vector.tensor_copy(dst, src))
                if blk >= 2:
                    dve.wait_ge(rope_done, blk - 1)
                nc.vector.memset(small[:, 248:249], 0.0).then_inc(banks_free, 1)
                nc.vector.memset(small[:, 249:250], 0.0).then_inc(rope_src, 1)
                if blk:
                    rope(blk - 1)
            rope(3)
            p = ph["v"]
            for blk in range(2):
                split(p, blk, blk % 2, 0)
                qk_lo_part(2 + blk)
                split(p, blk, blk % 2, 1)
                dve.wait_ge(quad_done, quad_at(p, blk, 2))
                to_tokens(y_tm)(blk, 4 * ((p.b + blk) % 2))
            dve.wait_ge(lam_exp, 1)
            step(tt(lam[:, 4:5], lam[:, 3:4], lam[:, 2:3], ALU.subtract))
            step(ts(lam[:, 5:6], lam[:, 4:5], LAMBDA_INIT, None, ALU.subtract))

            def diff_max(t, u, c):
                dve.wait_ge(s_mm[c], t + 1)
                if not (isinstance(t, int) and t < 2):
                    dve.wait_ge(s_exp[c], t - 1)
                for i in range(TT):
                    n = P * (i + 1)
                    last = nc.vector.tensor_reduce(nmax[:, u, c, i:i + 1], psf[:, 1536 * c + ROW[i]:1536 * c + ROW[i] + n],
                                                   AX.X, ALU.max, negate=True)
                last.then_inc(s_max[c], 1)

            def diff_mix(t, u):
                dve.wait_ge(s_exp[0], t + 1)
                dve.wait_ge(s_exp[1], t + 1)
                rec = drec[:, :, bass.ds(4 * t, 4)]
                nc.vector.reciprocal(rec, dsum[:, u]).then_inc(rec_made, 1)
                dve.wait_ge(rec_made, t + 1)
                stt(nmax[:, u, 1], drec[:, 1, bass.ds(4 * t, 4)], lam[:, 5:6], dsum[:, u, 0], ALU.mult, ALU.mult).then_inc(ratio_made, 1)
                dve.wait_ge(ratio_made, t + 1)
                for i in range(TT):
                    n = P * (i + 1)
                    cs = slice(ROW[i], ROW[i] + n)
                    last = stt(d_p[u][0][:, cs], d_p[u][1][:, cs], nmax[:, u, 1, i:i + 1], d_p[u][0][:, cs], ALU.mult, ALU.add)
                last.then_inc(p_mixed, 1)

            def diff_lo(t, u, b):
                n = len_batch[b]
                dve.wait_ge(pt_hi, 3 * t + b + 1)
                if b == 0 and not (isinstance(t, int) and t < 2):
                    dve.wait_ge(o_mm, t - 1)
                tt(d_lo(u, 512 * b, n), ps[:, 6, 0:n], d_hi[u][:, 512 * b:512 * b + n].bitcast(F32), ALU.subtract).then_inc(pt_lo, 1)

            def diff_step(t, u):
                for c in range(2):
                    diff_lo(t - 1, 1 - u, c)
                    diff_max(t, u, c)
                diff_lo(t - 1, 1 - u, 2)
                diff_mix(t, u)

            diff_max(0, 0, 0)
            diff_max(0, 0, 1)
            diff_mix(0, 0)
            dve.wait_ge(v_hi, 1)
            tt(alf, yf, ahf.bitcast(F32), ALU.subtract).then_inc(v_lo, 1)
            diff_step(1, 1)
            with dve.Fori(1, DIFF_HEADS // 2) as i:
                for u in range(2):
                    diff_step(i * 2 + u, u)
            for b in range(3):
                diff_lo(DIFF_HEADS - 1, 1, b)
            refine(32, dvar, drs0, drs1, drstd, 0, DIFF_V, dss, (o_out, DIFF_HEADS), ovar_ready, (ogs_ready, 1), sem_orstd)
            dve.wait_ge(sem_orstd, 1)
            for g in range(4):
                o = qk[:, 2 * g:2 * g + 2].rearrange("p a (i e) -> p (a i) e", e=P)
                r = drstd[:, 8 * g:8 * g + 8].rearrange("p (n one) -> p n one", one=1).to_broadcast([P, 8, P])
                tt(o, o, r, ALU.mult).then_inc(o_normed, 1)
            turned_out("o_diff", lambda k: gains[:, N_GAINS:N_GAINS + 1], a_hi, a_lo)
            if stop < 7:
                return
            phase_to_junction("w_o", to_tokens(y_tm))
            junction("h_mlp1", move_tile("w_o", y_tm), 6, held_split("w_o"))
            clear_y(dve)
            mlp("mlp1", 4 + 16, EXPS + 16, y_tm, 3 * 6)
            junction("h_conv", add_tile("mlp1", y_tm), 8, held_split("mlp1"))
            if stop < 8:
                return

            def conv(k):
                u_, y_ = y_fm[:, k], qk[:, 8 + k]
                step(ts(y_, u_, convw[:, 2, k:k + 1], None, ALU.mult))
                step(stt(y_[:, 1:SEQ], u_[:, 0:SEQ - 1], convw[:, 1, k:k + 1], y_[:, 1:SEQ], ALU.mult, ALU.add))
                step(stt(y_[:, 2:SEQ], u_[:, 0:SEQ - 2], convw[:, 0, k:k + 1], y_[:, 2:SEQ], ALU.mult, ALU.add))
                tt(qk[:, k], qk[:, k], y_, ALU.mult).then_inc(chunk_f32, 1)
                lo_chunk(4 + 32 + k + 1, qk[:, k], h_hi[:, k], h_lo[:, k])

            p = ph["conv_in"]
            for blk in range(p.blocks):
                for qi in range(2):
                    split(p, blk, blk % 2, qi)
                dve.wait_ge(quad_done, quad_at(p, blk, 2))
                bank0 = 4 * ((p.b + blk) % 2)
                src = ps[:, bank0:bank0 + 4]
                if blk < 4:
                    nc.vector.tensor_copy(qk[:, 4 * blk:4 * blk + 4], src).then_inc(banks_free, 1)
                    continue
                g = 4 * (blk - 4)
                dve.wait_ge(banks_free, p.b + blk)
                tt(y_fm[:, g:g + 4], src, qk[:, 8 + g:12 + g], ALU.mult).then_inc(banks_free, 1)
                dve.wait_ge(banks_free, p.b + blk + 1)
                for a in range(4):
                    conv(g + a)
            phase_to_junction("conv_out", to_tokens(y_tm))
            junction("h_mlp2", move_tile("conv_out", y_tm), 10, held_split("conv_out"))
            if stop < 9:
                return
            clear_y(dve)
            mlp("mlp2", 4 + 32 + 8, EXPS + 32, y_tm, 3 * 11)
            junction("out", add_tile("mlp2", y_tm), 11, lambda: None)


_OUT = ((1, SEQ, D), "float32")
_INS = ["x", "norm_mix", "w_in", "w_gate_up", "b_gate_up", "gla_norm", "w_proj_sb", "w_proj_gla", "w_out", "norm_mlp",
        "w_ff1", "w_ff2", "norm_final", "attn_w_qkv_2", "attn_w_o_2", "attn_lambda_q1_2", "attn_lambda_k1_2",
        "attn_lambda_q2_2", "attn_lambda_k2_2", "attn_subln_g_2", "conv_w_in_2", "conv_w_2", "conv_w_out_2",
        "mlp_w_up_2", "mlp_w_down_2", "norm_mixer_pre_2", "norm_mixer_post_2", "norm_mlp_pre_2", "norm_mlp_post_2"]


def kernel(**inputs):
    import concourse.bacc as bacc
    from concourse.bass_utils import run_bass_kernel_spmd

    nc = bacc.Bacc("TRN2", target_bir_lowering=False, num_devices=1)
    arrays, args = {}, {}
    for name, a in [(n, np.ascontiguousarray(inputs[n])) for n in _INS] + [("shape_consts", shape_constants())]:
        arrays[f"in_{name}"] = a
        args[name] = nc.dram_tensor(f"in_{name}", a.shape, mybir.dt.from_np(a.dtype), kind="ExternalInput").ap()
    out = nc.dram_tensor("out", _OUT[0], mybir.dt.from_np(np.dtype(_OUT[1])), kind="ExternalOutput").ap()
    build(nc, args, out)
    result = run_bass_kernel_spmd(nc, [arrays], core_ids=[0])
    return result.results[0]["out"]
```

```python
from contextlib import ExitStack

import numpy as np

import concourse.bass as bass
from concourse import mybir

F32 = mybir.dt.float32
F32R = mybir.dt.float32r
BF16 = mybir.dt.bfloat16
U8 = mybir.dt.uint8
ALU = mybir.AluOpType
ACT = mybir.ActivationFunctionType
AX = mybir.AxisListType

P = 128
SEQ = 512
D = 1024
TT = SEQ // P
KT = D // P
NBLK = 512
QUAD = 4
EPS = 1e-6
GATE_MIN = -43.0

SB_HEADS, SB_DIM = 8, 64
GLA_HEADS, GLA_DK, GLA_DV, GLA_RANK, GLA_TAU = 4, 128, 256, 16, 16.0
DIFF_HEADS, DIFF_DIM, DIFF_V = 8, 64, 128
N_GAINS = 2 + 1 + GLA_HEADS + 3 * KT
ROT, THETA = 16, 500000.0
LAMBDA_INIT = 0.8 - 0.6
D_FF = 4096
ROUNDS = D_FF // D
LEVELS = 7

C_SBQ, C_SBK, C_SBV = 0, 512, 1024
C_GQ, C_GK, C_GV, C_GOUT, C_LOW = 1536, 2048, 2560, 3584, 4608
C_GATE_SB, C_GATE_GLA = 4624, 5648

K_ID, K_NTRI, K_NONE, K_STRICT, K_CAUSAL, K_COS, K_SIN, K_MASKS = 0, 128, 256, 384, 512, 640, 1152, 1664
K_ALL = K_MASKS + (LEVELS + 1) * P

TRI = 10 * P
COL = {0: 0, 1: 512, 3: 896, 2: 1024}
AFTER = {0: TRI, 1: TRI + 3 * P, 2: TRI + 5 * P}
TRI_AFTER = TRI + 6 * P
ROW = {3: 0, 2: 512, 0: 896, 1: 1024}


class Phase:

    def __init__(self, name, blocks, quads=2):
        self.name, self.blocks, self.quads = name, blocks, quads
        self.q = self.b = 0


def plan():
    names = [Phase("sb_qk", 2), Phase("sb_v", 1), Phase("g_qk", 2), Phase("g_v", 2), Phase("g_out", 2),
             Phase("gate_sb", 2), Phase("gate_gla", 2), Phase("proj_sb", 2, 1), Phase("proj_gla", 2),
             Phase("w_out", 2), Phase("mlp0", 4 * ROUNDS), Phase("qk", 4), Phase("v", 2), Phase("w_o", 2),
             Phase("mlp1", 4 * ROUNDS), Phase("conv_in", 6), Phase("conv_out", 2), Phase("mlp2", 4 * ROUNDS)]
    q = b = 0
    for ph in names:
        ph.q, ph.b = q, b
        q += ph.blocks * ph.quads
        b += ph.blocks
    return {ph.name: ph for ph in names}, q, b


def shape_constants():
    c = np.zeros((P, K_ALL), np.float32)
    r, s = np.arange(P)[:, None], np.arange(P)[None, :]
    c[:, K_ID:K_ID + P] = r == s
    c[:, K_NTRI:K_NTRI + P] = np.where(r >= s, -1.0, 0.0)
    c[:, K_NONE:K_NONE + P] = -1.0
    c[:, K_STRICT:K_STRICT + P] = s > r
    c[:, K_CAUSAL:K_CAUSAL + P] = np.where(s > r, -1e30, 0.0)
    half = ROT // 2
    inv = np.float32(THETA) ** (-np.arange(0, ROT, 2, dtype=np.float32) / np.float32(ROT))
    ang = np.arange(SEQ, dtype=np.float32)[None, :] * inv[:, None].astype(np.float32)
    cos, sin = np.ones((P, SEQ), np.float32), np.zeros((P, SEQ), np.float32)
    for base in (0, DIFF_DIM):
        for part, sign in ((0, -1.0), (half, 1.0)):
            cos[base + part:base + part + half] = np.cos(ang)
            sin[base + part:base + part + half] = sign * np.sin(ang)
    c[:, K_COS:K_COS + SEQ] = cos
    c[:, K_SIN:K_SIN + SEQ] = sin
    c[:, K_MASKS:K_MASKS + P] = r == s
    for n in range(LEVELS):
        h = 1 << n
        m = K_MASKS + P * (n + 1)
        c[:, m:m + P] = (r // (2 * h) == s // (2 * h)) & (r % (2 * h) < h) & (s % (2 * h) >= h)
    return c


def build(nc, w, out):
    ph, n_quads, n_blocks = plan()
    ctx = ExitStack()
    with ctx:
        def sb(name, shape, dt=F32):
            return ctx.enter_context(nc.sbuf_tensor(name, shape, dt))

        def twin(name, shape, dt):
            return nc.alloc_sbuf_tensor_at(name, shape, dt, offset=-(-nc.sbuf_base // 32) * 32)

        sems = {}

        def sem(name):
            sems[name] = ctx.enter_context(nc.semaphore(name))
            return sems[name]

        x_r = twin("x_r", [P, TT * D], F32R)
        x_tm = sb("x_tm", [P, TT, D])
        a_hi = sb("a_hi", [P, KT, SEQ], F32R)
        a_lo = sb("a_lo", [P, KT, SEQ], F32R)
        h_hi_f = twin("h_hi_f", [P, KT * SEQ], F32)
        h_hi = sb("h_hi", [P, KT, SEQ], F32R)
        h_lo_f = twin("h_lo_f", [P, KT * SEQ], F32)
        h_lo = sb("h_lo", [P, KT, SEQ], F32R)
        w_raw = sb("w_raw", [P, 2, QUAD, NBLK])
        w_hi = sb("w_hi", [P, 2, QUAD, NBLK], F32R)
        w_lo = sb("w_lo", [P, 2, QUAD, NBLK], F32R)
        y_r = twin("y_r", [P, TT * D], F32R)
        y_tm = sb("y_tm", [P, TT, D])
        qk_r = twin("qk_r", [P, 16, SEQ], F32R)
        qk = sb("qk", [P, 16, SEQ])
        arena_r = twin("arena_r", [P, 6144], F32R)
        arena = sb("arena", [P, 6144])
        consts = sb("consts", [P, K_STRICT + P])
        masks = sb("masks", [P, LEVELS + 1, P], U8)
        ntri = sb("ntri", [P, P], F32R)
        nones = sb("nones", [P, P], F32R)
        ident_b = sb("ident_b", [P, P], BF16)
        causal_b = sb("causal_b", [P, P], BF16)
        strict_b = sb("strict_b", [P, P], BF16)
        gains = sb("gains", [P, N_GAINS + 1])
        b_gate = gains[:, 3:7]
        convw = gains[:, 7:31].rearrange("p (a b) -> p a b", a=3)
        small = sb("small", [P, 256])
        stat = sb("stat", [P, 7, DIFF_HEADS * TT])
        ps = ctx.enter_context(nc.psum_tensor("ps", [P, 8, 512], F32))
        psf = ps[:].rearrange("p b n -> p (b n)")

        xf = x_tm[:].rearrange("p a b -> p (a b)")
        yf = y_tm[:].rearrange("p a b -> p (a b)")
        hhf = h_hi[:].rearrange("p a b -> p (a b)")
        hlf = h_lo[:].rearrange("p a b -> p (a b)")
        qkf = qk[:].rearrange("p a b -> p (a b)")
        y_fm = yf.rearrange("p (a b) -> p a b", a=KT)
        ident = consts[:, K_ID:K_ID + P]
        strict = consts[:, K_STRICT:K_STRICT + P]
        b_cum = arena[:, 2048:4096]
        tmp = arena[:, 4096:6144]
        w_up16 = arena[0:GLA_RANK, 0:GLA_HEADS * GLA_DK]
        lam_in = tmp[:, 2 * SEQ:2 * SEQ + 4 * DIFF_DIM].rearrange("p (a b) -> p a b", a=4)
        masks_f = arena[:, 0:(LEVELS + 1) * P]
        gain_rows = tmp[:, P:2 * P]
        tmp4 = tmp.rearrange("p (a b) -> p a b", a=4)

        junk = qkf[:, 0:1024]
        g_add, g_turn = qkf[:, 7168:8192], qkf[:, 6144:7168]
        sb_t = [yf[:, 1280 * u:1280 * (u + 1)] for u in range(2)]
        sb_sp = [h_lo_f[:, 2048 * u:2048 * (u + 1)] for u in range(2)]
        sb_lo = [hlf[:, 2048 * u:2048 * (u + 1)] for u in range(2)]
        sb_hi = [hhf[:, 2048 * u:2048 * (u + 1)] for u in range(2)]
        sb_w = [xf[:, 1280 * u:1280 * (u + 1)] for u in range(2)]
        sb_wlo = [x_r[:, 1280 * u:1280 * (u + 1)] for u in range(2)]
        sb_whi = [x_r[:, 2560:3840], y_r[:, 2560:3840]]
        sbq_hi, sbq_lo = qk_r[:, 0:8], qk_r[:, 8:16]
        sbv_hi = arena_r[:, 0:2048].rearrange("p (a b) -> p a b", a=TT)
        sbv_lo = arena_r[:, 2048:4096].rearrange("p (a b) -> p a b", a=TT)
        o_sb = tmp4
        g_q, g_k = qkf[:, 4096:6144], qkf[:, 6144:8192]
        g_f = [qkf[:, 0:2048], qkf[:, 2048:4096], h_hi_f[:, 2048:4096], h_lo_f[:, 2048:4096]]
        g_at = arena[:, 0:2048]
        g_kt = tmp[:, 0:1536]
        g_state = [arena[:, 2048:3072], arena[:, 3072:4096], tmp[:, 0:1024]]
        g_o = qkf[:, 0:4096]
        ahf = a_hi[:].rearrange("p a b -> p (a b)")
        alf = a_lo[:].rearrange("p a b -> p (a b)")
        d_p = [[arena[:, 2560 * u + 1280 * c:2560 * u + 1280 * (c + 1)] for c in range(2)] for u in range(2)]
        d_hi = [y_r[:, 0:1280], y_r[:, 1280:2560]]

        def d_lo(u, c, n):
            if u == 0:
                return y_r[:, 2560 + c:2560 + c + n]
            return arena_r[:, 5120 + c:5120 + c + n] if c < 1024 else y_r[:, 2816 + c:2816 + c + n]

        diff_qk_hi = (h_hi, h_lo)
        rot = [arena[:, 0:2048], arena[:, 2048:4096]]
        cos_t, sin_t = tmp[:, 0:SEQ], tmp[:, SEQ:2 * SEQ]
        gates_sb, gates_gla = qkf[:, 0:4096], qkf[:, 4096:8192]

        sumsq, var, log_var, guess0, newton, rstd = (
            [small[:, 170 + 8 * n + 4 * u:174 + 8 * n + 4 * u] for u in range(2)] for n in range(6))
        eps_col = small[:, 0:1]
        gss, gvar, grs0, grs1, grstd = (small[:, 20 + 16 * n:36 + 16 * n] for n in range(5))
        elast = small[:, 100:116]
        nmax = small[:, 116:132].rearrange("p (u c i) -> p u c i", u=2, c=2)
        dsum = small[:, 132:148].rearrange("p (u c i) -> p u c i", u=2, c=2)
        drec = stat[:, 5:7]
        lam = small[:, 164:170]
        dss, dvar, drs0, drs1, drstd = (stat[:, n] for n in range(5))

        raw_full = [sem("raw_full0"), sem("raw_full1")]
        x_in = [sem(f"x_in{i}") for i in range(TT)]
        consts_in = sem("consts_in")
        ident_in, mix_row_in = sem("ident_in"), sem("mix_row_in")
        gains_in = sem("gains_in")
        low_in = sem("low_in")
        x_again = sem("x_again")
        tables_in = sem("tables_in")
        swapped = [sem(f"swapped{i}") for i in range(2)]
        grow_in = sem("grow_in")
        up_in = sem("up_in")
        y_clear = sem("y_clear")
        consts_r = sem("consts_r")
        out_sent = sem("out_sent")
        quad_done = sem("quad_done")
        turned = sem("turned")
        hi_ready = sem("hi_ready")
        exp_ready = sem("exp_ready")
        chunk_hi = sem("chunk_hi")
        turned_hi = sem("turned_hi")
        sumsq_ready = sem("sumsq_ready")
        guess_ready = sem("guess_ready")
        act_step = sem("act_step")
        lo_ready = sem("lo_ready")
        banks_free = sem("banks_free")
        chunk_f32 = sem("chunk_f32")
        chunk_lo = sem("chunk_lo")
        turned_lo = sem("turned_lo")
        rstd_ready = sem("rstd_ready")
        normed = sem("normed")
        resid_ready = sem("resid_ready")
        tile_done = sem("tile_done")
        tile_out = sem("tile_out")
        eps_set = sem("eps_set")
        pool_step = sem("pool_step")
        dve_step = sem("dve_step")
        z_ready, sb_abs, sb_exp, soft_log = sem("z_ready"), sem("sb_abs"), sem("sb_exp"), sem("soft_log")
        sp_made, sp_summed, sp_hi, sp_lo = sem("sp_made"), sem("sp_summed"), sem("sp_hi"), sem("sp_lo")
        c_ready, w_exp, sbw_lo = sem("c_ready"), sem("w_exp"), sem("sbw_lo")
        sp_pair, sp_after = sem("sp_pair"), sem("sp_after")
        qkv_hi, osb_hi, osb_lo = sem("qkv_hi"), sem("osb_hi"), sem("osb_lo")
        sb_pv, osb_out = sem("sb_pv"), sem("osb_out")
        low_split, low_mm, low_out, up_mm = sem("low_split"), sem("low_mm"), sem("low_out"), sem("up_mm")
        gate_log, b_ready = sem("gate_log"), sem("b_ready")
        g_diff, g_exp, g_fac, g_mm, g_sel = sem("g_diff"), sem("g_exp"), sem("g_fac"), sem("g_mm"), sem("g_sel")
        kd_ready, kd_turned, kd_out = sem("kd_ready"), sem("kd_turned"), sem("kd_out")
        st_mm, st_ready, go_mm, go_act, go_dve = sem("st_mm"), sem("st_ready"), sem("go_mm"), sem("go_act"), sem("go_dve")
        gss_ready, gvar_ready, ggs_ready, gout_ready = sem("gss_ready"), sem("gvar_ready"), sem("ggs_ready"), sem("gout_ready")
        rope_src, rope_done, lam_sum, lam_exp = sem("rope_src"), sem("rope_done"), sem("lam_sum"), sem("lam_exp")
        v_hi, v_lo, qk_hi, qk_lo = sem("v_hi"), sem("v_lo"), sem("qk_hi"), sem("qk_lo")
        s_mm = [sem("s_mm0"), sem("s_mm1")]
        s_max = [sem("s_max0"), sem("s_max1")]
        s_exp = [sem("s_exp0"), sem("s_exp1")]
        rec_made, ratio_made, p_mixed = sem("rec_made"), sem("ratio_made"), sem("p_mixed")
        p_turned, pt_hi, pt_lo, o_mm, o_out = sem("p_turned"), sem("pt_hi"), sem("pt_lo"), sem("o_mm"), sem("o_out")
        ot_out, o_turned = sem("ot_out"), sem("o_turned")
        ovar_ready, ogs_ready, o_normed = sem("ovar_ready"), sem("ogs_ready"), sem("o_normed")

        junctions = {"h": (None, None, None, 0, 0, 0), "h_mlp0": (0, None, None, 0, 1, 1),
                     "h_mix1": (3 * 4, "F", 2, 0, 3, 2), "h_mlp1": (3 * 5, "P", 4, 1, 5, 3),
                     "h_conv": (3 * 9, "P", 6, 2, 7, 4), "h_mlp2": (3 * 10, "P", 8, 3, 9, 5),
                     "out": (3 * 14, "P", 10, 4, None, 6)}
        after_block = {"h": 0, "h_mlp0": ph["mlp0"].b, "h_mix1": ph["qk"].b, "h_mlp1": ph["mlp1"].b,
                       "h_conv": ph["conv_in"].b, "h_mlp2": ph["mlp2"].b, "out": n_blocks}
        turns = {"h": 8, "o_gla": 8, "h_mlp0": 8, "h_mix1": 8, "o_diff": 8, "h_mlp1": 8,
                 "h_conv": 8, "h_mlp2": 8}
        turn_base, n = {}, 0
        for name, k in turns.items():
            turn_base[name] = n
            n += k
        turn_banks = {"h": 0, "o_gla": ph["proj_sb"].b % 2, "h_mlp0": ph["mlp0"].b % 2,
                      "h_mix1": ph["qk"].b % 2, "o_diff": ph["w_o"].b % 2, "h_mlp1": ph["mlp1"].b % 2,
                      "h_conv": ph["conv_in"].b % 2, "h_mlp2": ph["mlp2"].b % 2}
        G_GLA, G_SUBLN = 0, 2

        GAIN_LOADS = 4
        SB_Z, SB_OUT = (2048, 0), (7, 3)
        DIFF_S, DIFF_TURN, DIFF_OUT = (2048, 0), 3, 7
        NORM_HEADS = (slice(0, TT * (DIFF_HEADS - 2)), slice(TT * (DIFF_HEADS - 2), TT * DIFF_HEADS))
        len_batch = (512, 512, 256)
        low_bank = 4 * (ph["g_out"].b % 2)
        up_bank = 4 * ((ph["g_out"].b + 1) % 2)
        m_min, u_abs = qkf[:, 0:2048], qkf[:, 2048:4096]
        gate_u = sem("gate_u")
        clamped = sem("clamped")
        last_tap = sem("last_tap")
        gates_made = sem("gates_made")
        low_t = qkf[0:GLA_RANK, 0:SEQ]
        gains_turned, gains_out = sem("gains_turned"), sem("gains_out")
        low_split_hi, sem_grstd, sem_orstd = sem("low_split_hi"), sem("gla_rstd_ready"), sem("o_rstd_ready")

        class Steps:

            def __init__(self, eng, sm):
                self.eng, self.sm, self.n = eng, sm, 0

            def __call__(self, ins):
                self.n += 1
                ins.then_inc(self.sm, 1)
                self.eng.wait_ge(self.sm, self.n)

        def slot_fill(p, blk, qi):
            if p.quads == 1:
                return (p.q + blk + 2) // 2 + 1
            assert p.q % 2 == 0
            return p.q // 2 + blk + 2

        def tok_block(dst, blk):
            return dst[:, :, bass.ds(blk * NBLK, NBLK)]

        def fm_tiles(dst, blk, c):
            return dst.rearrange("p (a b) -> p a b", a=8)[:, 4 * blk + 2 * c:4 * blk + 2 * c + 2]

        def fm_block(dst, blk):
            return dst.rearrange("p (a b) -> p a b", a=8)[:, 4 * blk:4 * blk + 4]

        def clear_y(eng, n):
            nc.vector.memset(yf, 0.0).then_inc(y_clear, 1)
            eng.wait_ge(y_clear, n)

        def gemm_low_up(pe, mm):
            pe.wait_ge(low_out, 1)
            pe.wait_ge(up_in, 16)
            for h in range(GLA_HEADS):
                last = mm(ps[:, up_bank + h], w_up16[:, GLA_DK * h:GLA_DK * (h + 1)], low_t, start=True, stop=True)
            last.then_inc(up_mm, 1)
            pe.wait_ge(gate_u, 1)

        def turn_bank(name, k):
            return (4 * turn_banks[name] + k) % 8

        def tile_bank(name, i, half):
            return (4 * (after_block[name] % 2) + 2 * i + half) % 8

        def tile_lo(name, quad):
            return turn_base[name] + 7 + quad

        def stat_count(name, n, i):
            _, _, add, _, turn_, _ = junctions[name]
            if add is None:
                return 4 * n + i + 1
            first = 4 * add
            if turn_ is None:
                return first + i + 1
            if n == add:
                return first + (1 if i == 0 else 2 * i)
            return first + (2 * i + 3 if i < TT - 1 else 2 * TT)

        def level_col(n):
            return 2048 * ((ph["g_out"].b + n) % 2)

        def sb_z(u):
            return psf[:, SB_Z[u]:SB_Z[u] + TRI]

        def quad_at(p, blk, qi):
            return p.q + blk * p.quads + qi

        def slot_of(p, u, qi):
            return (p.q + u * p.quads + qi) % 2

        def pairs(eng, p, blocks=None, peel=0):
            blocks = p.blocks if blocks is None else blocks
            assert blocks % 2 == 0
            for n in range(0, min(peel, blocks), 2):
                yield n
            left = blocks - peel
            if left == 2:
                yield peel
            elif left > 2:
                with eng.Fori(peel // 2, blocks // 2) as i:
                    yield i * 2

        block = ctx.enter_context(nc.Block())

        @block.sync
        def _(sp):
            def load(p, blk, u, src):
                for qi in range(p.quads):
                    n = quad_at(p, blk, qi)
                    s = slot_of(p, u, qi)
                    if not (isinstance(n, int) and n < 2):
                        sp.wait_ge(lo_ready, n - 1)
                    sp.dma_start(w_raw[:, s], src(blk, qi).rearrange("(a p) n -> p a n", p=P)).then_inc(raw_full[s], 16)

            def stream(name, src):
                p = ph[name]
                if p.blocks % 2:
                    return load(p, 0, 0, src)
                for blk in pairs(sp, p):
                    for u in range(2):
                        load(p, blk + u, u, src)

            def cols(wt, c0=0):
                return lambda blk, qi: wt[QUAD * P * qi:QUAD * P * (qi + 1), bass.ds(c0 + blk * NBLK, NBLK)]

            def mlp(name, up, down):
                p = ph[name]
                with sp.Fori(0, ROUNDS) as r:
                    for u in range(2):
                        load(p, r * 4 + u, u, lambda blk, qi: up[QUAD * P * qi:QUAD * P * (qi + 1),
                                                                 bass.ds(r * D + u * NBLK, NBLK)])
                    for u in range(2):
                        load(p, r * 4 + 2 + u, u, lambda blk, qi: down[bass.ds(r * D + qi * QUAD * P, QUAD * P),
                                                                       u * NBLK:(u + 1) * NBLK])

            w_in = w["w_in"][0]
            for i in range(TT):
                sp.dma_start(x_tm[:, i], w["x"][0, P * i:P * (i + 1), :]).then_inc(x_in[i], 16)
            stream("sb_qk", cols(w_in, C_SBQ))
            stream("sb_v", cols(w_in, C_SBV))
            stream("g_qk", cols(w_in, C_GQ))
            stream("g_v", cols(w_in, C_GV))
            stream("g_out", cols(w_in, C_GOUT))
            stream("gate_sb", cols(w_in, C_GATE_SB))
            stream("gate_gla", cols(w_in, C_GATE_GLA))
            stream("proj_sb", cols(w["w_proj_sb"][0]))
            stream("proj_gla", cols(w["w_proj_gla"][0]))
            stream("w_out", cols(w["w_out"][0]))
            mlp("mlp0", w["w_ff1"][0], w["w_ff2"][0])
            stream("qk", cols(w["attn_w_qkv_2"][0]))
            stream("v", cols(w["attn_w_qkv_2"][0], 2 * D))
            stream("w_o", cols(w["attn_w_o_2"][0]))
            mlp("mlp1", w["mlp_w_up_2"][0], w["mlp_w_down_2"][0])
            stream("conv_in", cols(w["conv_w_in_2"][0]))
            stream("conv_out", cols(w["conv_w_out_2"][0]))
            mlp("mlp2", w["mlp_w_up_2"][1], w["mlp_w_down_2"][1])
            for i in range(TT):
                sp.wait_ge(resid_ready, 4 * 4 + i + 1)
                sp.dma_start(out[0, P * i:P * (i + 1), :], x_tm[:, i]).then_inc(out_sent, 16)
            sp.wait_ge(out_sent, 16 * TT)

        @block.gpsimd
        def _(pool):
            dma = pool.dma_start
            pstep = Steps(pool, pool_step)

            def gain_row(dst, name, row=None):
                src = w[name] if row is None else w[name][row]
                dma(dst, src.rearrange("(a n) -> a n", a=1).partition_broadcast(P)).then_inc(grow_in, 16)

            def refine(name, n, i):
                pool.wait_ge(sumsq_ready, stat_count(name, n, i))
                v, y, t, r, ss = (z[n % 2][:, i:i + 1] for z in (var, guess0, newton, rstd, sumsq))
                pstep(nc.gpsimd.tensor_scalar(v, ss, 1.0 / D, EPS, ALU.mult, ALU.add))
                pool.wait_ge(guess_ready, stat_count(name, n, i))
                pstep(nc.gpsimd.tensor_tensor(t, y, y, ALU.mult))
                pstep(nc.gpsimd.tensor_tensor(t, t, v, ALU.mult))
                pstep(nc.gpsimd.tensor_scalar(t, t, -0.5, 1.5, ALU.mult, ALU.add))
                nc.gpsimd.tensor_tensor(r, t, y, ALU.mult).then_inc(rstd_ready, 1)

            def refine_tiles(name):
                _, _, add, _, turn_, _ = junctions[name]
                for s_ in range(TT + 1):
                    if add is not None and s_ < TT:
                        refine(name, add, s_)
                    if turn_ is not None and s_ > 0:
                        refine(name, turn_, s_ - 1)

            nc.gpsimd.memset(eps_col, EPS).then_inc(eps_set, 1)
            dma(tmp[:, 0:P], w["shape_consts"][:, K_CAUSAL:K_CAUSAL + P]).then_inc(consts_in, 16)
            dma(masks_f, w["shape_consts"][:, K_MASKS:K_ALL]).then_inc(consts_in, 16)
            rows = [(w["gla_norm"][0].rearrange("(k p) -> k p", p=P), 2), (w["attn_subln_g_2"], 1),
                    (w["b_gate_up"][0].rearrange("(k p) -> k p", p=P), GLA_HEADS),
                    (w["conv_w_2"][0].rearrange("c (k p) -> (c k) p", p=P), 3 * KT)]
            r = 0
            for src, n in rows:
                dma(gain_rows[r:r + n], src).then_inc(gains_in, 16)
                r += n
            assert r == N_GAINS

            refine_tiles("h")
            def sb_after(t, u):
                pool.wait_ge(sp_made, t + 1)
                sp = sb_sp[u]
                nc.gpsimd.tensor_tensor(sp[:, AFTER[0] + P:AFTER[0] + 2 * P], sp[:, COL[1] + P:COL[1] + 2 * P],
                                        sp[:, COL[2]:COL[2] + P], ALU.add)
                for j in range(3):
                    last = nc.gpsimd.tensor_copy(sp[:, AFTER[j]:AFTER[j] + P], sp[:, COL[j + 1]:COL[j + 1] + P])
                last.then_inc(sp_after, 1)

            with pool.Fori(0, SB_HEADS // 2) as i:
                for u in range(2):
                    sb_after(i * 2 + u, u)

            pool.wait_ge(osb_lo, 1)
            dma(tmp[:, 0:KT * P].rearrange("p (a b) -> p a b", a=KT),
                w["w_in"][0][:, C_LOW:C_LOW + P].rearrange("(a p) n -> p a n", p=P)).then_inc(low_in, 16)
            dma(w_up16, w["w_gate_up"][0]).then_inc(up_in, 16)

            pool.wait_ge(b_ready, 1)
            for n in range(LEVELS):
                h = 1 << n
                if n >= 4:
                    pool.wait_ge(g_mm, n - 2)
                b2 = b_cum.rearrange("p (m two n) -> p m two n", two=2, n=h)
                f2 = g_f[n % 4].rearrange("p (m two n) -> p m two n", two=2, n=h)
                mid = b2[:, :, 0, h - 1:h].to_broadcast([P, 2048 // (2 * h), h])
                nc.gpsimd.tensor_tensor(f2[:, :, 1], b2[:, :, 1], mid, ALU.subtract)
                nc.gpsimd.tensor_tensor(f2[:, :, 0], mid, b2[:, :, 0], ALU.subtract).then_inc(g_diff, 1)

            pool.wait_ge(go_mm, 4)
            dma(x_tm[:], w["x"][0].rearrange("(i p) n -> p i n", p=P)).then_inc(x_again, 16)
            pool.wait_ge(chunk_lo, 4)
            gain_row(g_turn, "norm_mlp", 0)
            refine_tiles("h_mlp0")
            pool.wait_ge(normed, 8)
            gain_row(g_add, "norm_final")
            gain_row(g_turn, "norm_mixer_pre_2", 0)
            refine_tiles("h_mix1")
            pool.wait_ge(resid_ready, 4)
            dma(tmp[:, 0:2 * SEQ], w["shape_consts"][:, K_COS:K_MASKS]).then_inc(tables_in, 16)
            for n, name in enumerate(("q1", "k1", "q2", "k2")):
                dma(lam_in[:, n], w[f"attn_lambda_{name}_2"].partition_broadcast(P)).then_inc(tables_in, 16)
            half = ROT // 2
            for blk in range(4):
                pool.wait_ge(rope_src, blk + 1)
                r4 = rot[blk % 2].rearrange("p (a b) -> p a b", a=4)
                for base in (0, DIFF_DIM):
                    for a, b in ((0, half), (half, 0)):
                        dma(r4[base + a:base + a + half], qk[base + b:base + b + half, 4 * blk:4 * blk + 4]).then_inc(swapped[blk % 2], 16)
            pool.wait_ge(turned_lo, turn_base["o_diff"] + KT)
            gain_row(g_add, "norm_mixer_post_2", 0)
            gain_row(g_turn, "norm_mlp_pre_2", 0)
            refine_tiles("h_mlp1")
            pool.wait_ge(normed, 16)
            gain_row(g_add, "norm_mlp_post_2", 0)
            gain_row(g_turn, "norm_mixer_pre_2", 1)
            refine_tiles("h_conv")
            pool.wait_ge(chunk_lo, 4 + 2 * 16 + 8)
            gain_row(g_add, "norm_mixer_post_2", 1)
            gain_row(g_turn, "norm_mlp_pre_2", 1)
            refine_tiles("h_mlp2")
            pool.wait_ge(normed, 24)
            gain_row(g_add, "norm_mlp_post_2", 1)
            refine_tiles("out")

        @block.tensor
        def _(pe):
            mm = nc.tensor.matmul

            def gemm(name, operand, token_major, waits=None, ordered=False, begun=False, after_first=None):
                p = ph[name]
                hi, lo = operand

                def one(blk, u):
                    blk_no = p.b + blk
                    bank0 = 4 * ((p.b + u) % 2)
                    if not (isinstance(blk_no, int) and blk_no < 2):
                        pe.wait_ge(banks_free, blk_no - 1)
                    for qi in range(p.quads):
                        n, s = quad_at(p, blk, qi), slot_of(p, u, qi)
                        pe.wait_ge(lo_ready, n + 1)
                        for sm, value in (waits(blk, qi) if waits else ()):
                            pe.wait_ge(sm, value)
                        if begun and isinstance(blk, int) and blk == 0 and qi == 0:
                            multiply_half(hi, lo, s, bank0, 1).then_inc(quad_done, 1)
                        elif ordered and blk == 1 and qi == 1:
                            multiply_ordered(hi, lo, s, bank0).then_inc(quad_done, 1)
                        else:
                            multiply(hi, lo, s, qi, bank0, p.quads, token_major,
                                     begun and isinstance(blk, int) and blk == 0).then_inc(quad_done, 1)
                        if after_first and blk == 0 and qi == 0:
                            after_first()

                if p.blocks % 2:
                    return one(0, 0)
                for blk in pairs(pe, p, peel=2 if begun else 0):
                    for u in range(2):
                        one(blk + u, u)

            def multiply(hi, lo, s, qi, bank0, quads, token_major, halves=False):
                for a in range(QUAD):
                    k = QUAD * qi + a
                    for j in range(4):
                        js = slice(P * j, P * (j + 1))
                        if token_major:
                            parts = ((hi[:, k, js], w_hi[:, s, a]), (hi[:, k, js], w_lo[:, s, a]), (lo[:, k, js], w_hi[:, s, a]))
                        else:
                            parts = ((w_hi[:, s, a, js], hi[:, k]), (w_hi[:, s, a, js], lo[:, k]), (w_lo[:, s, a, js], hi[:, k]))
                        for x, (left, right) in enumerate(parts):
                            last = mm(ps[:, bank0 + j], left, right, start=(k == 0 and x == 0),
                                      stop=(k == QUAD * quads - 1 and x == 2), skip_group_check=halves)
                return last

            def multiply_ordered(hi, lo, s, bank0):
                for j in range(TT):
                    js = slice(P * j, P * (j + 1))
                    for a in range(QUAD):
                        k = QUAD + a
                        for x, (left, right) in enumerate(((hi[:, k, js], w_hi[:, s, a]), (hi[:, k, js], w_lo[:, s, a]),
                                                           (lo[:, k, js], w_hi[:, s, a]))):
                            last = mm(ps[:, bank0 + j], left, right, start=False, stop=(a == QUAD - 1 and x == 2))
                    if j < TT - 1:
                        last.then_inc(tile_done, 1)
                return last

            def multiply_half(hi, lo, s, bank0, half, ks=range(QUAD)):
                ts_ = slice(SEQ // 2 * half, SEQ // 2 * (half + 1))
                for k in ks:
                    for j in range(4):
                        js = slice(P * j, P * (j + 1))
                        for x, (left, right) in enumerate(((w_hi, hi), (w_hi, lo), (w_lo, hi))):
                            last = mm(ps[:, bank0 + j, ts_], left[:, s, k, js], right[:, k, ts_],
                                      start=(half == 0 and k == 0 and x == 0), stop=False, skip_group_check=True)
                return last

            def turn(name, src, wait):
                for k in range(turns[name]):
                    for i in range(TT):
                        for sm, value in wait(k, i):
                            pe.wait_ge(sm, value)
                        last = nc.tensor.transpose(ps[:, turn_bank(name, k), P * i:P * (i + 1)], src(i, k), ident)
                    last.then_inc(turned, 1)

            def turn_tiles(name, p):
                before = junctions[name][5]
                if after_block[name]:
                    pe.wait_ge(banks_free, after_block[name] - 1)
                for i in range(TT):
                    pe.wait_ge(normed, 4 * before + i + 1)
                    for half in range(2):
                        for a in range(4):
                            k = 4 * half + a
                            last = nc.tensor.transpose(ps[:, tile_bank(name, i, half), P * a:P * (a + 1)],
                                                       y_tm[:, i, P * k:P * (k + 1)], ident)
                        last.then_inc(turned, 1)
                    if i == TT - 2:
                        pe.wait_ge(lo_ready, p.q + 1)
                        pe.wait_ge(turned_lo, turn_base[name] + 4)
                        multiply_half(a_hi, a_lo, slot_of(p, 0, 0), 4 * (p.b % 2), 0, range(0, 2))
                multiply_half(a_hi, a_lo, slot_of(p, 0, 0), 4 * (p.b % 2), 0, range(2, 4))

            def turned_waits(name):
                if name in junctions:
                    return lambda blk, qi: [(turned_lo, tile_lo(name, qi))]
                return lambda blk, qi: [(turned_lo, turn_base[name] + 4 * qi + 4)]

            A, H = (a_hi, a_lo), (h_hi, h_lo)

            def mlp(name, turned_name, chunks):
                p = ph[name]

                def rounds(r):
                    for u in range(4):
                        blk = r * 4 + u
                        bank0 = 4 * ((p.b + u) % 2)
                        pe.wait_ge(banks_free, p.b + blk - 1)
                        for qi in range(2):
                            n, s = quad_at(p, blk, qi), slot_of(p, u, qi)
                            pe.wait_ge(lo_ready, n + 1)
                            if u < 2:
                                pe.wait_ge(turned_lo, tile_lo(turned_name, qi))
                            else:
                                pe.wait_ge(chunk_lo, chunks + r * 4 + 2 * qi + 2)
                            hi, lo = A if u < 2 else H
                            if isinstance(r, int) and u == 0 and qi == 0:
                                multiply_half(hi, lo, s, bank0, 1).then_inc(quad_done, 1)
                            elif u == 3 and qi == 1:
                                multiply_ordered(hi, lo, s, bank0).then_inc(quad_done, 1)
                            else:
                                multiply(hi, lo, s, qi, bank0, 2, u >= 2, isinstance(r, int) and u == 0).then_inc(quad_done, 1)

                rounds(0)
                with pe.Fori(1, ROUNDS) as r:
                    rounds(r)

            pe.wait_ge(ident_in, 16)
            turn_tiles("h", ph["sb_qk"])
            gemm("sb_qk", A, False, turned_waits("h"), begun=True)
            gemm("sb_v", A, True)

            pe.wait_ge(banks_free, ph["sb_v"].b)
            pe.wait_ge(consts_r, 5)

            def sb_region(t):
                return sb_z(t % 2)

            def sb_scores(t):
                z = sb_region(t)
                rows = slice(SB_DIM * (t % 2), SB_DIM * (t % 2) + SB_DIM)
                (qh, kh), (ql, kl) = ((z_[rows, t // 2], z_[rows, 4 + t // 2]) for z_ in (sbq_hi, sbq_lo))
                if t >= 2:
                    pe.wait_ge(w_exp, t - 1)
                for j in (0, 1, 3, 2):
                    out_ = z[:, COL[j]:COL[j] + SEQ - P * j]
                    js = slice(P * j, P * (j + 1))
                    for x, (k_, q_) in enumerate(((kh, qh), (kh, ql), (kl, qh))):
                        mm(out_, k_[:, js], q_[:, P * j:], start=(x == 0 and j != 3), stop=True, skip_group_check=True)
                    last = mm(out_[:, 0:P], ident_b[:], strict_b[:], start=False, stop=True, skip_group_check=True)
                last.then_inc(z_ready, 1)

            def sb_sums(t):
                z = sb_region(t)
                pe.wait_ge(sp_lo, t + 1)
                for part in (sb_hi[t % 2], sb_lo[t % 2]):
                    for c, n in ((0, 512), (512, 512), (1024, 256)):
                        mm(z[:, c:c + n], ntri[:], part[:, c:c + n], start=False, stop=True, skip_group_check=True)
                    for j in range(3):
                        n, c = SEQ - P * (j + 1), COL[j] + P
                        last = mm(z[:, c:c + n], nones[:], part[:, AFTER[j]:AFTER[j] + n], start=False, stop=True,
                                  skip_group_check=True)
                last.then_inc(c_ready, 1)

            def sb_values(t):
                pe.wait_ge(sbw_lo, t + 1)
                if t >= 2:
                    pe.wait_ge(osb_out, t - 1)
                vs = slice(P * (t // 2), P * (t // 2 + 1))
                w_h, w_l = sb_whi[t % 2], sb_wlo[t % 2]
                for j in range(TT):
                    ws = slice(COL[j], COL[j] + SEQ - P * j)
                    for x, (v_, w_) in enumerate(((sbv_hi, w_h), (sbv_hi, w_l), (sbv_lo, w_h))):
                        last = mm(ps[:, SB_OUT[t % 2], P * j:], v_[:, j, vs], w_[:, ws], start=(j == 0 and x == 0), stop=True,
                                  skip_group_check=True)
                last.then_inc(sb_pv, 1)

            for t in range(SB_HEADS + 1):
                if t < SB_HEADS:
                    sb_scores(t)
                if t == 0:
                    pe.wait_ge(gains_in, GAIN_LOADS * 16)
                    nc.tensor.transpose(ps[:, 7, 0:N_GAINS], gain_rows[0:N_GAINS], ident[0:N_GAINS, 0:N_GAINS]).then_inc(gains_turned, 1)
                    pe.wait_ge(gains_out, 1)
                if 1 <= t <= SB_HEADS:
                    sb_sums(t - 1)
                if t >= 2:
                    sb_values(t - 2)
            pe.wait_ge(osb_out, SB_HEADS - 1)
            gemm("g_qk", A, False, lambda blk, qi: [(osb_out, SB_HEADS)] if blk else [],
                 after_first=lambda: sb_values(SB_HEADS - 1))
            gemm("g_v", A, True)

            low_bank = 4 * (ph["g_out"].b % 2)
            pe.wait_ge(banks_free, ph["g_out"].b)
            pe.wait_ge(low_split, 1)
            low_hi = hhf[:, 2048:3072].rearrange("p (a b) -> p a b", a=KT)
            low_lo = hlf[:, 2048:3072].rearrange("p (a b) -> p a b", a=KT)
            for k in range(KT):
                for x, (left, right) in enumerate(((low_hi, a_hi), (low_hi, a_lo), (low_lo, a_hi))):
                    last = mm(ps[:, low_bank], left[:, k], right[:, k], start=(k == 0 and x == 0), stop=(k == KT - 1 and x == 2))
            last.then_inc(low_mm, 1)
            gemm_low_up(pe, mm)
            gemm("g_out", A, True)

            for n in range(LEVELS + 1):
                pe.wait_ge(g_fac, n) if n else pe.wait_ge(banks_free, ph["gate_sb"].b - 1)
                if n >= 2:
                    pe.wait_ge(g_sel, n - 1)
                if n == 1:
                    pe.wait_ge(banks_free, ph["gate_sb"].b)
                left, right = (g_k, g_q) if n == 0 else (g_f[(n - 1) % 4], g_f[(n - 1) % 4])
                for m in range(16):
                    ms = slice(P * m, P * (m + 1))
                    last = mm(psf[:, level_col(n) + P * m:level_col(n) + P * (m + 1)], left[:, ms], right[:, ms],
                              start=True, stop=True)
                last.then_inc(g_mm, 1)
            pe.wait_ge(kd_ready, 1)
            pe.wait_ge(g_sel, LEVELS + 1)
            for m in range(12):
                h, c = m // 3, m % 3
                col = SEQ * h + P * c
                last = nc.tensor.transpose(psf[:, P * m:P * (m + 1)], g_k[:, col:col + P], ident)
            last.then_inc(kd_turned, 1)
            pe.wait_ge(kd_out, 1)
            for m in range(12):
                h, c = m // 3, m % 3
                dst = psf[:, 1024 + GLA_DV * (4 * c + h):1024 + GLA_DV * (4 * c + h + 1)]
                last = mm(dst, g_kt[:, P * m:P * (m + 1)], x_tm[:, c, GLA_DV * h:GLA_DV * (h + 1)], start=True, stop=True)
            last.then_inc(st_mm, 1)
            pe.wait_ge(st_ready, 3)
            for c in range(TT):
                for h in range(GLA_HEADS):
                    dst = ps[:, 2 * c + h // 2, GLA_DV * (h % 2):GLA_DV * (h % 2 + 1)]
                    col = SEQ * h + P * c
                    last = mm(dst, g_at[:, col:col + P], x_tm[:, c, GLA_DV * h:GLA_DV * (h + 1)], start=True, stop=(c == 0))
                    if c:
                        last = mm(dst, g_q[:, col:col + P], g_state[c - 1][:, GLA_DV * h:GLA_DV * (h + 1)], start=False, stop=True)
                last.then_inc(go_mm, 1)
            pe.wait_ge(go_act, 2)
            pe.wait_ge(go_dve, 2)
            gemm("gate_sb", A, False)
            gemm("gate_gla", A, False)
            pe.wait_ge(banks_free, ph["proj_sb"].b)
            turn("o_gla", lambda i, k: y_tm[:, i, P * k:P * (k + 1)], lambda k, i: [] if k else [(gout_ready, i + 1)])
            pe.wait_ge(turned_lo, turn_base["o_gla"] + 4)
            pe.wait_ge(osb_lo, 1)
            gemm("proj_sb", H, False, lambda blk, qi: [(turned_lo, turn_base["o_gla"] + 4 * blk + 4)])
            gemm("proj_gla", A, False, turned_waits("o_gla"))
            gemm("w_out", H, True, lambda blk, qi: [(chunk_lo, 2 * qi + 2)], True)
            turn_tiles("h_mlp0", ph["mlp0"])
            mlp("mlp0", "h_mlp0", 4)
            turn_tiles("h_mix1", ph["qk"])
            gemm("qk", A, False, turned_waits("h_mix1"), begun=True)
            gemm("v", A, True)

            pe.wait_ge(banks_free, ph["w_o"].b - 1)
            pe.wait_ge(qk_lo, 4)

            def diff_scores(t, c):
                rows = slice(DIFF_DIM * c, DIFF_DIM * (c + 1))
                (qh, kh), (ql, kl) = (z_[rows, t] for z_ in diff_qk_hi), (qk_r[rows, 8 * z_ + t] for z_ in range(2))
                if t:
                    pe.wait_ge(s_exp[c], t)
                elif c:
                    pe.wait_ge(banks_free, ph["w_o"].b)
                s = psf[:, DIFF_S[c]:DIFF_S[c] + TRI]
                for i in (3, 2, 0, 1):
                    n = P * (i + 1)
                    for x, (q_, k_) in enumerate(((qh, kh), (qh, kl), (ql, kh))):
                        mm(s[:, ROW[i]:ROW[i] + n], q_[:, P * i:P * (i + 1)], k_[:, 0:n], start=(i != 0 and x == 0), stop=True,
                           skip_group_check=True)
                    last = mm(s[:, ROW[i] + n - P:ROW[i] + n], ident_b[:], causal_b[:], start=False, stop=True,
                              skip_group_check=True)
                last.then_inc(s_mm[c], 1)

            batches = (((0, 0), (1, 0), (2, 0), (3, 0)), ((1, 1), (2, 1), (3, 1), (3, 3)), ((2, 2), (3, 2)))

            def diff_turn(t, b):
                pe.wait_ge(p_mixed, t + 1)
                if 3 * t + b:
                    pe.wait_ge(pt_lo, 3 * t + b)
                for n, (i, j) in enumerate(batches[b]):
                    c = ROW[i] + P * j
                    last = nc.tensor.transpose(ps[:, DIFF_TURN, P * n:P * (n + 1)], d_p[t % 2][0][:, c:c + P], ident)
                last.then_inc(p_turned, 1)

            def diff_values(t):
                pe.wait_ge(pt_lo, 3 * t + 3)
                if t:
                    pe.wait_ge(o_out, t)
                else:
                    pe.wait_ge(v_lo, 1)
                for j in range(TT):
                    ph_, pl_ = d_hi[t % 2][:, COL[j]:COL[j] + SEQ - P * j], d_lo(t % 2, COL[j], SEQ - P * j)
                    vs = slice(D * j + P * t, D * j + P * (t + 1))
                    for x, (left, right) in enumerate(((ahf[:, vs], ph_), (alf[:, vs], ph_), (ahf[:, vs], pl_))):
                        last = mm(ps[:, DIFF_OUT, P * j:], left, right, start=(j == 0 and x == 0), stop=True,
                                  skip_group_check=True)
                last.then_inc(o_mm, 1)

            def diff_back(t):
                pe.wait_ge(ot_out, t + 1)
                for i in range(TT):
                    last = nc.tensor.transpose(ps[:, DIFF_OUT, P * i:P * (i + 1)], qk[:, 8 + t, P * i:P * (i + 1)], ident)
                last.then_inc(o_turned, 1)

            for t in range(DIFF_HEADS + 3):
                for c in range(2):
                    if t < DIFF_HEADS:
                        diff_scores(t, c)
                    if c == 0 and t >= 3:
                        diff_back(t - 3)
                    if 1 <= t <= DIFF_HEADS:
                        diff_turn(t - 1, c)
                if 1 <= t <= DIFF_HEADS:
                    diff_turn(t - 1, 2)
                if 2 <= t < DIFF_HEADS + 2:
                    diff_values(t - 2)
            pe.wait_ge(o_out, DIFF_HEADS)
            turn("o_diff", lambda i, k: qk[:, k, P * i:P * (i + 1)], lambda k, i: [] if i else [(o_normed, k // 2 + 1)])
            gemm("w_o", A, True, turned_waits("o_diff"), True)
            turn_tiles("h_mlp1", ph["mlp1"])
            mlp("mlp1", "h_mlp1", 4 + 16)
            turn_tiles("h_conv", ph["conv_in"])
            gemm("conv_in", A, False, turned_waits("h_conv"), begun=True)
            gemm("conv_out", H, True, lambda blk, qi: [(chunk_lo, 4 + 32 + 4 * qi + 4)], True)
            turn_tiles("h_mlp2", ph["mlp2"])
            mlp("mlp2", "h_mlp2", 4 + 32 + 8)

        @block.scalar
        def _(act):
            step = Steps(act, act_step)

            def split(p, blk, u, qi):
                n, s = quad_at(p, blk, qi) + 2, slot_of(p, u, qi)
                if isinstance(n, int) and n >= n_quads:
                    return
                act.wait_ge(raw_full[s], slot_fill(p, blk, qi) * 16)
                act.wait_ge(quad_done, n - 1)
                nc.scalar.activation(w_hi[:, s], w_raw[:, s], ACT.Copy).then_inc(hi_ready, 1)

            def first_split(s):
                act.wait_ge(raw_full[s], 16)
                nc.scalar.activation(w_hi[:, s], w_raw[:, s], ACT.Copy).then_inc(hi_ready, 1)

            def body(p, blk, u, evac=None):
                for qi in range(p.quads):
                    split(p, blk, u, qi)
                if evac:
                    act.wait_ge(quad_done, quad_at(p, blk, p.quads))
                    evac(blk, 4 * ((p.b + u) % 2))

            def phase(name, evac=None):
                p = ph[name]
                if p.blocks % 2:
                    return body(p, 0, 0, evac)
                for blk in pairs(act, p):
                    for u in range(2):
                        body(p, blk + u, u, evac)

            def gates(dst, moved, base):
                def evac(blk, bank0):
                    d = dst(blk)
                    act.wait_ge(moved, base + blk + 1)
                    step(nc.scalar.activation(d, d, ACT.Exp, scale=-1.0))
                    step(nc.scalar.activation(d, d, ACT.Ln, bias=1.0))
                    nc.scalar.activation(d, d, ACT.Exp, scale=-1.0).then_inc(gates_made, 1)
                return evac

            def round_chunk(n, src, dst):
                act.wait_ge(chunk_f32, n)
                nc.scalar.activation(dst, src, ACT.Copy).then_inc(chunk_hi, 1)

            def mlp(name, chunks):
                p = ph[name]

                def rounds(r, tail=False):
                    for u in range(4):
                        blk = r * 4 + u
                        for qi in range(1 if tail and u == 3 else 2):
                            split(p, blk, u, qi)
                        if u < 2:
                            bank0 = 4 * ((p.b + u) % 2)
                            act.wait_ge(quad_done, quad_at(p, blk, 2))
                            for c in range(2):
                                g = chunks + r * 4 + 2 * u + c
                                act.wait_ge(chunk_lo, g - 1)
                                nc.scalar.activation(tmp4[:, 2 * c:2 * c + 2], ps[:, bank0 + 2 * c:bank0 + 2 * c + 2],
                                                     ACT.Relu).then_inc(exp_ready, 1)
                            for c in range(2):
                                g = chunks + r * 4 + 2 * u + c
                                round_chunk(g + 1, tmp4[:, 2 * c:2 * c + 2], h_hi[:, 4 * u + 2 * c:4 * u + 2 * c + 2])

                with act.Fori(0, ROUNDS - 1) as r:
                    rounds(r)
                rounds(ROUNDS - 1, True)

            def square(name, n, i, src):
                ss, lv, y = (z[n % 2][:, i:i + 1] for z in (sumsq, log_var, guess0))
                count = stat_count(name, n, i)
                if count > 1:
                    act.wait_ge(sumsq_ready, count - 1)
                nc.scalar.activation(junk, src[:, i], ACT.Square, accum_out=ss).then_inc(sumsq_ready, 1)
                act.wait_ge(sumsq_ready, count)
                step(nc.scalar.activation(lv, ss, ACT.Ln, bias=eps_col, scale=1.0 / D))
                nc.scalar.activation(y, lv, ACT.Exp, scale=-0.5).then_inc(guess_ready, 1)

            def junction(name, last_split, early_split=None):
                tile0, kind, add, adds, turn_, _ = junctions[name]
                for s_ in range(TT + 3):
                    if s_ < TT:
                        if name == "h":
                            act.wait_ge(x_in[s_], 16)
                        elif s_ < 3:
                            act.wait_ge(tile_out, tile0 + s_ + 1)
                        else:
                            act.wait_ge(banks_free, after_block[name])
                        square(name, turn_ if add is None else add, s_, y_tm if kind == "P" else x_tm)
                    if turn_ is not None and add is not None and 1 <= s_ <= TT:
                        act.wait_ge(resid_ready, 4 * adds + s_)
                        square(name, turn_, s_ - 1, x_tm)
                    if s_ == 3 and early_split:
                        early_split()
                    if turn_ is not None and s_ >= 3:
                        for half in range(2):
                            i = s_ - 3
                            act.wait_ge(turned, turn_base[name] + 2 * i + half + 1)
                            nc.scalar.activation(a_hi[:, 4 * half:4 * half + 4, P * i:P * (i + 1)],
                                                 ps[:, tile_bank(name, i, half)].rearrange("p (a b) -> p a b", a=4),
                                                 ACT.Copy).then_inc(turned_hi, 1)
                last_split()

            def guess(n, v, dst0, dst, made, sm):
                act.wait_ge(*made)
                step(nc.scalar.activation(dst0, v, ACT.Ln))
                nc.scalar.activation(dst, dst0, ACT.Exp, scale=-0.5).then_inc(sm, 1)

            def held_split(name, u=3):
                p = ph[name]
                return lambda: split(p, p.blocks - 1, 1, 1)

            def phase_to_junction(name):
                p = ph[name]
                body(p, 0, 0)
                split(p, 1, 1, 0)

            def turned_out(name, gain, dst):
                for k in range(turns[name]):
                    act.wait_ge(turned, turn_base[name] + k + 1)
                    src = ps[:, turn_bank(name, k)]
                    g = gain(k)
                    if g is None:
                        last = nc.scalar.activation(dst[:, k], src, ACT.Copy)
                    else:
                        last = nc.scalar.activation(dst[:, k], src, ACT.Copy, scale=g)
                    last.then_inc(turned_hi, 1)

            act.dma_start(consts[:], w["shape_consts"][:, 0:K_STRICT + P]).then_inc(ident_in, 16)
            act.dma_start(g_turn, w["norm_mix"][0].rearrange("(a n) -> a n", a=1).partition_broadcast(P)).then_inc(mix_row_in, 16)
            nc.scalar.preload_act_table_set("natural_log_exp_and_others")
            act.wait_ge(eps_set, 1)
            junction("h", lambda: first_split(1), lambda: first_split(0))
            def sbq_round(blk, bank0):
                nc.scalar.activation(sbq_hi[:, bass.ds(4 * blk, 4)], ps[:, bank0:bank0 + 4], ACT.Copy,
                                     scale=1.0 if blk else SB_DIM ** -0.5).then_inc(qkv_hi, 1)

            phase("sb_qk", sbq_round)
            phase("sb_v", lambda blk, bank0: nc.scalar.activation(sbv_hi, ps[:, bank0:bank0 + 4], ACT.Copy).then_inc(qkv_hi, 1))

            def sb_soft(t, u):
                z = sb_z(u)
                act.wait_ge(z_ready, t + 1)
                if not (isinstance(t, int) and t < 2):
                    act.wait_ge(sp_made, t - 1)
                nc.scalar.activation(sb_t[u], z, ACT.Abs).then_inc(sb_abs, 1)
                act.wait_ge(sb_abs, t + 1)
                nc.scalar.activation(sb_t[u], sb_t[u], ACT.Exp, scale=-1.0).then_inc(sb_exp, 1)
                act.wait_ge(sb_exp, t + 1)
                nc.scalar.activation(sb_t[u], sb_t[u], ACT.Ln, bias=1.0).then_inc(soft_log, 1)

            def sb_weights(t, u):
                act.wait_ge(c_ready, t + 1)
                if not (isinstance(t, int) and t < 2):
                    act.wait_ge(sb_pv, t - 1)
                z = sb_z(u)
                nc.scalar.activation(sb_w[u], z, ACT.Exp)
                nc.scalar.activation(sb_whi[u], z, ACT.Exp).then_inc(w_exp, 1)

            def sb_round(t, u):
                act.wait_ge(sp_summed, t + 1)
                act.wait_ge(sp_after, t + 1)
                if not (isinstance(t, int) and t < 2):
                    act.wait_ge(c_ready, t - 1)
                nc.scalar.activation(sb_hi[u], sb_sp[u], ACT.Copy).then_inc(sp_hi, 1)

            sb_soft(0, 0)
            sb_round(0, 0)
            sb_soft(1, 1)
            sb_weights(0, 0)
            sb_round(1, 1)
            with act.Fori(1, SB_HEADS // 2) as i:
                for u in range(2):
                    t = i * 2 + u
                    sb_soft(t, u)
                    sb_weights(t - 1, 1 - u)
                    sb_round(t, u)
            sb_weights(SB_HEADS - 1, 1)
            p = ph["g_qk"]
            body(p, 0, 0)
            act.wait_ge(osb_out, SB_HEADS)
            nc.scalar.activation(h_hi[:, 0:4], o_sb, ACT.Copy).then_inc(osb_hi, 1)
            body(p, 1, 1)
            act.wait_ge(low_in, 16)
            nc.scalar.activation(hhf[:, 2048:3072], tmp[:, 0:1024], ACT.Copy).then_inc(low_split_hi, 1)
            phase("g_v")
            act.wait_ge(up_mm, 1)
            for h in range(GLA_HEADS):
                last = nc.scalar.activation(tmp4[:, h], ps[:, up_bank + h], ACT.Identity, bias=b_gate[:, h:h + 1])
            last.then_inc(gate_u, 1)
            act.wait_ge(gate_u, 1)
            step(nc.scalar.activation(u_abs, tmp, ACT.Abs))
            step(nc.scalar.activation(u_abs, u_abs, ACT.Exp, scale=-1.0))
            nc.scalar.activation(u_abs, u_abs, ACT.Ln, bias=1.0).then_inc(gate_log, 1)
            def level_exp(n):
                act.wait_ge(g_diff, n + 1)
                nc.scalar.activation(g_f[n % 4], g_f[n % 4], ACT.Exp).then_inc(g_exp, 1)

            p = ph["g_out"]
            body(p, 0, 0, gates(lambda blk: tok_block(y_tm, blk), clamped, 0))
            level_exp(0)
            level_exp(1)
            body(p, 1, 1, gates(lambda blk: tok_block(y_tm, blk), clamped, 0))
            for n in range(2, LEVELS + 2):
                level_exp(n)
            nc.scalar.activation(elast, b_cum.rearrange("p (m n) -> p m n", n=P)[:, :, P - 1], ACT.Exp).then_inc(g_exp, 1)
            for c in range(2):
                act.wait_ge(go_mm, c + 1)
                nc.scalar.activation(g_o[:, 1024 * c:1024 * (c + 1)], psf[:, 1024 * c:1024 * (c + 1)], ACT.Copy).then_inc(go_act, 1)
            act.wait_ge(go_dve, 2)
            act.wait_ge(go_act, 2)
            for m in range(16):
                step(nc.scalar.activation(tmp[:, 1024:1024 + GLA_DV], g_o[:, GLA_DV * m:GLA_DV * (m + 1)], ACT.Square,
                                          accum_out=gss[:, m:m + 1]))
            nc.scalar.activation(small[:, 251:252], gss[:, 0:1], ACT.Copy).then_inc(gss_ready, 1)
            guess(0, gvar, grs0, grs1, (gvar_ready, 1), ggs_ready)
            phase("gate_sb", gates(lambda blk: fm_block(gates_sb, blk), banks_free, ph["gate_sb"].b))
            phase("gate_gla", gates(lambda blk: fm_block(gates_gla, blk), banks_free, ph["gate_gla"].b))
            turned_out("o_gla", lambda k: gains[:, G_GLA + k % 2:G_GLA + k % 2 + 1], a_hi)
            phase("proj_sb")

            def mix_hi(blk, bank0):
                for c in range(2):
                    round_chunk(2 * blk + c + 1, tmp4[:, 2 * c:2 * c + 2], h_hi[:, bass.ds(4 * blk + 2 * c, 2)])
            phase("proj_gla", mix_hi)
            phase_to_junction("w_out")
            junction("h_mlp0", held_split("w_out"))
            mlp("mlp0", 4)
            junction("h_mix1", held_split("mlp0"))
            def qk_round(blk):
                act.wait_ge(rope_done, blk + 1)
                nc.scalar.activation(diff_qk_hi[blk // 2][:, 4 * (blk % 2):4 * (blk % 2) + 4], qk[:, 4 * blk:4 * blk + 4],
                                     ACT.Copy).then_inc(qk_hi, 1)

            for p in (ph["qk"], ph["v"]):
                for blk in range(p.blocks):
                    split(p, blk, blk % 2, 0)
                    n = blk + p.b - ph["qk"].b
                    if n >= 2:
                        qk_round(n - 2)
                    split(p, blk, blk % 2, 1)
            act.wait_ge(lam_sum, 1)
            nc.scalar.activation(lam[:, 2:4], lam[:, 0:2], ACT.Exp).then_inc(lam_exp, 1)

            def diff_exp(t, u, c):
                act.wait_ge(s_max[c], t + 1)
                if not (isinstance(t, int) and t < 2):
                    if c == 0:
                        act.wait_ge(p_turned, 3 * t - 3)
                    else:
                        act.wait_ge(p_mixed, t - 1)
                for i in range(TT):
                    n = P * (i + 1)
                    last = nc.scalar.activation(d_p[u][c][:, ROW[i]:ROW[i] + n], psf[:, DIFF_S[c] + ROW[i]:DIFF_S[c] + ROW[i] + n],
                                                ACT.Exp, bias=nmax[:, u, c, i:i + 1], accum_out=dsum[:, u, c, i:i + 1])
                last.then_inc(s_exp[c], 1)

            def diff_round(t, u, b):
                n = len_batch[b]
                act.wait_ge(p_turned, 3 * t + b + 1)
                if b == 0 and isinstance(t, int) and t == 0:
                    act.wait_ge(v_lo, 1)
                if b == 0 and not (isinstance(t, int) and t < 2):
                    act.wait_ge(o_mm, t - 1)
                nc.scalar.activation(d_hi[u][:, 512 * b:512 * b + n], ps[:, DIFF_TURN, 0:n], ACT.Copy).then_inc(pt_hi, 1)

            def diff_copy(t):
                act.wait_ge(o_mm, t + 1)
                nc.scalar.activation(qk[:, bass.ds(8 + t, 1)].rearrange("p a b -> p (a b)"), ps[:, DIFF_OUT], ACT.Copy).then_inc(ot_out, 1)

            def diff_out(t):
                act.wait_ge(o_turned, t + 1)
                for i in range(TT):
                    o = ps[:, DIFF_OUT, P * i:P * (i + 1)]
                    rec = drec[:, 0, bass.ds(4 * t + i, 1)]
                    nc.scalar.activation(qk[:, bass.ds(t, 1), P * i:P * (i + 1)].rearrange("p a b -> p (a b)"), o, ACT.Copy, scale=rec)
                    last = nc.scalar.activation(o, o, ACT.Square, scale=rec, accum_out=dss[:, bass.ds(4 * t + i, 1)])
                last.then_inc(o_out, 1)

            def diff_step(t, u):
                diff_round(t - 1, 1 - u, 0)
                if not (isinstance(t, int) and t < 3):
                    diff_out(t - 3)
                diff_exp(t, u, 0)
                diff_round(t - 1, 1 - u, 1)
                diff_exp(t, u, 1)
                diff_round(t - 1, 1 - u, 2)
                if not (isinstance(t, int) and t < 2):
                    diff_copy(t - 2)

            diff_exp(0, 0, 0)
            diff_exp(0, 0, 1)
            act.wait_ge(banks_free, ph["w_o"].b)
            nc.scalar.activation(ahf, yf, ACT.Copy).then_inc(v_hi, 1)
            for t in range(1, 4):
                diff_step(t, t % 2)
            with act.Fori(2, DIFF_HEADS // 2) as i:
                for u in range(2):
                    diff_step(i * 2 + u, u)
            diff_out(DIFF_HEADS - 3)
            diff_round(DIFF_HEADS - 1, 1, 0)
            diff_round(DIFF_HEADS - 1, 1, 1)
            diff_round(DIFF_HEADS - 1, 1, 2)
            for n, hs in enumerate(NORM_HEADS):
                if n:
                    for t in range(DIFF_HEADS - 2, DIFF_HEADS):
                        diff_copy(t)
                        diff_out(t)
                guess(0, dvar[:, hs], drs0[:, hs], drs1[:, hs], (ovar_ready, n + 1), ogs_ready)
            turned_out("o_diff", lambda k: gains[:, N_GAINS:N_GAINS + 1], a_hi)
            phase_to_junction("w_o")
            junction("h_mlp1", held_split("w_o"))
            mlp("mlp1", 4 + 16)
            junction("h_conv", held_split("mlp1"))

            def conv_hi(blk, bank0):
                if blk >= 4:
                    act.wait_ge(banks_free, p.b + blk + 1)
                    for a in range(4):
                        k = 4 * (blk - 4) + a
                        nc.scalar.activation(qk[:, 8 + k], y_fm[:, k], ACT.Copy, scale=convw[:, 2, k:k + 1]).then_inc(last_tap, 1)
                    for a in range(4):
                        k = 4 * (blk - 4) + a
                        round_chunk(4 + 32 + k + 1, qk[:, k], h_hi[:, k])
            p = ph["conv_in"]
            for blk in range(p.blocks):
                body(p, blk, blk % 2, conv_hi)
            phase_to_junction("conv_out")
            junction("h_mlp2", held_split("conv_out"))
            mlp("mlp2", 4 + 32 + 8)
            junction("out", lambda: None)

        @block.vector
        def _(dve):
            step = Steps(dve, dve_step)
            tt, ts, stt = nc.vector.tensor_tensor, nc.vector.tensor_scalar, nc.vector.scalar_tensor_tensor

            def split(p, blk, u, qi):
                n, s = quad_at(p, blk, qi) + 2, slot_of(p, u, qi)
                if isinstance(n, int) and n >= n_quads:
                    return
                dve.wait_ge(hi_ready, n + 1)
                tt(w_lo[:, s], w_raw[:, s], w_hi[:, s].bitcast(F32), ALU.subtract).then_inc(lo_ready, 1)

            def first_split(s):
                dve.wait_ge(hi_ready, s + 1)
                tt(w_lo[:, s], w_raw[:, s], w_hi[:, s].bitcast(F32), ALU.subtract).then_inc(lo_ready, 1)

            def body(p, blk, u, evac):
                for qi in range(p.quads):
                    split(p, blk, u, qi)
                dve.wait_ge(quad_done, quad_at(p, blk, p.quads))
                evac(blk, 4 * ((p.b + u) % 2))

            def phase(name, evac):
                p = ph[name]
                if p.blocks % 2:
                    return body(p, 0, 0, evac)
                for blk in pairs(dve, p):
                    for u in range(2):
                        body(p, blk + u, u, evac)

            def to_tiles(first, scale=None):
                def evac(blk, bank0):
                    dst = qk[:, bass.ds(first + 4 * blk, 4)]
                    src = ps[:, bank0:bank0 + 4]
                    if scale is None or blk:
                        nc.vector.tensor_copy(dst, src).then_inc(banks_free, 1)
                    else:
                        ts(dst, src, scale, None, ALU.mult).then_inc(banks_free, 1)
                return evac

            def to_tokens(dst):
                def evac(blk, bank0):
                    nc.vector.tensor_copy(tok_block(dst, blk), ps[:, bank0:bank0 + 4]).then_inc(banks_free, 1)
                return evac

            def add_tokens(dst):
                def evac(blk, bank0):
                    d = tok_block(dst, blk)
                    tt(d, ps[:, bank0:bank0 + 4], d, ALU.add).then_inc(banks_free, 1)
                return evac

            def lo_chunk(n, src, hi, dst):
                dve.wait_ge(chunk_hi, n)
                tt(dst, src, hi.bitcast(F32), ALU.subtract).then_inc(chunk_lo, 1)

            def mlp(name, chunks, exps, acc, first_tile):
                p = ph[name]

                def rounds(r, tail=False):
                    for u in range(4):
                        blk = r * 4 + u
                        bank0 = 4 * ((p.b + u) % 2)
                        split(p, blk, u, 0)
                        if u == 3:
                            if tail:
                                return
                            for i in range(TT):
                                if i < TT - 1:
                                    dve.wait_ge(tile_done, first_tile + r * 3 + i + 1)
                                else:
                                    dve.wait_ge(quad_done, quad_at(p, blk, 2))
                                d = acc[:, i, NBLK:]
                                tt(d, ps[:, bank0 + i], d, ALU.add).then_inc(tile_out if i < TT - 1 else banks_free, 1)
                            split(p, blk, u, 1)
                            continue
                        split(p, blk, u, 1)
                        if u >= 2:
                            dve.wait_ge(quad_done, quad_at(p, blk, 2))
                            d = acc[:, :, NBLK * (u - 2):NBLK * (u - 1)]
                            tt(d, ps[:, bank0:bank0 + 4], d, ALU.add).then_inc(banks_free, 1)
                            continue
                        for c in range(2):
                            dve.wait_ge(exp_ready, exps + r * 4 + 2 * u + c + 1)
                            f = tmp4[:, 2 * c:2 * c + 2]
                            last = stt(f.rearrange("p a b -> p (a b)"), psf[:, 512 * (bank0 + 2 * c):512 * (bank0 + 2 * c + 2)], 0.0,
                                       f.rearrange("p a b -> p (a b)"), ALU.max, ALU.mult)
                            last.then_inc(chunk_f32, 1)
                        for c in range(2):
                            g = chunks + r * 4 + 2 * u + c
                            ks = slice(4 * u + 2 * c, 4 * u + 2 * c + 2)
                            dve.wait_ge(chunk_hi, g + 1)
                            tt(h_lo[:, ks], tmp4[:, 2 * c:2 * c + 2], h_hi[:, ks].bitcast(F32), ALU.subtract).then_inc(chunk_lo, 1)
                            if c == 0:
                                dve.wait_ge(chunk_f32, g + 2)
                                nc.vector.memset(small[:, 252:253], 0.0).then_inc(banks_free, 1)

                with dve.Fori(0, ROUNDS - 1) as r:
                    rounds(r)
                rounds(ROUNDS - 1, True)

            def refine(n_cols, v, y0, y1, out_, count, denom, sums, ready, v_done, guessed, done):
                dve.wait_ge(*ready)
                ts(v, sums, 1.0 / denom, EPS, ALU.mult, ALU.add).then_inc(v_done, 1)
                dve.wait_ge(*guessed)
                step(tt(y0, y1, y1, ALU.mult))
                step(tt(y0, y0, v, ALU.mult))
                step(ts(y0, y0, -0.5, 1.5, ALU.mult, ALU.add))
                tt(out_, y0, y1, ALU.mult).then_inc(done, 1)

            def junction(name, move, rows, last_split, early_split=None):
                tile0, kind, add, adds, turn_, turns_before = junctions[name]
                for s_ in range(TT + 3):
                    if move and s_ < TT:
                        if s_ < TT - 1:
                            dve.wait_ge(tile_done, tile0 + s_ + 1)
                        else:
                            dve.wait_ge(quad_done, last_quad[name])
                        move(s_).then_inc(tile_out if s_ < TT - 1 else banks_free, 1)
                    if s_ == 0 and rows:
                        dve.wait_ge(grow_in, 16 * rows)
                    if s_ == 3 and early_split:
                        early_split()
                    if add is not None and 1 <= s_ <= TT:
                        i = s_ - 1
                        dve.wait_ge(rstd_ready, stat_count(name, add, i))
                        r = rstd[add % 2][:, i:i + 1]
                        if kind == "F":
                            stt(x_tm[:, i], x_tm[:, i], r, g_add, ALU.mult, ALU.mult).then_inc(resid_ready, 1)
                        else:
                            step(stt(y_tm[:, i], y_tm[:, i], r, g_add, ALU.mult, ALU.mult))
                            tt(x_tm[:, i], x_tm[:, i], y_tm[:, i], ALU.add).then_inc(resid_ready, 1)
                    if turn_ is not None and 2 <= s_ <= TT + 1:
                        i = s_ - 2
                        dve.wait_ge(rstd_ready, stat_count(name, turn_, i))
                        stt(y_tm[:, i], x_tm[:, i], rstd[turn_ % 2][:, i:i + 1], g_turn, ALU.mult, ALU.mult).then_inc(normed, 1)
                    if turn_ is not None and s_ >= 3:
                        i = s_ - 3
                        for half in range(2):
                            dve.wait_ge(turned_hi, turn_base[name] + 2 * i + half + 1)
                            cs = (slice(None), slice(4 * half, 4 * half + 4), slice(P * i, P * (i + 1)))
                            tt(a_lo[cs], ps[:, tile_bank(name, i, half)].rearrange("p (a b) -> p a b", a=4),
                               a_hi[cs].bitcast(F32), ALU.subtract).then_inc(turned_lo, 1)
                last_split()

            last_quad = {"h_mlp0": ph["mlp0"].q, "h_mix1": ph["qk"].q, "h_mlp1": ph["mlp1"].q,
                         "h_conv": ph["conv_in"].q, "h_mlp2": ph["mlp2"].q, "out": n_quads}

            def held_split(name):
                p = ph[name]
                return lambda: split(p, p.blocks - 1, 1, 1)

            def phase_to_junction(name, evac):
                p = ph[name]
                body(p, 0, 0, evac)
                split(p, 1, 1, 0)

            def move_tile(name, dst):
                bank0 = 4 * ((ph[name].b + 1) % 2)
                return lambda i: nc.vector.tensor_copy(dst[:, i, NBLK:], ps[:, bank0 + i])

            def add_tile(name, dst):
                bank0 = 4 * ((ph[name].b + 1) % 2)
                return lambda i: tt(dst[:, i, NBLK:], ps[:, bank0 + i], dst[:, i, NBLK:], ALU.add)

            def turned_out(name, gain, hi, lo):
                for k in range(turns[name]):
                    dve.wait_ge(turned_hi, turn_base[name] + k + 1)
                    src = ps[:, turn_bank(name, k)]
                    g = gain(k)
                    if g is None:
                        last = tt(lo[:, k], src, hi[:, k].bitcast(F32), ALU.subtract)
                    else:
                        last = stt(lo[:, k], src, g, hi[:, k].bitcast(F32), ALU.mult, ALU.subtract)
                    last.then_inc(turned_lo, 1)

            for i in range(TT):
                dve.wait_ge(x_in[i], 16)
            dve.wait_ge(mix_row_in, 16)
            junction("h", None, 0, lambda: first_split(1), lambda: first_split(0))
            dve.wait_ge(consts_in, 32)
            dve.wait_ge(ident_in, 16)
            nc.vector.tensor_copy(ntri[:], consts[:, K_NTRI:K_NTRI + P]).then_inc(consts_r, 1)
            nc.vector.tensor_copy(nones[:], consts[:, K_NONE:K_NONE + P]).then_inc(consts_r, 1)
            nc.vector.tensor_copy(ident_b[:], ident).then_inc(consts_r, 1)
            nc.vector.tensor_copy(causal_b[:], tmp[:, 0:P]).then_inc(consts_r, 1)
            ts(strict_b[:], strict, 1.0, 1e30, ALU.subtract, ALU.mult).then_inc(consts_r, 1)
            step(nc.vector.tensor_copy(masks[:].rearrange("p a b -> p (a b)"), masks_f))

            def sbq_lo_part(blk, bank0):
                dve.wait_ge(qkv_hi, blk + 1)
                stt(sbq_lo[:, 4 * blk:4 * blk + 4].rearrange("p a b -> p (a b)"), psf[:, 512 * bank0:512 * bank0 + 2048],
                    1.0 if blk else SB_DIM ** -0.5, sbq_hi[:, 4 * blk:4 * blk + 4].bitcast(F32).rearrange("p a b -> p (a b)"),
                    ALU.mult, ALU.subtract).then_inc(banks_free, 1)

            def sbv_lo_part(blk, bank0):
                dve.wait_ge(qkv_hi, 3)
                tt(sbv_lo, ps[:, bank0:bank0 + 4], sbv_hi.bitcast(F32), ALU.subtract).then_inc(banks_free, 1)

            phase("sb_qk", sbq_lo_part)
            phase("sb_v", sbv_lo_part)
            dve.wait_ge(gains_turned, 1)
            nc.vector.tensor_copy(gains[:, 0:N_GAINS], ps[:, 7, 0:N_GAINS]).then_inc(gains_out, 1)
            dve.wait_ge(gains_out, 1)
            step(ts(gains[:, N_GAINS:N_GAINS + 1], gains[:, G_SUBLN:G_SUBLN + 1], 1.0 - LAMBDA_INIT, None, ALU.mult))

            def sb_softplus(t, u):
                dve.wait_ge(soft_log, t + 1)
                if not (isinstance(t, int) and t < 2):
                    dve.wait_ge(c_ready, t - 1)
                stt(sb_sp[u][:, 0:TRI], sb_z(u), 0.0, sb_t[u], ALU.max, ALU.add).then_inc(sp_made, 1)
                dve.wait_ge(sp_made, t + 1)
                tile = lambda c: sb_sp[u][:, c:c + P]
                tt(tile(AFTER[1] + P), tile(COL[2] + P), tile(COL[3]), ALU.add).then_inc(sp_pair, 1)
                dve.wait_ge(sp_pair, t + 1)
                tt(tile(AFTER[0] + 2 * P), tile(COL[1] + 2 * P), tile(AFTER[1] + P), ALU.add).then_inc(sp_summed, 1)

            def sb_softplus_lo(t, u):
                dve.wait_ge(sp_hi, t + 1)
                tt(sb_lo[u], sb_sp[u], sb_hi[u].bitcast(F32), ALU.subtract).then_inc(sp_lo, 1)

            def sb_weights_lo(t, u):
                dve.wait_ge(w_exp, t + 1)
                tt(sb_wlo[u], sb_w[u], sb_whi[u].bitcast(F32), ALU.subtract).then_inc(sbw_lo, 1)

            def sb_out(t, u, pair):
                dve.wait_ge(sb_pv, t + 1)
                rows = slice(SB_DIM * u, SB_DIM * (u + 1))
                nc.vector.tensor_copy(o_sb[rows, bass.ds(pair, 1)].rearrange("p a b -> p (a b)"),
                                      ps[rows, SB_OUT[u]]).then_inc(osb_out, 1)

            sb_softplus(0, 0)
            sb_softplus_lo(0, 0)
            sb_softplus(1, 1)
            sb_weights_lo(0, 0)
            sb_softplus_lo(1, 1)
            with dve.Fori(1, SB_HEADS // 2) as i:
                for u in range(2):
                    t = i * 2 + u
                    sb_softplus(t, u)
                    sb_weights_lo(t - 1, 1 - u)
                    sb_softplus_lo(t, u)
                    sb_out(t - 2, u, i - 1)
            sb_weights_lo(SB_HEADS - 1, 1)
            for u in range(2):
                sb_out(SB_HEADS - 2 + u, u, SB_HEADS // 2 - 1)
            p = ph["g_qk"]
            body(p, 0, 0, to_tiles(8, GLA_DK ** -0.5))
            dve.wait_ge(osb_hi, 1)
            tt(h_lo[:, 0:4], o_sb, h_hi[:, 0:4].bitcast(F32), ALU.subtract).then_inc(osb_lo, 1)
            body(p, 1, 1, to_tiles(8, GLA_DK ** -0.5))
            dve.wait_ge(low_split_hi, 1)
            tt(hlf[:, 2048:3072], tmp[:, 0:1024], hhf[:, 2048:3072].bitcast(F32), ALU.subtract).then_inc(low_split, 1)
            phase("g_v", to_tokens(x_tm))

            dve.wait_ge(low_mm, 1)
            nc.vector.tensor_copy(low_t, ps[0:GLA_RANK, low_bank]).then_inc(low_out, 1)
            dve.wait_ge(gate_u, 1)
            step(ts(m_min, tmp, 0.0, None, ALU.min))
            dve.wait_ge(gate_log, 1)
            step(tt(m_min, m_min, u_abs, ALU.subtract))
            step(ts(m_min, m_min, 1.0 / GLA_TAU, None, ALU.mult))
            keep = arena[:, 0:2048]
            step(nc.vector.memset(keep, 1.0))
            step(nc.vector.memset(keep.rearrange("p (m n) -> p m n", n=P)[:, :, 0:1], 0.0))
            nc.vector.tensor_tensor_scan(b_cum, keep, m_min, 0.0, ALU.mult, ALU.add).then_inc(b_ready, 1)

            b_chunk = b_cum.rearrange("p (m n) -> p m n", n=P)

            def level_factor(n):
                h = 1 << n
                dve.wait_ge(g_exp, n + 1)
                f2, q2, k2 = (z.rearrange("p (m two n) -> p m two n", two=2, n=h) for z in (g_f[n % 4], g_q, g_k))
                tt(f2[:, :, 1], f2[:, :, 1], q2[:, :, 1], ALU.mult)
                tt(f2[:, :, 0], f2[:, :, 0], k2[:, :, 0], ALU.mult).then_inc(g_fac, 1)

            def silu(blk, bank0):
                d, src = tok_block(y_tm, blk), ps[:, bank0:bank0 + 4]
                ts(d, src, GATE_MIN, None, ALU.max).then_inc(clamped, 1)
                dve.wait_ge(gates_made, blk + 1)
                tt(d, src, d, ALU.mult).then_inc(banks_free, 1)
            dve.wait_ge(b_ready, 1)
            step(nc.vector.memset(g_at, 0.0))
            p = ph["g_out"]
            body(p, 0, 0, silu)
            level_factor(0)
            body(p, 1, 1, silu)

            def level_select(n):
                dve.wait_ge(g_mm, n + 1)
                if n:
                    dve.wait_ge(g_sel, n)
                nc.vector.copy_predicated(g_at.rearrange("p (m n) -> p m n", n=P),
                                          masks[:, n:n + 1].to_broadcast([P, 16, P]),
                                          psf[:, level_col(n):level_col(n) + 2048].rearrange("p (m n) -> p m n", n=P)).then_inc(g_sel, 1)

            for n in range(2, LEVELS):
                level_select(n - 2)
                level_factor(n - 1)
            level_select(LEVELS - 2)
            level_factor(LEVELS - 1)
            dve.wait_ge(g_mm, LEVELS)
            step(nc.vector.tensor_copy(g_f[LEVELS % 4], b_cum))
            nc.vector.memset(small[:, 253:254], 0.0).then_inc(g_diff, 1)
            level_select(LEVELS - 1)
            dve.wait_ge(g_mm, LEVELS + 1)
            tt(g_f[(LEVELS + 1) % 4].rearrange("p (m n) -> p m n", n=P), b_chunk[:, :, P - 1:P].to_broadcast([P, 16, P]), b_chunk,
               ALU.subtract).then_inc(g_diff, 1)
            level_select(LEVELS)
            dve.wait_ge(g_exp, LEVELS + 2)
            tt(g_k, g_k, g_f[(LEVELS + 1) % 4], ALU.mult).then_inc(kd_ready, 1)
            step(tt(g_q, g_q, g_f[LEVELS % 4], ALU.mult))
            dve.wait_ge(kd_turned, 1)
            nc.vector.tensor_copy(g_kt, psf[:, 0:1536]).then_inc(kd_out, 1)
            dve.wait_ge(st_mm, 1)
            dve.wait_ge(g_exp, LEVELS + 3)
            step(nc.vector.tensor_copy(g_state[0], psf[:, 1024:2048]))
            nc.vector.memset(small[:, 254:255], 0.0).then_inc(st_ready, 1)
            for c in range(1, 3):
                for h in range(GLA_HEADS):
                    hs = slice(GLA_DV * h, GLA_DV * (h + 1))
                    last = stt(g_state[c][:, hs], g_state[c - 1][:, hs], elast[:, 4 * h + c:4 * h + c + 1],
                               psf[:, 1024 * (c + 1) + GLA_DV * h:1024 * (c + 1) + GLA_DV * (h + 1)], ALU.mult, ALU.add)
                step(last)
                nc.vector.memset(small[:, 254:255], 0.0).then_inc(st_ready, 1)
            for c in range(2, 4):
                dve.wait_ge(go_mm, c + 1)
                nc.vector.tensor_copy(g_o[:, 1024 * c:1024 * (c + 1)], psf[:, 1024 * c:1024 * (c + 1)]).then_inc(go_dve, 1)
            refine(16, gvar, grs0, grs1, grstd, 0, GLA_DV, gss, (gss_ready, 1), gvar_ready, (ggs_ready, 1), sem_grstd)
            dve.wait_ge(sem_grstd, 1)
            for m in range(16):
                i, h = m // 4, m % 4
                ys = y_tm[:, i, GLA_DV * h:GLA_DV * (h + 1)]
                last = stt(ys, g_o[:, GLA_DV * m:GLA_DV * (m + 1)], grstd[:, m:m + 1], ys, ALU.mult, ALU.mult)
                if h == 3:
                    last.then_inc(gout_ready, 1)

            def move_gates(tiles):
                def evac(blk, bank0):
                    ts(fm_block(tiles, blk), ps[:, bank0:bank0 + 4], GATE_MIN, None, ALU.max).then_inc(banks_free, 1)
                return evac
            dve.wait_ge(gout_ready, 4)
            phase("gate_sb", move_gates(gates_sb))
            phase("gate_gla", move_gates(gates_gla))
            turned_out("o_gla", lambda k: gains[:, G_GLA + k % 2:G_GLA + k % 2 + 1], a_hi, a_lo)

            def mix_sb(blk, bank0):
                dve.wait_ge(gates_made, 2 + blk + 1)
                d = gates_sb.rearrange("p (a b) -> p a b", a=8)[:, 4 * blk:4 * blk + 4]
                tt(d, ps[:, bank0:bank0 + 4], d, ALU.mult).then_inc(banks_free, 1)

            def mix_gla(blk, bank0):
                dve.wait_ge(gates_made, 4 + blk + 1)
                for c in range(2):
                    f = tmp4[:, 2 * c:2 * c + 2]
                    last = tt(f, ps[:, bank0 + 2 * c:bank0 + 2 * c + 2], fm_tiles(gates_gla, blk, c), ALU.mult)
                    if c:
                        last.then_inc(banks_free, 1)
                step(nc.vector.memset(small[:, 255:256], 0.0))
                for c in range(2):
                    f = tmp4[:, 2 * c:2 * c + 2]
                    tt(f, f, fm_tiles(gates_sb, blk, c), ALU.add).then_inc(chunk_f32, 1)
                for c in range(2):
                    ks = slice(4 * blk + 2 * c, 4 * blk + 2 * c + 2)
                    lo_chunk(2 * blk + c + 1, tmp4[:, 2 * c:2 * c + 2], h_hi[:, ks], h_lo[:, ks])
                dve.wait_ge(chunk_lo, 2 * blk + 2)
            phase("proj_sb", mix_sb)
            dve.wait_ge(banks_free, ph["proj_gla"].b)
            phase("proj_gla", mix_gla)
            dve.wait_ge(x_again, 16)
            phase_to_junction("w_out", add_tokens(x_tm))
            junction("h_mlp0", add_tile("w_out", x_tm), 1, held_split("w_out"))
            mlp("mlp0", 4, 0, x_tm, 3)
            junction("h_mix1", add_tile("mlp0", x_tm), 3, held_split("mlp0"))

            for u in range(2):
                step(nc.vector.memset(rot[u], 0.0))
            dve.wait_ge(tables_in, 80)
            prod = stat[:, 0:4].rearrange("p a b -> p (a b)")
            step(tt(prod.rearrange("p (a b) -> p a b", a=2), lam_in[:, 0:4:2], lam_in[:, 1:4:2], ALU.mult))
            nc.vector.tensor_reduce(lam[:, 0:2], prod.rearrange("p (a b) -> p a b", a=2), AX.X, ALU.add).then_inc(lam_sum, 1)

            def rope(blk):
                sw = rot[blk % 2].rearrange("p (a b) -> p a b", a=4)
                tiles = qk[:, 4 * blk:4 * blk + 4]
                dve.wait_ge(swapped[blk % 2], 64 * (blk // 2 + 1))
                step(tt(sw, sw, sin_t.rearrange("p (a b) -> p a b", a=1).to_broadcast([P, 4, SEQ]), ALU.mult))
                step(tt(tiles, tiles, cos_t.rearrange("p (a b) -> p a b", a=1).to_broadcast([P, 4, SEQ]), ALU.mult))
                tt(tiles, tiles, sw, ALU.add).then_inc(rope_done, 1)

            p = ph["qk"]
            def qk_lo_part(blk):
                dve.wait_ge(qk_hi, blk + 1)
                d = qk[:, 4 * blk:4 * blk + 4]
                tt(qk_r[:, 4 * blk:4 * blk + 4], d, diff_qk_hi[blk // 2][:, 4 * (blk % 2):4 * (blk % 2) + 4].bitcast(F32), ALU.subtract).then_inc(qk_lo, 1)

            for blk in range(4):
                split(p, blk, blk % 2, 0)
                if blk >= 2:
                    qk_lo_part(blk - 2)
                split(p, blk, blk % 2, 1)
                dve.wait_ge(quad_done, quad_at(p, blk, 2))
                bank0 = 4 * ((p.b + blk) % 2)
                dst, src = qk[:, 4 * blk:4 * blk + 4], ps[:, bank0:bank0 + 4]
                if blk < 2:
                    step(ts(dst, src, DIFF_DIM ** -0.5, None, ALU.mult))
                else:
                    step(nc.vector.tensor_copy(dst, src))
                if blk >= 2:
                    dve.wait_ge(rope_done, blk - 1)
                nc.vector.memset(small[:, 248:249], 0.0).then_inc(banks_free, 1)
                nc.vector.memset(small[:, 249:250], 0.0).then_inc(rope_src, 1)
                if blk:
                    rope(blk - 1)
            rope(3)
            p = ph["v"]
            for blk in range(2):
                split(p, blk, blk % 2, 0)
                qk_lo_part(2 + blk)
                split(p, blk, blk % 2, 1)
                dve.wait_ge(quad_done, quad_at(p, blk, 2))
                to_tokens(y_tm)(blk, 4 * ((p.b + blk) % 2))
            dve.wait_ge(lam_exp, 1)
            step(tt(lam[:, 4:5], lam[:, 3:4], lam[:, 2:3], ALU.subtract))
            step(ts(lam[:, 5:6], lam[:, 4:5], LAMBDA_INIT, None, ALU.subtract))

            def diff_max(t, u, c):
                dve.wait_ge(s_mm[c], t + 1)
                if not (isinstance(t, int) and t < 2):
                    dve.wait_ge(s_exp[c], t - 1)
                for i in range(TT):
                    n = P * (i + 1)
                    last = nc.vector.tensor_reduce(nmax[:, u, c, i:i + 1], psf[:, DIFF_S[c] + ROW[i]:DIFF_S[c] + ROW[i] + n],
                                                   AX.X, ALU.max, negate=True)
                last.then_inc(s_max[c], 1)

            def diff_mix(t, u):
                dve.wait_ge(s_exp[0], t + 1)
                dve.wait_ge(s_exp[1], t + 1)
                rec = drec[:, :, bass.ds(4 * t, 4)]
                nc.vector.reciprocal(rec, dsum[:, u]).then_inc(rec_made, 1)
                dve.wait_ge(rec_made, t + 1)
                stt(nmax[:, u, 1], drec[:, 1, bass.ds(4 * t, 4)], lam[:, 5:6], dsum[:, u, 0], ALU.mult, ALU.mult).then_inc(ratio_made, 1)
                dve.wait_ge(ratio_made, t + 1)
                for i in range(TT):
                    n = P * (i + 1)
                    cs = slice(ROW[i], ROW[i] + n)
                    last = stt(d_p[u][0][:, cs], d_p[u][1][:, cs], nmax[:, u, 1, i:i + 1], d_p[u][0][:, cs], ALU.mult, ALU.add)
                last.then_inc(p_mixed, 1)

            def diff_lo(t, u, b):
                n = len_batch[b]
                dve.wait_ge(pt_hi, 3 * t + b + 1)
                if b == 0 and not (isinstance(t, int) and t < 2):
                    dve.wait_ge(o_mm, t - 1)
                tt(d_lo(u, 512 * b, n), ps[:, DIFF_TURN, 0:n], d_hi[u][:, 512 * b:512 * b + n].bitcast(F32), ALU.subtract).then_inc(pt_lo, 1)

            def diff_step(t, u):
                for c in range(2):
                    diff_max(t, u, c)
                    diff_lo(t - 1, 1 - u, c)
                diff_lo(t - 1, 1 - u, 2)
                diff_mix(t, u)

            diff_max(0, 0, 0)
            diff_max(0, 0, 1)
            diff_mix(0, 0)
            dve.wait_ge(v_hi, 1)
            tt(alf, yf, ahf.bitcast(F32), ALU.subtract).then_inc(v_lo, 1)
            diff_step(1, 1)
            with dve.Fori(1, DIFF_HEADS // 2) as i:
                for u in range(2):
                    diff_step(i * 2 + u, u)
            for b in range(3):
                diff_lo(DIFF_HEADS - 1, 1, b)
            for n, hs in enumerate(NORM_HEADS):
                refine(0, dvar[:, hs], drs0[:, hs], drs1[:, hs], drstd[:, hs], 0, DIFF_V, dss[:, hs],
                       (o_out, DIFF_HEADS - 2 + 2 * n), ovar_ready, (ogs_ready, n + 1), sem_orstd)
                dve.wait_ge(sem_orstd, n + 1)
                for g in range(hs.start // 8, hs.stop // 8):
                    o = qk[:, 2 * g:2 * g + 2].rearrange("p a (i e) -> p (a i) e", e=P)
                    r = drstd[:, 8 * g:8 * g + 8].rearrange("p (n one) -> p n one", one=1).to_broadcast([P, 8, P])
                    tt(o, o, r, ALU.mult).then_inc(o_normed, 1)
            turned_out("o_diff", lambda k: gains[:, N_GAINS:N_GAINS + 1], a_hi, a_lo)
            phase_to_junction("w_o", to_tokens(y_tm))
            junction("h_mlp1", move_tile("w_o", y_tm), 5, held_split("w_o"))
            clear_y(dve, 1)
            mlp("mlp1", 4 + 16, 16, y_tm, 3 * 6)
            junction("h_conv", add_tile("mlp1", y_tm), 7, held_split("mlp1"))

            def conv(k):
                u_, y_ = y_fm[:, k], qk[:, 8 + k]
                dve.wait_ge(last_tap, k + 1)
                step(stt(y_[:, 1:SEQ], u_[:, 0:SEQ - 1], convw[:, 1, k:k + 1], y_[:, 1:SEQ], ALU.mult, ALU.add))
                step(stt(y_[:, 2:SEQ], u_[:, 0:SEQ - 2], convw[:, 0, k:k + 1], y_[:, 2:SEQ], ALU.mult, ALU.add))
                tt(qk[:, k], qk[:, k], y_, ALU.mult).then_inc(chunk_f32, 1)
                lo_chunk(4 + 32 + k + 1, qk[:, k], h_hi[:, k], h_lo[:, k])

            p = ph["conv_in"]
            for blk in range(p.blocks):
                for qi in range(2):
                    split(p, blk, blk % 2, qi)
                dve.wait_ge(quad_done, quad_at(p, blk, 2))
                bank0 = 4 * ((p.b + blk) % 2)
                src = ps[:, bank0:bank0 + 4]
                if blk < 4:
                    nc.vector.tensor_copy(qk[:, 4 * blk:4 * blk + 4], src).then_inc(banks_free, 1)
                    continue
                g = 4 * (blk - 4)
                dve.wait_ge(banks_free, p.b + blk)
                tt(y_fm[:, g:g + 4], src, qk[:, 8 + g:12 + g], ALU.mult).then_inc(banks_free, 1)
                dve.wait_ge(banks_free, p.b + blk + 1)
                for a in range(4):
                    conv(g + a)
            phase_to_junction("conv_out", to_tokens(y_tm))
            junction("h_mlp2", move_tile("conv_out", y_tm), 9, held_split("conv_out"))
            clear_y(dve, 2)
            mlp("mlp2", 4 + 32 + 8, 32, y_tm, 3 * 11)
            junction("out", add_tile("mlp2", y_tm), 10, lambda: None)


_OUT = ((1, SEQ, D), "float32")
_INS = ["x", "norm_mix", "w_in", "w_gate_up", "b_gate_up", "gla_norm", "w_proj_sb", "w_proj_gla", "w_out", "norm_mlp",
        "w_ff1", "w_ff2", "norm_final", "attn_w_qkv_2", "attn_w_o_2", "attn_lambda_q1_2", "attn_lambda_k1_2",
        "attn_lambda_q2_2", "attn_lambda_k2_2", "attn_subln_g_2", "conv_w_in_2", "conv_w_2", "conv_w_out_2",
        "mlp_w_up_2", "mlp_w_down_2", "norm_mixer_pre_2", "norm_mixer_post_2", "norm_mlp_pre_2", "norm_mlp_post_2"]


def kernel(**inputs):
    import concourse.bacc as bacc
    from concourse.bass_utils import run_bass_kernel_spmd

    nc = bacc.Bacc("TRN2", target_bir_lowering=False, num_devices=1)
    arrays, args = {}, {}
    for name, a in [(n, np.ascontiguousarray(inputs[n])) for n in _INS] + [("shape_consts", shape_constants())]:
        arrays[f"in_{name}"] = a
        args[name] = nc.dram_tensor(f"in_{name}", a.shape, mybir.dt.from_np(a.dtype), kind="ExternalInput").ap()
    out = nc.dram_tensor("out", _OUT[0], mybir.dt.from_np(np.dtype(_OUT[1])), kind="ExternalOutput").ap()
    build(nc, args, out)
    result = run_bass_kernel_spmd(nc, [arrays], core_ids=[0])
    return result.results[0]["out"]
```
